# Optimizing a Trainium2 kernel written in Bass

```python
import math
import jax, jax.numpy as jnp
from jax import lax
import numpy as np

D_MODEL = 1024
BATCH = 1
SEQ = 256
DEPTH = 2

N_A = DEPTH // 2
N_B = DEPTH - N_A

GLA_HEADS = 4
GLA_KD = D_MODEL // 2
GLA_VD = D_MODEL
GLA_DK = GLA_KD // GLA_HEADS
GLA_DV = GLA_VD // GLA_HEADS
GLA_RANK = 16
GLA_TAU = 16.0
GLA_CHUNK = 64

FOX_HEADS = 16
FOX_HEAD_DIM = 64
FOX_WIDTH = FOX_HEADS * FOX_HEAD_DIM
FOX_BLOCK = 128

D_FF = 2816
PLE_DIM = 256
LN_EPS = 1e-5
DEEPNORM_ALPHA = (2 * DEPTH) ** 0.25
DEEPNORM_BETA = (8 * DEPTH) ** -0.25

kernel_name = "yoco_gla_fox_macaron_deepnorm"

def layer_norm(x, g, b):
    xf = x.astype(jnp.float32)
    mu = jnp.mean(xf, axis=-1, keepdims=True)
    var = jnp.mean(jnp.square(xf - mu), axis=-1, keepdims=True)
    return ((xf - mu) * lax.rsqrt(var + LN_EPS) * g + b).astype(x.dtype)

def swiglu(x, w_in, w_out):
    g, u = jnp.split(x @ w_in, 2, axis=-1)
    return (jax.nn.silu(g) * u) @ w_out

def _to_chunks(t, hd):
    b, s, _ = t.shape
    return t.reshape(b, s // GLA_CHUNK, GLA_CHUNK, GLA_HEADS, hd).transpose(0, 3, 1, 2, 4)

def gla_mixer(x, w_in, w_a2, b_a, gn_g, gn_b, w_o):
    bsz, s, _ = x.shape
    proj = x @ w_in
    q, k, v, r, a_lr = jnp.split(
        proj, [GLA_KD, 2 * GLA_KD, 2 * GLA_KD + GLA_VD, 2 * GLA_KD + 2 * GLA_VD], axis=-1)
    log_a = jax.nn.log_sigmoid((a_lr @ w_a2).astype(jnp.float32) + b_a) / GLA_TAU

    q = _to_chunks(q * (GLA_DK ** -0.5), GLA_DK)
    k = _to_chunks(k, GLA_DK)
    v = _to_chunks(v, GLA_DV)
    bcum = jnp.cumsum(_to_chunks(log_a, GLA_DK), axis=3)
    b_last = bcum[..., -1:, :]

    q_dec = q * jnp.exp(bcum)
    k_intra = k * jnp.exp(-bcum)
    k_state = k * jnp.exp(b_last - bcum)

    causal = jnp.tril(jnp.ones((GLA_CHUNK, GLA_CHUNK), dtype=bool))
    attn = jnp.einsum('bhncd,bhnsd->bhncs', q_dec, k_intra)
    attn = jnp.where(causal, attn, 0.0)
    o_intra = jnp.einsum('bhncs,bhnsv->bhncv', attn, v.astype(attn.dtype))

    def step(state, inp):
        q_c, k_c, v_c, dec_c = inp
        o_c = jnp.einsum('bhcd,bhdv->bhcv', q_c, state)
        state = state * dec_c[..., None] + jnp.einsum('bhcd,bhcv->bhdv', k_c, v_c.astype(state.dtype))
        return state, o_c

    state0 = jnp.zeros((bsz, GLA_HEADS, GLA_DK, GLA_DV), dtype=q_dec.dtype)
    xs = (jnp.moveaxis(q_dec, 2, 0), jnp.moveaxis(k_state, 2, 0),
          jnp.moveaxis(v, 2, 0), jnp.moveaxis(jnp.exp(b_last[..., 0, :]), 2, 0))
    _, o_inter = lax.scan(step, state0, xs)
    o = o_intra + jnp.moveaxis(o_inter, 0, 2)

    o = o.transpose(0, 2, 3, 1, 4).reshape(bsz, s, GLA_HEADS, GLA_DV)
    o = layer_norm(o, gn_g.reshape(GLA_HEADS, GLA_DV), gn_b.reshape(GLA_HEADS, GLA_DV))
    o = o.reshape(bsz, s, GLA_VD).astype(x.dtype) * jax.nn.silu(r)
    return o @ w_o

def fox_shared_kv(h, w_kvf, b_f):
    bsz, s, _ = h.shape
    kvf = h @ w_kvf
    k, v, f_logit = jnp.split(kvf, [FOX_WIDTH, 2 * FOX_WIDTH], axis=-1)
    log_f = jax.nn.log_sigmoid(f_logit.astype(jnp.float32) + b_f)
    c = jnp.cumsum(log_f, axis=1).transpose(0, 2, 1)
    k = k.reshape(bsz, s, FOX_HEADS, FOX_HEAD_DIM).transpose(0, 2, 1, 3)
    v = v.reshape(bsz, s, FOX_HEADS, FOX_HEAD_DIM).transpose(0, 2, 1, 3)
    return k, v, c

def fox_mixer(x, k, v, c, w_in, w_o):
    bsz, s, _ = x.shape
    q, g = jnp.split(x @ w_in, 2, axis=-1)
    q = (q * (FOX_HEAD_DIM ** -0.5)).reshape(bsz, s, FOX_HEADS, FOX_HEAD_DIM).transpose(0, 2, 1, 3)
    nb = s // FOX_BLOCK
    q_blocks = q.reshape(bsz, FOX_HEADS, nb, FOX_BLOCK, FOX_HEAD_DIM).transpose(2, 0, 1, 3, 4)
    c_blocks = c.reshape(bsz, FOX_HEADS, nb, FOX_BLOCK).transpose(2, 0, 1, 3)
    k_pos = jnp.arange(s)

    def one_block(args):
        qb, cb, start = args
        logits = jnp.einsum('bhqd,bhkd->bhqk', qb, k).astype(jnp.float32)
        logits = logits + cb[..., :, None] - c[:, :, None, :]
        q_pos = start + jnp.arange(FOX_BLOCK)
        logits = jnp.where(k_pos[None, :] <= q_pos[:, None], logits, -jnp.inf)
        probs = jax.nn.softmax(logits, axis=-1)
        return jnp.einsum('bhqk,bhkd->bhqd', probs.astype(v.dtype), v)

    o = lax.map(one_block, (q_blocks, c_blocks, jnp.arange(nb) * FOX_BLOCK))
    o = o.transpose(1, 0, 3, 2, 4).reshape(bsz, s, FOX_WIDTH)
    o = o * jax.nn.sigmoid(g)
    return o @ w_o

def setup_inputs(seed: int = 0) -> dict:
    key = jax.random.key(seed)
    ks = jax.random.split(key, 32)
    f32 = jnp.float32

    def nrm(k, shape, fan_in, scale=1.0):
        return jax.random.normal(k, shape, f32) * (scale * fan_in ** -0.5)

    def gain(k, shape):
        return 1.0 + 0.02 * jax.random.normal(k, shape, f32)

    def bias(k, shape):
        return 0.02 * jax.random.normal(k, shape, f32)

    gla_in_width = 2 * GLA_KD + 2 * GLA_VD + GLA_RANK
    return {
        "x": jax.random.normal(ks[0], (BATCH, SEQ, D_MODEL), f32),
        "p": jax.random.normal(ks[1], (DEPTH, BATCH, SEQ, PLE_DIM), f32),
        "ffn1_w_in": nrm(ks[2], (DEPTH, D_MODEL, 2 * D_FF), D_MODEL),
        "ffn1_w_out": nrm(ks[3], (DEPTH, D_FF, D_MODEL), D_FF, DEEPNORM_BETA),
        "ln1_g": gain(ks[4], (DEPTH, D_MODEL)),
        "ln1_b": bias(ks[5], (DEPTH, D_MODEL)),
        "gla_w_in": nrm(ks[6], (N_A, D_MODEL, gla_in_width), D_MODEL),
        "gla_w_a2": nrm(ks[7], (N_A, GLA_RANK, GLA_KD), GLA_RANK),
        "gla_b_a": bias(ks[8], (N_A, GLA_KD)),
        "gla_gn_g": gain(ks[9], (N_A, GLA_VD)),
        "gla_gn_b": bias(ks[10], (N_A, GLA_VD)),
        "gla_w_o": nrm(ks[11], (N_A, GLA_VD, D_MODEL), GLA_VD, DEEPNORM_BETA),
        "fox_w_kvf": nrm(ks[12], (D_MODEL, 2 * FOX_WIDTH + FOX_HEADS), D_MODEL),
        "fox_b_f": 2.0 + 2.0 * jax.random.uniform(ks[13], (FOX_HEADS,), f32),
        "fox_w_in": nrm(ks[14], (N_B, D_MODEL, 2 * FOX_WIDTH), D_MODEL),
        "fox_w_o": nrm(ks[15], (N_B, FOX_WIDTH, D_MODEL), FOX_WIDTH, DEEPNORM_BETA),
        "ln2_g": gain(ks[16], (DEPTH, D_MODEL)),
        "ln2_b": bias(ks[17], (DEPTH, D_MODEL)),
        "ffn2_w_in": nrm(ks[18], (DEPTH, D_MODEL, 2 * D_FF), D_MODEL),
        "ffn2_w_out": nrm(ks[19], (DEPTH, D_FF, D_MODEL), D_FF, DEEPNORM_BETA),
        "ple_w_gate": nrm(ks[20], (DEPTH, D_MODEL, D_MODEL), D_MODEL),
        "ple_w_proj": nrm(ks[21], (DEPTH, PLE_DIM, D_MODEL), PLE_DIM, DEEPNORM_BETA),
        "ln3_g": gain(ks[22], (DEPTH, D_MODEL)),
        "ln3_b": bias(ks[23], (DEPTH, D_MODEL)),
    }

def reference(x, p, ffn1_w_in, ffn1_w_out, ln1_g, ln1_b, gla_w_in, gla_w_a2, gla_b_a, gla_gn_g,
              gla_gn_b, gla_w_o, fox_w_kvf, fox_b_f, fox_w_in, fox_w_o, ln2_g, ln2_b,
              ffn2_w_in, ffn2_w_out, ple_w_gate, ple_w_proj, ln3_g, ln3_b):
    k_sh = v_sh = c_sh = None
    for i in range(DEPTH):
        if i == N_A:
            k_sh, v_sh, c_sh = fox_shared_kv(x, fox_w_kvf, fox_b_f)
        x = layer_norm(DEEPNORM_ALPHA * x + 0.5 * swiglu(x, ffn1_w_in[i], ffn1_w_out[i]),
                       ln1_g[i], ln1_b[i])
        if i < N_A:
            mix = gla_mixer(x, gla_w_in[i], gla_w_a2[i], gla_b_a[i], gla_gn_g[i], gla_gn_b[i], gla_w_o[i])
        else:
            j = i - N_A
            mix = fox_mixer(x, k_sh, v_sh, c_sh, fox_w_in[j], fox_w_o[j])
        x = layer_norm(DEEPNORM_ALPHA * x + mix, ln2_g[i], ln2_b[i])
        ple = jax.nn.sigmoid(x @ ple_w_gate[i]) * (p[i] @ ple_w_proj[i])
        x = layer_norm(DEEPNORM_ALPHA * x + 0.5 * swiglu(x, ffn2_w_in[i], ffn2_w_out[i]) + ple,
                       ln3_g[i], ln3_b[i])
    return x


_drawn_inputs = setup_inputs


def setup_inputs(seed=0):
    import zlib

    import numpy as np

    out = dict(_drawn_inputs(seed))
    spreads = {}
    factors = {'gla_w_a2': 2.913,
     'gla_b_a': 8.0,
     'gla_gn_g': 26.735,
     'gla_gn_b': 27.406,
     'fox_b_f': 30.576}
    for name, (base, spread) in spreads.items():
        noise = np.random.default_rng([zlib.crc32(name.encode()), seed]).standard_normal(out[name].shape)
        drawn = base * np.exp(spread * noise) if base else spread * noise
        out[name] = __import__('jax').numpy.asarray(drawn.astype(out[name].dtype))
    for name, factor in factors.items():
        out[name] = (out[name] * factor).astype(out[name].dtype)
    return out
```

```python
import concourse.bass as bass
from concourse import mybir
from contextlib import ExitStack


def trunk(nc, x_in, p_in, ffn1_w_in, ffn1_w_out, ln1_g, ln1_b, gla_w_in, gla_w_a2, gla_b_a,
          gla_gn_g, gla_gn_b, gla_w_o, fox_w_kvf, fox_b_f, fox_w_in, fox_w_o, ln2_g, ln2_b,
          ffn2_w_in, ffn2_w_out, ple_w_gate, ple_w_proj, ln3_g, ln3_b, out):
    f32 = mybir.dt.float32
    f32r = mybir.dt.float32r
    u32 = mybir.dt.uint32
    ALU = mybir.AluOpType
    ACT = mybir.ActivationFunctionType

    P = 128
    TOK = x_in.shape[1]
    DM = x_in.shape[2]
    TB = TOK // P
    KT = DM // P
    DEPTH = p_in.shape[0]
    FF = ffn1_w_out.shape[1]
    HC = 256
    NCH = FF // HC
    FU = 3 * NCH
    WU = 2048
    NS = 3
    LOADS = 32
    ALPHA = (2 * DEPTH) ** 0.25
    EPS = 1e-5
    GH, DK, DV, RANK, CH = 4, 128, 256, 16, 64
    NC = TOK // CH
    TAU = 16.0
    FH, FD = 16, 64
    NEG = -1.0e30
    LAST_J = NCH - 1

    FFN1_0 = 0
    PP_0 = FFN1_0 + FU
    GLA_Q = PP_0 + 1
    GLA_K = GLA_Q + 2
    GLA_V = GLA_K + 2
    GLA_R = GLA_V + 4
    GLA_O = GLA_R + 4
    GATE_0 = GLA_O + 4
    FFN2_0 = GATE_0 + 4
    PP_1 = FFN2_0 + FU
    FFN1_1 = PP_1 + 1
    FOX_K = FFN1_1 + FU
    FOX_V = FOX_K + 4
    FOX_Q = FOX_V + 4
    FOX_G = FOX_Q + 4
    FOX_O = FOX_G + 4
    GATE_1 = FOX_O + 4
    FFN2_1 = GATE_1 + 4
    UNITS = FFN2_1 + FU
    FFN_BASE = [FFN1_0, FFN2_0, FFN1_1, FFN2_1]
    FFN_X = [0, 2, 3, 5]
    LN_BANK = [[4, 6], [4, 2], [4, 6], [4, 6], [0, 2], [4, 6]]
    LN_SCALE = [0.5, 1.0, 0.5, 0.5, 1.0, 0.5]
    X_BANK = [[0, 2], [4, 6], [0, 6], [4, 6], [4, 6], [4, 6]]

    w_in = [ffn1_w_in[0], ffn2_w_in[0], ffn1_w_in[1], ffn2_w_in[1]]
    w_out = [ffn1_w_out[0], ffn2_w_out[0], ffn1_w_out[1], ffn2_w_out[1]]
    ln_g = [ln1_g[0], ln2_g[0], ln3_g[0], ln1_g[1], ln2_g[1], ln3_g[1]]
    ln_b = [ln1_b[0], ln2_b[0], ln3_b[0], ln1_b[1], ln2_b[1], ln3_b[1]]

    def spread(vector):
        return vector.unsqueeze(0).broadcast_to([P, vector.shape[0]])

    def square(w, cols, q, n):
        return w[q * 512:(q + 1) * 512, cols + n * 512:cols + (n + 1) * 512] \
            .rearrange("(k p) c -> p k c", p=P)

    ctx = ExitStack()
    with ctx:
        def sb(name, shape, dt=f32):
            return ctx.enter_context(nc.sbuf_tensor(name, shape, dt))

        def sem(name):
            return ctx.enter_context(nc.semaphore(name))

        raw = sb("raw", [P, NS, WU])
        whi = sb("whi", [P, NS, WU], f32r)
        wlo = sb("wlo", [P, NS, WU], f32r)
        x = sb("x", [P, TB, DM])
        res = sb("res", [P, TB, DM])
        xhi = sb("xhi", [P, KT, TOK], f32r)
        xlo = sb("xlo", [P, KT, TOK], f32r)
        hhi = sb("hhi", [P, TB, 2, P], f32r)
        hlo = sb("hlo", [P, TB, 2, P], f32r)
        phi = sb("phi", [P, DEPTH, TB, 2, P], f32r)
        plo = sb("plo", [P, DEPTH, TB, 2, P], f32r)
        hid = sb("hid", [P, 2, TB, HC])
        pp = sb("pp", [P, TB, DM])
        gb = sb("gb", [P, 2, DM])
        mix = sb("mix", [P, 7 * 2048 + 768])
        pad = sb("pad", [P, TB, P])
        aT = sb("aT", [RANK, TOK])
        wa2 = sb("wa2", [RANK, GH * DK])
        ba = sb("ba", [P, GH])
        bf = sb("bf", [P, FH])
        sraw = sb("sraw", [P, 2, KT, RANK])
        shi = sb("shi", [P, 2, KT, RANK], f32r)
        slo = sb("slo", [P, 2, KT, RANK], f32r)
        ident = sb("ident", [P, P])
        chunk_mask = sb("chunk_mask", [P, P])
        stats = sb("stats", [P, 8, 6])
        mv = sb("mv", [P, 8, 2])
        rstd = sb("rstd", [P, 8])
        mhalf = sb("mhalf", [P, 8])
        dec = sb("dec", [P, GH * NC])
        lf = sb("lf", [P, 2, TB, FH])
        ct = sb("ct", [P, TB, FH])
        cT = sb("cT", [P, TOK])
        ones16 = sb("ones16", [FH, TOK])
        nmax = sb("nmax", [P, FH, TB])
        rsum = sb("rsum", [P, TB, FH])
        rinv = sb("rinv", [P, TB, FH])
        ps = ctx.enter_context(nc.psum_tensor("ps", [P, 8, 512], f32))
        c_dram = nc.dram_tensor("c_scratch", (FH, TOK), f32, kind="Internal").ap()

        def part(at, n):
            return mix[:, at:at + n]

        p_raw = part(0, 1024).rearrange("p (l b c) -> p l b c", l=DEPTH, b=TB)
        g_v = part(0, 2048).rearrange("p (b c) -> p b c", b=TB)
        g_sr = part(2048, 2048).rearrange("p (b c) -> p b c", b=TB)
        gn = part(4096, 2048).rearrange("p (a c) -> p a c", a=2)
        cs = part(6144, 1024)
        lg = part(7168, 1024)
        qd = part(8192, 1024)
        ki = part(9216, 1024)
        ks = part(10240, 1024)
        state = part(11264, 3072).rearrange("p (n c) -> p n c", n=3)
        fresh = part(11264 + 2048, 1024)
        attn = cs
        kst = lg
        g_bs = [ks, ki]
        f_k = part(0, 2048).rearrange("p (m t) -> p m t", t=TOK)
        f_v = part(2048, 2048).rearrange("p (b c) -> p b c", b=TB)
        f_q = part(4096, 2048).rearrange("p (m t) -> p m t", t=TOK)
        f_th = part(6144, 2048).rearrange("p (b c) -> p b c", b=TB)
        c0 = part(8192, 2048).rearrange("p (h s) -> p h s", h=FH)
        c1 = part(10240, 4096).rearrange("p (h s) -> p h s", h=FH)
        f_pT = part(7 * 2048, 768).rearrange("p (r c) -> p r c", r=2)
        f_l = hid[:, :, :, :].rearrange("p a b c -> p (a b c)")[:, 0:768] \
            .rearrange("p (r c) -> p r c", r=2)

        raw_arrived = [sem(f"raw_arrived{s}") for s in range(NS)]
        names = """x_loaded p_loaded wa2_loaded ba_loaded bf_loaded narrow_loaded gn_loaded
            gb_loaded hi_ready lo_ready unit_used narrow_hi narrow_lo ident_ready mask_ready
            const_ready x_flipped xT_hi xT_ready p_flipped pT_hi pT_ready silu_ready h_ready
            h_flipped hT_hi hT_ready tb0_done stats_ready rstd_ready x_ready res_ready
            pp_read gate_tanh gate_read alr_done alr_read aT_done aT_ready zT_done zb_ready
            nz_ready log_ready cs_ready qd_ready ki_ready v_read kst_flipped kst_ready attn_done
            attn_ready kv_done state_ready sr_ready gs_ready o_done ohat_ready on_ready
            o_flipped oT_hi oT_ready f_done f_ready lf_ready lfT_done cT_ready ctT_done ct_ready
            c_stored c_spread c_ready kT_ready fv_read qT_ready th_ready qk_done l_ready p_ready
            prob_flipped pT_read pv_done half_read act_step dve_step pool_step stored""".split()
        S = {n: sem(n) for n in names}

        def arrived(n):
            return LOADS * (n // NS + 1)

        block = ctx.enter_context(nc.Block())

        @block.sync
        def _(sp):
            def unit_halves(n, s, first, second, wait):
                if wait is not None:
                    sp.wait_ge(S["lo_ready"], wait)
                for h, src in enumerate((first, second)):
                    k = src.shape[1]
                    dst = raw[:, s, h * 1024:(h + 1) * 1024].rearrange("p (k c) -> p k c", k=k)
                    sp.dma_start(dst, src).then_inc(raw_arrived[s], 16)

            def unit(n, src):
                k = src.shape[1] // 2
                unit_halves(n, n % NS, src[:, 0:k, :], src[:, k:2 * k, :],
                            n - 2 if n >= NS else None)

            def ffn_in(f, j, q, n, s, wait):
                v = w_in[f][q * 512:(q + 1) * 512, :].rearrange("(k p) c -> p k c", p=P)
                if wait is not None:
                    sp.wait_ge(S["lo_ready"], wait)
                dst = raw[:, s, :].rearrange("p (k g c) -> p k g c", k=4, g=2)
                for g in range(2):
                    sp.dma_start(dst[:, :, g, :], v[:, :, bass.ds(j * HC + g * FF, HC)]) \
                        .then_inc(raw_arrived[s], 16)

            def ffn_out(f, j, n, s, wait):
                v = w_out[f].rearrange("(k p) c -> p k c", p=P)
                sp.wait_ge(S["lo_ready"], wait)
                dst = raw[:, s, :].rearrange("p (k c) -> p k c", k=2)
                for h in range(2):
                    sp.dma_start(dst[:, h:h + 1, :], v[:, bass.ds(j * 2 + h, 1), :]) \
                        .then_inc(raw_arrived[s], 16)

            def wait_of(n):
                return n - 2 if isinstance(n, int) is False or n >= NS else None

            def ffn_round(f, b, j):
                n = j * 3 + (b - 1)
                ffn_in(f, j, 0, n, (b + 2) % NS, wait_of(n))
                ffn_in(f, j, 1, n + 1, b % NS, wait_of(n + 1))
                ffn_out(f, j - 1, n + 2, (b + 1) % NS, n)

            def layer_norm_vectors(k):
                if k:
                    sp.wait_ge(S["x_ready"], 2 * k)
                sp.dma_start(gb[:, 0, :], spread(ln_g[k])).then_inc(S["gb_loaded"], 16)
                sp.dma_start(gb[:, 1, :], spread(ln_b[k])).then_inc(S["gb_loaded"], 16)

            def ffn(f, extra):
                b = FFN_BASE[f]
                for q in range(2):
                    ffn_in(f, 0, q, b + q, (b + q) % NS, wait_of(b + q))
                ffn_round(f, b, 1)
                extra()
                with sp.Fori(2, NCH) as j:
                    ffn_round(f, b, j)
                ffn_out(f, LAST_J, b + FU - 1, (b + 2) % NS, b + FU - 3)

            def narrow(i, w, cols):
                sp.dma_start(sraw[:, i, :, :], w[:, cols:cols + RANK]
                             .rearrange("(k p) c -> p k c", p=P)).then_inc(S["narrow_loaded"], 16)

            def constants():
                sp.dma_start(p_raw.rearrange("p l b c -> p (l b) c"),
                             p_in.rearrange("l a (b p) c -> p (l a b) c", p=P)) \
                    .then_inc(S["p_loaded"], 16)
                layer_norm_vectors(0)
                sp.dma_start(gn[:, 0, :], spread(gla_gn_g[0])).then_inc(S["gn_loaded"], 16)
                sp.dma_start(gn[:, 1, :], spread(gla_gn_b[0])).then_inc(S["gn_loaded"], 16)
                sp.dma_start(wa2[:, :], gla_w_a2[0]).then_inc(S["wa2_loaded"], 16)
                with nc.allow_non_contiguous_dma(reason="512 values"):
                    sp.dma_start(ba[:, :], gla_b_a[0].rearrange("(h p) -> p h", p=P)) \
                        .then_inc(S["ba_loaded"], 16)
                sp.dma_start(bf[:, :], spread(fox_b_f)).then_inc(S["bf_loaded"], 16)
                narrow(0, gla_w_in[0], 2 * GH * DK + 2 * GH * DV)
                narrow(1, fox_w_kvf, 2 * FH * FD)

            xv = x_in[0].rearrange("(b p) c -> p b c", p=P)
            sp.dma_start(x[:, :, :], xv).then_inc(S["x_loaded"], 16)
            ffn(0, constants)
            unit(PP_0, ple_w_proj[0].rearrange("(k p) c -> p k c", p=P))
            for i in range(12):
                unit(GLA_Q + i, square(gla_w_in[0], 0, i % 2, i // 2))
                if i == 3:
                    layer_norm_vectors(1)
            for i in range(4):
                unit(GLA_O + i, square(gla_w_o[0], 0, i // 2, i % 2))
            for i in range(4):
                unit(GATE_0 + i, square(ple_w_gate[0], 0, i % 2, i // 2))
            ffn(1, lambda: layer_norm_vectors(2))
            unit(PP_1, ple_w_proj[1].rearrange("(k p) c -> p k c", p=P))
            ffn(2, lambda: layer_norm_vectors(3))
            for i in range(8):
                unit(FOX_K + i, square(fox_w_kvf, 0, i % 2, i // 2))
            for i in range(8):
                unit(FOX_Q + i, square(fox_w_in[0], 0, i % 2, i // 2))
                if i == 5:
                    layer_norm_vectors(4)
            for i in range(4):
                unit(FOX_O + i, square(fox_w_o[0], 0, i // 2, i % 2))
            for i in range(4):
                unit(GATE_1 + i, square(ple_w_gate[1], 0, i % 2, i // 2))
            ffn(3, lambda: layer_norm_vectors(5))
            ov = out[0].rearrange("(b p) c -> p b c", p=P)
            for tb in range(TB):
                sp.wait_ge(S["x_ready"], 2 * 5 + tb + 1)
                sp.dma_start(ov[:, tb, :], x[:, tb, :]).then_inc(S["stored"], 16)
            sp.wait_ge(S["stored"], 32)

        @block.gpsimd
        def _(pool):
            step = 0

            def chain(ins):
                nonlocal step
                ins.then_inc(S["pool_step"], 1)
                step += 1
                pool.wait_ge(S["pool_step"], step)

            chain(pool.memset(ident[:, :], 0.0))
            pool.affine_select(out=ident[:, :], in_=ident[:, :], compare_op=ALU.not_equal, fill=1.0,
                               base=0, pattern=[[-1, P]], channel_multiplier=1) \
                .then_inc(S["ident_ready"], 1)
            pool.memset(mhalf[:, :], -0.5).then_inc(S["const_ready"], 1)
            pool.memset(pad[:, :, :], 0.0).then_inc(S["const_ready"], 1)
            pool.memset(cT[:, :], 0.0).then_inc(S["const_ready"], 1)
            pool.memset(ones16[:, :], 1.0).then_inc(S["const_ready"], 1)
            chain(pool.memset(fresh, 1.0))
            pool.memset(fresh.rearrange("p (n t) -> p n t", t=CH)[:, :, 0:1], 0.0) \
                .then_inc(S["const_ready"], 1)
            chain(pool.memset(chunk_mask[:, :], 1.0))
            chain(pool.affine_select(out=chunk_mask[:, :], in_=chunk_mask[:, :],
                                     compare_op=ALU.is_ge, fill=0.0, base=0, pattern=[[1, P]],
                                     channel_multiplier=-1))
            pool.memset(chunk_mask[0:CH, CH:P], 0.0).then_inc(S["mask_ready"], 1)

            def reciprocal_deviation(count, n):
                pool.wait_ge(S["stats_ready"], count)
                chain(pool.tensor_scalar(rstd[:, 0:n].unsqueeze(2), mv[:, 0:n, 1:2], EPS, None,
                                         ALU.add))
                pool.tensor_tensor(rstd[:, 0:n], rstd[:, 0:n], mhalf[:, 0:n], ALU.pow) \
                    .then_inc(S["rstd_ready"], 1)

            pool.wait_ge(S["const_ready"], 1)
            reciprocal_deviation(1, 1)
            reciprocal_deviation(2, 1)
            pool.wait_ge(S["gn_loaded"], 32)

            def gated_vectors(c):
                sr = g_sr[:, :, c * 512:(c + 1) * 512]
                bs = g_bs[c].rearrange("p (b c) -> p b c", b=TB)
                pool.wait_ge(S["sr_ready"], c + 1)

                def vec(i):
                    return gn[:, i, c * 512:(c + 1) * 512].unsqueeze(1).broadcast_to([P, TB, 512])
                chain(pool.tensor_tensor(bs, sr, vec(1), ALU.mult))
                pool.tensor_tensor(sr, sr, vec(0), ALU.mult).then_inc(S["gs_ready"], 1)

            pool.wait_ge(S["kst_flipped"], 2)
            gated_vectors(0)
            reciprocal_deviation(3, 8)
            pool.wait_ge(S["attn_done"], 1)
            gated_vectors(1)
            for k in range(1, 4):
                for tb in range(TB):
                    reciprocal_deviation(2 * k + tb + 2, 1)
            pool.wait_ge(S["cT_ready"], 1)
            pool.dma_start(c_dram, cT[0:FH, :]).then_inc(S["c_stored"], 16)
            pool.wait_ge(S["c_stored"], 16)
            pool.dma_start(c1.rearrange("p h s -> p (h s)"), spread(c_dram.rearrange("h s -> (h s)"))) \
                .then_inc(S["c_spread"], 16)
            pool.wait_ge(S["c_spread"], 16)
            pool.wait_ge(S["ct_ready"], 1)
            for h in range(FH):
                last = pool.tensor_scalar(c0[:, h, :], c1[:, h, 0:P], -1.0, ct[:, 0, h:h + 1],
                                          ALU.mult, ALU.add)
            chain(last)
            for h in range(FH):
                last = pool.tensor_scalar(c1[:, h, :], c1[:, h, :], -1.0, ct[:, 1, h:h + 1],
                                          ALU.mult, ALU.add)
            chain(last)
            for c in (c0, c1[:, :, P:2 * P]):
                pool.affine_select(out=c, in_=c, compare_op=ALU.is_ge, fill=NEG, base=0,
                                   pattern=[[0, FH], [-1, P]], channel_multiplier=1) \
                    .then_inc(S["c_ready"], 1)
            for k in range(4, 6):
                for tb in range(TB):
                    reciprocal_deviation(2 * k + tb + 2, 1)

        @block.scalar
        def _(act):
            step = 0

            def chain(ins):
                nonlocal step
                ins.then_inc(S["act_step"], 1)
                step += 1
                act.wait_ge(S["act_step"], step)

            def split(n, s, arrivals, used):
                act.wait_ge(raw_arrived[s], arrivals)
                if used is not None:
                    act.wait_ge(S["unit_used"], used)
                act.copy(whi[:, s, :], raw[:, s, :]).then_inc(S["hi_ready"], 1)

            def units(a, b):
                for n in range(a, b):
                    split(n, n % NS, arrived(n), n - 2 if n >= NS else None)

            def x_transposed(v, tb):
                act.wait_ge(S["x_flipped"], 2 * v + tb + 1)
                b = X_BANK[v][tb]
                act.copy(xhi[:, :, tb * P:(tb + 1) * P],
                         ps[:, b:b + 2, :].rearrange("p a (k t) -> p (a k) t", t=P)) \
                    .then_inc(S["xT_hi"], 1)

            def residual(v, tb):
                if v:
                    act.wait_ge(S["x_ready"], 2 * (v - 1) + tb + 1)
                act.mul(res[:, tb, :], x[:, tb, :], ALPHA).then_inc(S["res_ready"], 1)

            def hidden_hi(it):
                act.wait_ge(S["h_flipped"], it + 1)
                act.copy(hhi[:, :, :, :].rearrange("p b k t -> p b (k t)"), ps[:, 2:4, 0:HC]) \
                    .then_inc(S["hT_hi"], 1)

            def silu(used):
                act.wait_ge(S["unit_used"], used)
                act.activation(hid[:, 0, :, :], ps[:, 0:2, 0:HC], ACT.Silu).then_inc(S["silu_ready"], 1)

            def ffn(f, extra=None):
                b, it = FFN_BASE[f], f * NCH
                units(b + 3, b + 4)
                silu(b + 2)
                units(b + 4, b + 5)
                if extra:
                    extra()
                with act.Fori(1, LAST_J) as j:
                    hidden_hi(j + (it - 1))
                    n = j * 3 + (b + 2)
                    split(n, (b + 2) % NS, (j + (b + 2) // NS + 1) * LOADS, n - 2)
                    silu(j * 3 + (b + 1))
                    split(n + 1, b % NS, (j + (b + 3) // NS + 1) * LOADS, n - 1)
                    split(n + 2, (b + 1) % NS, (j + (b + 4) // NS + 1) * LOADS, n)
                hidden_hi(it + LAST_J - 1)
                units(b + FU - 1, b + FU)
                silu(b + 3 * LAST_J + 1)
                units(b + FU, b + FU + 1) if b + FU < UNITS else None
                hidden_hi(it + LAST_J)
                units(b + FU + 1, b + FU + 2) if b + FU < UNITS else None

            def narrow(i):
                act.wait_ge(S["narrow_loaded"], 32)
                act.copy(shi[:, i, :, :], sraw[:, i, :, :]).then_inc(S["narrow_hi"], 1)

            def p_transposed():
                act.wait_ge(S["p_flipped"], 1)
                act.copy(phi[:, :, :, :, :].rearrange("p l b k t -> p l (b k t)"), ps[:, 2:4, :]) \
                    .then_inc(S["pT_hi"], 1)
                narrow(0)
                narrow(1)

            def half_projection(tb, done, count):
                act.wait_ge(done, count)
                act.mul(pp[:, tb, :], ps[:, 2 * tb:2 * tb + 2, :].rearrange("p a c -> p (a c)"), 0.5) \
                    .then_inc(S["pp_read"], 1)

            def gate(layer, base):
                act.wait_ge(S["res_ready"], 2 * (3 * layer + 2) + 2)
                for n in range(2):
                    act.wait_ge(S["unit_used"], base + 2 * n + 2)
                    for tb in range(TB):
                        b = LN_BANK[3 * layer + 1][tb] + n
                        act.activation(x[:, tb, n * 512:(n + 1) * 512], ps[:, b, :], ACT.Tanh,
                                       scale=0.5).then_inc(S["gate_tanh"], 1)
                    if base + 4 + 1 + n < UNITS:
                        units(base + 4 + 1 + n, base + 4 + 2 + n)

            act.wait_ge(S["x_loaded"], 16)
            for tb in range(TB):
                x_transposed(0, tb)
            units(0, 3)
            for tb in range(TB):
                residual(0, tb)
            ffn(0, p_transposed)

            half_projection(0, S["tb0_done"], 2)
            x_transposed(1, 0)
            half_projection(1, S["unit_used"], PP_0 + 1)
            x_transposed(1, 1)
            residual(1, 0)
            residual(1, 1)
            units(GLA_Q + 1, GLA_Q + 4)
            act.wait_ge(S["nz_ready"], 1)
            chain(act.activation(lg, lg, ACT.Exp))
            act.activation(lg, lg, ACT.Ln, bias=1.0).then_inc(S["log_ready"], 1)
            units(GLA_Q + 4, GLA_Q + 5)
            act.wait_ge(S["cs_ready"], 1)
            act.activation(qd, cs, ACT.Exp, scale=1.0 / TAU).then_inc(S["act_step"], 1)
            act.activation(ki, cs, ACT.Exp, scale=-1.0 / TAU).then_inc(S["act_step"], 1)
            act.activation(ks, ks, ACT.Exp, scale=1.0 / TAU).then_inc(S["act_step"], 1)
            act.activation(dec[:, :], cs.rearrange("p (n t) -> p n t", t=CH)[:, :, CH - 1],
                           ACT.Exp, scale=1.0 / TAU).then_inc(S["act_step"], 1)
            step += 4
            units(GLA_Q + 5, GLA_Q + 8)
            for c in range(2):
                act.wait_ge(S["unit_used"], GLA_V + 2 * c + 2)
                act.copy(g_v[:, :, c * 512:(c + 1) * 512], ps[:, 2 * c:2 * c + 2, :]) \
                    .then_inc(S["v_read"], 1)
                units(GLA_R + 2 * c, GLA_R + 2 * c + 1)
                if c == 0:
                    units(GLA_R + 1, GLA_R + 2)
            units(GLA_R + 3, GLA_R + 4)
            act.wait_ge(S["unit_used"], GLA_R + 2)
            act.activation(g_sr[:, :, 0:512], ps[:, 0:2, :], ACT.Silu).then_inc(S["sr_ready"], 1)
            units(GLA_O, GLA_O + 2)
            act.wait_ge(S["unit_used"], GLA_R + 4)
            act.activation(g_sr[:, :, 512:1024], ps[:, 0:2, :], ACT.Silu).then_inc(S["sr_ready"], 1)
            units(GLA_O + 2, GLA_O + 3)

            def o_transposed(count, half, b):
                act.wait_ge(S["o_flipped"], count)
                act.copy(xhi[:, 4 * half:4 * half + 4, :],
                         ps[:, b:b + 2, :].rearrange("p a (k t) -> p (a k) t", t=TOK)) \
                    .then_inc(S["oT_hi"], 1)

            o_transposed(1, 0, 6)
            units(GLA_O + 3, GLA_O + 4)
            o_transposed(2, 1, 0)
            units(GATE_0, GATE_0 + 2)
            x_transposed(2, 0)
            x_transposed(2, 1)
            residual(2, 0)
            residual(2, 1)
            units(GATE_0 + 2, GATE_0 + 5)
            gate(0, GATE_0)
            ffn(1)

            half_projection(0, S["tb0_done"], 5)
            x_transposed(3, 0)
            half_projection(1, S["unit_used"], PP_1 + 1)
            x_transposed(3, 1)
            residual(3, 0)
            residual(3, 1)
            units(FFN1_1 + 1, FFN1_1 + 3)
            ffn(2)

            act.wait_ge(S["nz_ready"], 2)
            chain(act.activation(lf[:, 1, :, :], lf[:, 1, :, :], ACT.Exp))
            act.activation(lf[:, 1, :, :], lf[:, 1, :, :], ACT.Ln, bias=1.0) \
                .then_inc(S["log_ready"], 1)
            units(FOX_K + 2, FOX_K + 4)
            for c in range(2):
                act.wait_ge(S["unit_used"], FOX_K + 2 * c + 2)
                act.copy(f_k[:, 4 * c:4 * c + 4, :].rearrange("p (a m) t -> p a (m t)", a=2),
                         ps[:, 2 * c:2 * c + 2, :]).then_inc(S["kT_ready"], 1)
                units(FOX_V + 2 * c, FOX_V + 2 * c + 2)
            for c in range(2):
                act.wait_ge(S["unit_used"], FOX_V + 2 * c + 2)
                act.copy(f_v[:, :, c * 512:(c + 1) * 512], ps[:, 2 * c:2 * c + 2, :]) \
                    .then_inc(S["fv_read"], 1)
                if c == 0:
                    units(FOX_Q, FOX_Q + 2)
            x_transposed(4, 0)
            x_transposed(4, 1)
            residual(4, 0)
            residual(4, 1)
            units(FOX_Q + 2, FOX_Q + 4)
            for c in range(2):
                act.wait_ge(S["unit_used"], FOX_Q + 2 * c + 2)
                b = 2 + 2 * c
                act.mul(f_q[:, 4 * c:4 * c + 4, :].rearrange("p (a m) t -> p a (m t)", a=2),
                        ps[:, b:b + 2, :], FD ** -0.5).then_inc(S["qT_ready"], 1)
                units(FOX_G + 2 * c, FOX_G + 2 * c + 1)
                if c == 0:
                    units(FOX_G + 1, FOX_G + 2)

            def softmax_exp(h):
                r = h % 2
                act.wait_ge(S["l_ready"], 2 * h + 2)
                for tb, (a, n) in enumerate(((0, P), (P, 2 * P))):
                    act.activation(f_l[:, r, a:a + n], f_l[:, r, a:a + n], ACT.Exp, scale=-1.0,
                                   bias=nmax[:, h, tb:tb + 1], accum_out=rsum[:, tb, h:h + 1]) \
                        .then_inc(S["p_ready"], 1)

            def gate_half(c):
                act.wait_ge(S["unit_used"], FOX_G + 2 * c + 2)
                act.activation(f_th[:, :, c * 512:(c + 1) * 512], ps[:, 6:8, :], ACT.Tanh,
                               scale=0.5).then_inc(S["th_ready"], 1)

            for h in range(4):
                softmax_exp(h)
            units(FOX_G + 3, FOX_G + 4)
            for h in range(4, 8):
                softmax_exp(h)
            gate_half(0)
            units(FOX_O, FOX_O + 1)
            for h in range(8, 12):
                softmax_exp(h)
            units(FOX_O + 1, FOX_O + 2)
            for h in range(12, 16):
                softmax_exp(h)
            gate_half(1)
            units(FOX_O + 2, FOX_O + 3)
            o_transposed(3, 0, 6)
            units(FOX_O + 3, FOX_O + 4)
            o_transposed(4, 1, 4)
            units(GATE_1, GATE_1 + 2)
            x_transposed(5, 0)
            x_transposed(5, 1)
            residual(5, 0)
            residual(5, 1)
            units(GATE_1 + 2, GATE_1 + 5)
            gate(1, GATE_1)
            ffn(3)

        @block.vector
        def _(dve):
            step = 0

            def note(ins):
                nonlocal step
                ins.then_inc(S["dve_step"], 1)
                step += 1

            def settle():
                dve.wait_ge(S["dve_step"], step)

            def split(n, s):
                dve.wait_ge(S["hi_ready"], n + 1)
                dve.tensor_tensor(wlo[:, s, :], raw[:, s, :], whi[:, s, :].bitcast(f32),
                                  ALU.subtract).then_inc(S["lo_ready"], 1)

            def units(a, b):
                for n in range(a, b):
                    split(n, n % NS)

            def x_transposed(v, tb):
                dve.wait_ge(S["xT_hi"], 2 * v + tb + 1)
                b = X_BANK[v][tb]
                dve.tensor_tensor(xlo[:, :, tb * P:(tb + 1) * P],
                                  ps[:, b:b + 2, :].rearrange("p a (k t) -> p (a k) t", t=P),
                                  xhi[:, :, tb * P:(tb + 1) * P].bitcast(f32),
                                  ALU.subtract).then_inc(S["xT_ready"], 1)

            def hidden_lo(it):
                dve.wait_ge(S["hT_hi"], it + 1)
                dve.tensor_tensor(hlo[:, :, :, :].rearrange("p b k t -> p b (k t)"),
                                  ps[:, 2:4, 0:HC],
                                  hhi[:, :, :, :].rearrange("p b k t -> p b (k t)").bitcast(f32),
                                  ALU.subtract).then_inc(S["hT_ready"], 1)

            def hidden(it):
                dve.wait_ge(S["silu_ready"], it + 1)
                dve.tensor_tensor(hid[:, 1, :, :], ps[:, 0:2, HC:2 * HC], hid[:, 0, :, :],
                                  ALU.mult).then_inc(S["h_ready"], 1)

            def ffn(f, extra=None):
                b, it = FFN_BASE[f], f * NCH
                units(b + 3, b + 4)
                hidden(it)
                units(b + 4, b + 5)
                if extra:
                    extra()
                with dve.Fori(1, LAST_J) as j:
                    hidden_lo(j + (it - 1))
                    n = j * 3 + (b + 2)
                    split(n, (b + 2) % NS)
                    hidden(j + it)
                    split(n + 1, b % NS)
                    split(n + 2, (b + 1) % NS)
                hidden_lo(it + LAST_J - 1)
                units(b + FU - 1, b + FU)
                hidden(it + LAST_J)
                units(b + FU, b + FU + 1) if b + FU < UNITS else None
                hidden_lo(it + LAST_J)
                units(b + FU + 1, b + FU + 2) if b + FU < UNITS else None

            def p_transposed():
                dve.wait_ge(S["pT_hi"], 1)
                dve.tensor_tensor(plo[:, :, :, :, :].rearrange("p l b k t -> p l (b k t)"),
                                  ps[:, 2:4, :],
                                  phi[:, :, :, :, :].rearrange("p l b k t -> p l (b k t)").bitcast(f32),
                                  ALU.subtract).then_inc(S["pT_ready"], 1)
                dve.wait_ge(S["narrow_hi"], 2)
                dve.tensor_tensor(slo[:, :, :, :], sraw[:, :, :, :], shi[:, :, :, :].bitcast(f32),
                                  ALU.subtract).then_inc(S["narrow_lo"], 1)

            def sum_and_statistics(k, tb, done_sem, done):
                dve.wait_ge(done_sem, done)
                dve.wait_ge(S["res_ready"], 2 * k + tb + 1)
                for n in range(2):
                    half = res[:, tb, n * 512:(n + 1) * 512]
                    note(dve.scalar_tensor_tensor(out=half, in0=ps[:, LN_BANK[k][tb] + n, :],
                                                  scalar=LN_SCALE[k], in1=half, op0=ALU.mult,
                                                  op1=ALU.add))
                settle()
                for n in range(2):
                    note(dve.bn_stats(stats[:, n, :], res[:, tb, n * 512:(n + 1) * 512]))
                settle()
                dve.bn_aggr(mv[:, 0, :], stats[:, 0:2, :].rearrange("p a b -> p (a b)")) \
                    .then_inc(S["stats_ready"], 1)

            def normalise(k, tb):
                count = 2 * k + tb + 1 + (1 if k else 0)
                dve.wait_ge(S["stats_ready"], count)
                dve.wait_ge(S["gb_loaded"], 32 * (k + 1))
                note(dve.scalar_tensor_tensor(out=res[:, tb, :], in0=res[:, tb, :],
                                              scalar=mv[:, 0, 0:1], in1=gb[:, 0, :],
                                              op0=ALU.subtract, op1=ALU.mult))
                settle()
                dve.wait_ge(S["rstd_ready"], count)
                dve.scalar_tensor_tensor(out=x[:, tb, :], in0=res[:, tb, :], scalar=rstd[:, 0:1],
                                         in1=gb[:, 1, :], op0=ALU.mult, op1=ALU.add) \
                    .then_inc(S["x_ready"], 1)

            def layer_norm(k, done0, done1):
                sum_and_statistics(k, 0, S["tb0_done"], done0)
                normalise(k, 0)
                sum_and_statistics(k, 1, S["unit_used"], done1)
                normalise(k, 1)

            def log_sigmoid_parts(z, nz):
                dve.scalar_tensor_tensor(out=nz, in0=z, scalar=-1.0, in1=z, op0=ALU.mult,
                                         op1=ALU.min).then_inc(S["nz_ready"], 1)

            def gate(layer, base):
                for n in range(2):
                    for tb in range(TB):
                        dve.wait_ge(S["gate_tanh"], 4 * layer + 2 * n + tb + 1)
                        dve.wait_ge(S["pp_read"], 2 * layer + tb + 1)
                        at = slice(n * 512, (n + 1) * 512)
                        note(dve.scalar_tensor_tensor(out=x[:, tb, at], in0=x[:, tb, at], scalar=1.0,
                                                      in1=pp[:, tb, at], op0=ALU.add, op1=ALU.mult))
                        settle()
                        dve.wait_ge(S["res_ready"], 2 * (3 * layer + 2) + 2)
                        ins = dve.tensor_tensor(res[:, tb, at], res[:, tb, at], x[:, tb, at], ALU.add)
                        ins.then_inc(S["gate_read"], 1)
                    units(base + 4 + 1 + n, base + 4 + 2 + n)
                dve.wait_ge(S["gate_read"], 4 * (layer + 1))

            for tb in range(TB):
                x_transposed(0, tb)
            units(0, 3)
            ffn(0, p_transposed)

            layer_norm(0, 1, FFN1_0 + FU)
            x_transposed(1, 0)
            x_transposed(1, 1)
            units(GLA_Q + 1, GLA_Q + 3)

            dve.wait_ge(S["alr_done"], 1)
            dve.wait_ge(S["const_ready"], 5)
            dve.tensor_copy(pad[:, :, 0:RANK], ps[:, 0:2, 0:RANK]).then_inc(S["alr_read"], 1)
            dve.wait_ge(S["aT_done"], 1)
            dve.tensor_copy(aT[:, :], ps[0:RANK, 2, 0:TOK]).then_inc(S["aT_ready"], 1)
            units(GLA_Q + 3, GLA_Q + 4)
            dve.wait_ge(S["zT_done"], 1)
            dve.wait_ge(S["ba_loaded"], 16)
            for h in range(GH):
                note(dve.tensor_scalar(cs[:, h * TOK:(h + 1) * TOK],
                                       ps[:, 2 + h // 2, (h % 2) * TOK:(h % 2 + 1) * TOK],
                                       ba[:, h:h + 1], None, ALU.add))
            settle()
            log_sigmoid_parts(cs, lg)
            units(GLA_Q + 4, GLA_Q + 5)
            dve.wait_ge(S["log_ready"], 1)
            note(dve.scalar_tensor_tensor(out=lg, in0=cs, scalar=0.0, in1=lg, op0=ALU.min,
                                          op1=ALU.subtract))
            settle()
            note(dve.tensor_tensor_scan(cs, fresh, lg, 0.0, ALU.mult, ALU.add))
            settle()
            csv = cs.rearrange("p (n t) -> p n t", t=CH)
            dve.tensor_tensor(ks.rearrange("p (n t) -> p n t", t=CH),
                              csv[:, :, CH - 1:CH].broadcast_to([P, GH * NC, CH]), csv,
                              ALU.subtract).then_inc(S["cs_ready"], 1)
            units(GLA_Q + 5, GLA_Q + 6)
            dve.wait_ge(S["act_step"], 5)
            dve.wait_ge(S["unit_used"], GLA_Q + 2)
            dve.scalar_tensor_tensor(out=qd, in0=ps[:, 4:6, :].rearrange("p a c -> p (a c)"),
                                     scalar=DK ** -0.5, in1=qd, op0=ALU.mult, op1=ALU.mult) \
                .then_inc(S["qd_ready"], 1)
            note(dve.memset(attn, 0.0))
            dve.wait_ge(S["unit_used"], GLA_K + 2)
            for e in (ki, ks):
                dve.tensor_tensor(e, ps[:, 6:8, :].rearrange("p a c -> p (a c)"), e, ALU.mult) \
                    .then_inc(S["ki_ready"], 1)
            units(GLA_Q + 6, GLA_Q + 10)
            for tb in range(TB):
                dve.wait_ge(S["kst_flipped"], tb + 1)
                dve.tensor_copy(kst[:, tb * 512:(tb + 1) * 512], ps[:, 4 + tb, :]) \
                    .then_inc(S["kst_ready"], 1)
            dve.wait_ge(S["attn_done"], 1)
            dve.wait_ge(S["mask_ready"], 1)
            settle()
            for tb in range(TB):
                dve.copy_predicated(attn[:, tb * 512:(tb + 1) * 512].rearrange("p (h t) -> p h t", h=GH),
                                    chunk_mask[:, :].bitcast(u32).unsqueeze(1).broadcast_to([P, GH, P]),
                                    ps[:, 6 + tb, :].rearrange("p (h t) -> p h t", h=GH)) \
                    .then_inc(S["attn_ready"], 1)
            units(GLA_R + 2, GLA_R + 4)
            dve.wait_ge(S["kv_done"], 1)
            note(dve.tensor_copy(state[:, 0, :], ps[:, 4:6, :].rearrange("p a c -> p (a c)")))
            settle()
            for n in (1, 2):
                dve.wait_ge(S["kv_done"], n + 1)
                b = (4, 2, 6)[n]
                for h in range(GH):
                    note(dve.scalar_tensor_tensor(
                        out=state[:, n, h * DV:(h + 1) * DV],
                        in0=state[:, n - 1, h * DV:(h + 1) * DV],
                        scalar=dec[:, h * NC + n:h * NC + n + 1],
                        in1=ps[:, b + h // 2, (h % 2) * DV:(h % 2 + 1) * DV],
                        op0=ALU.mult, op1=ALU.add))
                settle()
            dve.engine_nop().then_inc(S["state_ready"], 1)
            units(GLA_O, GLA_O + 2)

            dve.wait_ge(S["o_done"], 2)
            ob = [4, 2]
            for i in range(8):
                h, tb = i // 2, i % 2
                note(dve.bn_stats(stats[:, i, :],
                                  ps[:, ob[tb] + h // 2, (h % 2) * DV:(h % 2 + 1) * DV]))
            settle()
            for i in range(8):
                note(dve.bn_aggr(mv[:, i, :], stats[:, i, :]))
            settle()
            dve.engine_nop().then_inc(S["stats_ready"], 1)
            dve.wait_ge(S["rstd_ready"], 3)
            for i in range(8):
                h, tb = i // 2, i % 2
                note(dve.tensor_scalar(x[:, tb, h * DV:(h + 1) * DV],
                                       ps[:, ob[tb] + h // 2, (h % 2) * DV:(h % 2 + 1) * DV],
                                       mv[:, i, 0:1], rstd[:, i:i + 1], ALU.subtract, ALU.mult))
            settle()
            dve.engine_nop().then_inc(S["ohat_ready"], 1)

            def gated_output(c):
                v = x[:, :, c * 512:(c + 1) * 512]
                dve.wait_ge(S["gs_ready"], c + 1)
                note(dve.tensor_tensor(v, v, g_sr[:, :, c * 512:(c + 1) * 512], ALU.mult))
                settle()
                dve.tensor_tensor(v, v, g_bs[c].rearrange("p (b c) -> p b c", b=TB), ALU.add) \
                    .then_inc(S["on_ready"], 1)

            def o_transposed(count, half, b):
                dve.wait_ge(S["oT_hi"], count)
                dve.tensor_tensor(xlo[:, 4 * half:4 * half + 4, :],
                                  ps[:, b:b + 2, :].rearrange("p a (k t) -> p (a k) t", t=TOK),
                                  xhi[:, 4 * half:4 * half + 4, :].bitcast(f32),
                                  ALU.subtract).then_inc(S["oT_ready"], 1)

            gated_output(0)
            units(GLA_O + 2, GLA_O + 3)
            o_transposed(1, 0, 6)
            gated_output(1)
            units(GLA_O + 3, GLA_O + 4)
            o_transposed(2, 1, 0)
            units(GATE_0, GATE_0 + 2)
            layer_norm(1, 3, GLA_O + 4)
            x_transposed(2, 0)
            x_transposed(2, 1)
            units(GATE_0 + 2, GATE_0 + 5)
            gate(0, GATE_0)
            ffn(1)

            layer_norm(2, 4, FFN2_0 + FU)
            x_transposed(3, 0)
            x_transposed(3, 1)
            units(FFN1_1 + 1, FFN1_1 + 3)
            ffn(2)

            layer_norm(3, 6, FFN1_1 + FU)
            dve.wait_ge(S["f_done"], 1)
            dve.wait_ge(S["bf_loaded"], 16)
            note(dve.tensor_tensor(lf[:, 0, :, :], ps[:, 2:4, 0:FH],
                                   bf[:, :].unsqueeze(1).broadcast_to([P, TB, FH]), ALU.add))
            settle()
            dve.engine_nop().then_inc(S["f_ready"], 1)
            log_sigmoid_parts(lf[:, 0, :, :], lf[:, 1, :, :])
            dve.wait_ge(S["log_ready"], 2)
            dve.scalar_tensor_tensor(out=pad[:, :, 0:FH], in0=lf[:, 0, :, :], scalar=0.0,
                                     in1=lf[:, 1, :, :], op0=ALU.min, op1=ALU.subtract) \
                .then_inc(S["lf_ready"], 1)
            units(FOX_K + 2, FOX_K + 5)
            dve.wait_ge(S["lfT_done"], 1)
            dve.tensor_tensor_scan(cT[0:FH, :], ones16[:, :], ps[0:FH, 4, 0:TOK], 0.0, ALU.mult,
                                   ALU.add).then_inc(S["cT_ready"], 1)
            units(FOX_K + 5, FOX_K + 7)
            dve.wait_ge(S["ctT_done"], 1)
            dve.tensor_copy(ct[:, :, :], ps[:, 5, 0:TB * P].rearrange("p (b c) -> p b c", b=TB)[:, :, 0:FH]) \
                .then_inc(S["ct_ready"], 1)
            units(FOX_K + 7, FOX_Q + 2)
            x_transposed(4, 0)
            x_transposed(4, 1)
            units(FOX_Q + 2, FOX_G + 3)
            dve.wait_ge(S["c_ready"], 2)

            def logits(h):
                r = h % 2
                dve.wait_ge(S["qk_done"], h + 1)
                if h >= 2:
                    dve.wait_ge(S["prob_flipped"], h - 1)
                for tb, (a, n, c) in enumerate(((0, P, c0), (P, 2 * P, c1))):
                    dve.tensor_tensor_reduce(out=f_l[:, r, a:a + n], in0=ps[:, r, a:a + n],
                                             in1=c[:, h, :], scale=-1.0, scalar=3.0e38,
                                             op0=ALU.add, op1=ALU.min,
                                             accum_out=nmax[:, h, tb:tb + 1]) \
                        .then_inc(S["l_ready"], 1)

            def probs_transposed(h):
                r = h % 2
                dve.wait_ge(S["prob_flipped"], h + 1)
                if h >= 2:
                    dve.wait_ge(S["pv_done"], h - 1)
                dve.tensor_copy(f_pT[:, r, :], ps[:, 2 + r, 0:3 * P]).then_inc(S["pT_read"], 1)

            def head_output(half):
                hs = slice(8 * half, 8 * half + 8)
                dve.wait_ge(S["pv_done"], 8 * half + 8)
                dve.wait_ge(S["p_ready"], 2 * (8 * half + 8))
                note(dve.reciprocal(rinv[:, :, hs], rsum[:, :, hs]))
                settle()
                note(dve.tensor_scalar(rinv[:, :, hs], rinv[:, :, hs], 0.5, None, ALU.mult))
                settle()
                dve.wait_ge(S["th_ready"], half + 1)
                for tb in range(TB):
                    o = x[:, tb, 512 * half:512 * half + 512]
                    note(dve.tensor_tensor(o.rearrange("p (h d) -> p h d", d=FD),
                                           ps[:, 4 + tb, :].rearrange("p (h d) -> p h d", d=FD),
                                           rinv[:, tb, hs].unsqueeze(2).broadcast_to([P, 8, FD]),
                                           ALU.mult))
                settle()
                for tb in range(TB):
                    at = slice(512 * half, 512 * half + 512)
                    note(dve.scalar_tensor_tensor(out=x[:, tb, at], in0=f_th[:, tb, at], scalar=1.0,
                                                  in1=x[:, tb, at], op0=ALU.add, op1=ALU.mult))
                settle()
                dve.engine_nop().then_inc(S["half_read"], 1)

            for i in range(FH + 1):
                if i < FH:
                    logits(i)
                if i >= 1:
                    probs_transposed(i - 1)
                if i == 4:
                    units(FOX_G + 3, FOX_G + 4)
                if i == 8:
                    units(FOX_O, FOX_O + 1)
                    head_output(0)
                if i == 12:
                    units(FOX_O + 1, FOX_O + 2)
            head_output(1)
            units(FOX_O + 2, FOX_O + 3)
            o_transposed(3, 0, 6)
            units(FOX_O + 3, FOX_O + 4)
            o_transposed(4, 1, 4)
            units(GATE_1, GATE_1 + 2)
            layer_norm(4, 7, FOX_O + 4)
            x_transposed(5, 0)
            x_transposed(5, 1)
            units(GATE_1 + 2, GATE_1 + 5)
            gate(1, GATE_1)
            ffn(3)
            layer_norm(5, 8, UNITS)

        @block.tensor
        def _(pe):
            def product(dst, a, b, start, stop):
                return pe.matmul(dst, a, b, start=start, stop=stop, skip_group_check=True)

            def three(dst, ahi, alo, bhi, blo, first, last):
                product(dst, ahi, bhi, first, False)
                product(dst, ahi, blo, False, False)
                return product(dst, alo, bhi, False, last)

            def use(n):
                pe.wait_ge(S["lo_ready"], n + 1)

            def wide(s, q, tb, bank, cols=512):
                t = slice(tb * P, (tb + 1) * P)
                for k in range(4):
                    at = slice(k * 512, k * 512 + 512)
                    last = three(ps[:, bank, :], xhi[:, 4 * q + k, t], xlo[:, 4 * q + k, t],
                                 whi[:, s, at], wlo[:, s, at], q == 0 and k == 0, q == 1 and k == 3)
                return last

            def feature_major(s, q, banks):
                for m in range(4):
                    dst = ps[:, banks[m // 2], (m % 2) * TOK:(m % 2 + 1) * TOK]
                    for k in range(4):
                        at = slice(k * 512 + m * P, k * 512 + (m + 1) * P)
                        last = three(dst, whi[:, s, at], wlo[:, s, at], xhi[:, 4 * q + k, :],
                                     xlo[:, 4 * q + k, :], q == 0 and k == 0 and m % 2 == 0,
                                     q == 1 and k == 3)
                return last

            def deep(s, hi, lo, tb, banks, first, last):
                for n in range(2):
                    for k in range(2):
                        at = slice(k * 1024 + n * 512, k * 1024 + n * 512 + 512)
                        ins = three(ps[:, banks + n, :], hi[:, tb, k, :], lo[:, tb, k, :],
                                    whi[:, s, at], wlo[:, s, at], first and k == 0,
                                    last and k == 1)
                return ins

            def flip_x(v):
                for tb in range(TB):
                    if v:
                        pe.wait_ge(S["x_ready"], 2 * (v - 1) + tb + 1)
                    for k in range(KT):
                        last = pe.transpose(ps[:, X_BANK[v][tb] + k // 4, (k % 4) * P:(k % 4 + 1) * P],
                                            x[:, tb, k * P:(k + 1) * P], ident[:, :])
                    last.then_inc(S["x_flipped"], 1)

            def xT(v, tb):
                pe.wait_ge(S["xT_ready"], 2 * v + tb + 1)

            def flip_h(it):
                pe.wait_ge(S["h_ready"], it + 1)
                for tb in range(TB):
                    for k in range(2):
                        last = pe.transpose(ps[:, 2 + tb, k * P:(k + 1) * P],
                                            hid[:, 1, tb, k * P:(k + 1) * P], ident[:, :])
                last.then_inc(S["h_flipped"], 1)

            def first_units(n, banks, v):
                for tb in range(TB):
                    xT(v, tb)
                    for q in range(2):
                        use(n + q)
                        last = wide((n + q) % NS, q, tb, banks[tb])
                        if tb == TB - 1:
                            last.then_inc(S["unit_used"], 1)

            def two_units(n, banks):
                for q in range(2):
                    use(n + q)
                    for tb in range(TB):
                        last = wide((n + q) % NS, q, tb, banks[tb])
                    last.then_inc(S["unit_used"], 1)

            def two_feature_units(n, banks):
                for q in range(2):
                    use(n + q)
                    feature_major((n + q) % NS, q, banks).then_inc(S["unit_used"], 1)

            def ffn_in(n, s, q):
                use(n)
                for tb in range(TB):
                    last = wide(s, q, tb, tb)
                last.then_inc(S["unit_used"], 1)

            def ffn_out(n, s, it, first, last):
                pe.wait_ge(S["hT_ready"], it + 1)
                use(n)
                ins = deep(s, hhi, hlo, 0, 4, first, last)
                if last:
                    ins.then_inc(S["tb0_done"], 1)
                deep(s, hhi, hlo, 1, 6, first, last).then_inc(S["unit_used"], 1)

            def ffn(f, flip_banks=None):
                b, it = FFN_BASE[f], f * NCH
                first_units(b, (0, 1), FFN_X[f])
                if flip_banks:
                    flip_banks()

                def turn(j, first=False):
                    n = j * 3 + (b - 1)
                    pe.wait_ge(S["h_ready"], j + it)
                    ffn_in(n, (b + 2) % NS, 0)
                    flip_h(j + (it - 1))
                    ffn_in(n + 1, b % NS, 1)
                    ffn_out(n + 2, (b + 1) % NS, j + (it - 1), first, False)

                turn(1, True)
                with pe.Fori(2, NCH) as j:
                    turn(j)
                flip_h(it + LAST_J)
                ffn_out(b + FU - 1, (b + FU - 1) % NS, it + LAST_J, False, True)

            def projection(layer, n):
                use(n)
                s = n % NS
                deep(s, phi[:, layer], plo[:, layer], 0, 0, True, True).then_inc(S["tb0_done"], 1)
                deep(s, phi[:, layer], plo[:, layer], 1, 2, True, True).then_inc(S["unit_used"], 1)

            def narrow(i, b, done):
                pe.wait_ge(S["narrow_lo"], 1)
                for tb in range(TB):
                    t = slice(tb * P, (tb + 1) * P)
                    for k in range(KT):
                        last = three(ps[:, b + tb, 0:RANK], xhi[:, k, t], xlo[:, k, t],
                                     shi[:, i, k, :], slo[:, i, k, :], k == 0, k == KT - 1)
                last.then_inc(S[done], 1)

            def flip_pad(b, done):
                for tb in range(TB):
                    last = pe.transpose(ps[:, b, tb * P:(tb + 1) * P], pad[:, tb, :], ident[:, :])
                last.then_inc(S[done], 1)

            def flip_o(half, b):
                for k in range(4):
                    for tb in range(TB):
                        last = pe.transpose(
                            ps[:, b + k // 2, (k % 2) * TOK + tb * P:(k % 2) * TOK + (tb + 1) * P],
                            x[:, tb, (4 * half + k) * P:(4 * half + k + 1) * P], ident[:, :])
                last.then_inc(S["o_flipped"], 1)

            def output_units(n, half, count, bank):
                pe.wait_ge(S["oT_ready"], count)
                for c in range(2):
                    use(n + c)
                    for tb in range(TB):
                        last = wide((n + c) % NS, half, tb, bank[tb] + c)
                        if half == 1 and c == 1 and tb == 0:
                            last.then_inc(S["tb0_done"], 1)
                    last.then_inc(S["unit_used"], 1)

            def gate(layer, base):
                bank = LN_BANK[3 * layer + 1]
                first_units(base, bank, 3 * layer + 2)
                two_units(base + 2, [bank[0] + 1, bank[1] + 1])

            pe.wait_ge(S["ident_ready"], 1)
            pe.wait_ge(S["x_loaded"], 16)
            flip_x(0)

            def flip_p():
                pe.wait_ge(S["p_loaded"], 16)
                for layer in range(DEPTH):
                    for tb in range(TB):
                        for k in range(2):
                            i = 2 * tb + k
                            last = pe.transpose(ps[:, 2 + layer, i * P:(i + 1) * P],
                                                p_raw[:, layer, tb, k * P:(k + 1) * P], ident[:, :])
                last.then_inc(S["p_flipped"], 1)
                pe.wait_ge(S["pT_ready"], 1)

            ffn(0, flip_p)
            projection(0, PP_0)
            flip_x(1)

            xT(1, 0)
            xT(1, 1)
            pe.wait_ge(S["pp_read"], 2)
            narrow(0, 0, "alr_done")
            n = GLA_Q
            use(n)
            feature_major(n % NS, 0, (4, 5)).then_inc(S["unit_used"], 1)
            pe.wait_ge(S["alr_read"], 1)
            flip_pad(2, "aT_done")
            use(n + 1)
            feature_major((n + 1) % NS, 1, (4, 5)).then_inc(S["unit_used"], 1)
            pe.wait_ge(S["aT_ready"], 1)
            pe.wait_ge(S["wa2_loaded"], 16)
            for h in range(GH):
                last = pe.matmul(ps[:, 2 + h // 2, (h % 2) * TOK:(h % 2 + 1) * TOK],
                                 wa2[:, h * DK:(h + 1) * DK], aT[:, :], start=True, stop=True)
            last.then_inc(S["zT_done"], 1)
            two_feature_units(GLA_K, (6, 7))
            two_units(GLA_V, (0, 1))
            pe.wait_ge(S["nz_ready"], 1)
            two_units(GLA_V + 2, (2, 3))
            pe.wait_ge(S["qd_ready"], 1)
            pe.wait_ge(S["ki_ready"], 2)
            for tb in range(TB):
                for h in range(GH):
                    last = pe.transpose(ps[:, 4 + tb, h * P:(h + 1) * P],
                                        ks[:, h * TOK + tb * P:h * TOK + (tb + 1) * P], ident[:, :])
                last.then_inc(S["kst_flipped"], 1)
            for tb in range(TB):
                for h in range(GH):
                    t = slice(h * TOK + tb * P, h * TOK + (tb + 1) * P)
                    last = pe.matmul(ps[:, 6 + tb, h * P:(h + 1) * P], ki[:, t], qd[:, t],
                                     start=True, stop=True)
            last.then_inc(S["attn_done"], 1)
            pe.wait_ge(S["v_read"], 1)
            two_units(GLA_R, (0, 1))
            pe.wait_ge(S["v_read"], 2)
            pe.wait_ge(S["kst_ready"], 2)
            pe.wait_ge(S["attn_ready"], 2)
            for c, b in enumerate((4, 2, 6)):
                t = slice((c % 2) * CH, (c % 2 + 1) * CH)
                for h in range(GH):
                    last = pe.matmul(ps[:, b + h // 2, (h % 2) * DV:(h % 2 + 1) * DV],
                                     kst[t, (c // 2) * 512 + h * DK:(c // 2) * 512 + (h + 1) * DK],
                                     g_v[t, c // 2, h * DV:(h + 1) * DV], start=True, stop=True)
                last.then_inc(S["kv_done"], 1)
            pe.wait_ge(S["sr_ready"], 1)
            n = GLA_R + 2
            use(n)
            for tb in range(TB):
                last = wide(n % NS, 0, tb, tb)
            last.then_inc(S["unit_used"], 1)
            pe.wait_ge(S["state_ready"], 1)
            for tb, b in enumerate((4, 2)):
                for h in range(GH):
                    o = ps[:, b + h // 2, (h % 2) * DV:(h % 2 + 1) * DV]
                    last = pe.matmul(o, attn[:, tb * 512 + h * P:tb * 512 + (h + 1) * P],
                                     g_v[:, tb, h * DV:(h + 1) * DV], start=True, stop=False,
                                     skip_group_check=True)
                    for e in range(2):
                        c = 2 * tb + e
                        if c == 0:
                            continue
                        last = pe.matmul(o[e * CH:(e + 1) * CH, :],
                                         qd[:, h * TOK + c * CH:h * TOK + (c + 1) * CH],
                                         state[:, c - 1, h * DV:(h + 1) * DV], start=False,
                                         stop=e == 1, skip_group_check=True)
                last.then_inc(S["o_done"], 1)
            n = GLA_R + 3
            use(n)
            for tb in range(TB):
                last = wide(n % NS, 1, tb, tb)
            last.then_inc(S["unit_used"], 1)
            pe.wait_ge(S["on_ready"], 1)
            flip_o(0, 6)
            pe.wait_ge(S["ohat_ready"], 1)
            output_units(GLA_O, 0, 1, LN_BANK[1])
            pe.wait_ge(S["on_ready"], 2)
            flip_o(1, 0)
            output_units(GLA_O + 2, 1, 2, LN_BANK[1])
            flip_x(2)
            gate(0, GATE_0)
            pe.wait_ge(S["gate_read"], 4)
            ffn(1)
            projection(1, PP_1)
            flip_x(3)
            pe.wait_ge(S["pp_read"], 4)
            ffn(2)

            narrow(1, 2, "f_done")
            two_feature_units(FOX_K, (0, 1))
            pe.wait_ge(S["f_ready"], 1)
            two_feature_units(FOX_K + 2, (2, 3))
            pe.wait_ge(S["lf_ready"], 1)
            flip_pad(4, "lfT_done")
            pe.wait_ge(S["kT_ready"], 1)
            two_units(FOX_V, (0, 1))
            pe.wait_ge(S["cT_ready"], 1)
            for tb in range(TB):
                last = pe.transpose(ps[:, 5, tb * P:(tb + 1) * P], cT[:, tb * P:(tb + 1) * P],
                                    ident[:, :])
            last.then_inc(S["ctT_done"], 1)
            pe.wait_ge(S["kT_ready"], 2)
            two_units(FOX_V + 2, (2, 3))
            pe.wait_ge(S["ct_ready"], 1)
            flip_x(4)
            xT(4, 0)
            xT(4, 1)
            pe.wait_ge(S["fv_read"], 2)
            two_feature_units(FOX_Q, (2, 3))
            two_feature_units(FOX_Q + 2, (4, 5))
            pe.wait_ge(S["qT_ready"], 2)

            def scores(h):
                r = h % 2
                if h >= 2:
                    pe.wait_ge(S["l_ready"], 2 * (h - 1))
                row = slice(r * FD, (r + 1) * FD)
                for tb, (a, n) in enumerate(((0, P), (P, 2 * P))):
                    last = pe.matmul(ps[:, r, a:a + n], f_q[row, h // 2, tb * P:(tb + 1) * P],
                                     f_k[row, h // 2, 0:n], start=True, stop=True)
                last.then_inc(S["qk_done"], 1)

            def flip_probs(h):
                r = h % 2
                pe.wait_ge(S["p_ready"], 2 * h + 2)
                if h >= 2:
                    pe.wait_ge(S["pT_read"], h - 1)
                for i in range(3):
                    last = pe.transpose(ps[:, 2 + r, i * P:(i + 1) * P],
                                        f_l[:, r, i * P:(i + 1) * P], ident[:, :])
                last.then_inc(S["prob_flipped"], 1)

            def values(h):
                pe.wait_ge(S["pT_read"], h + 1)
                if h == 8:
                    pe.wait_ge(S["half_read"], 1)
                r, d = h % 2, slice(h * FD, (h + 1) * FD)
                c = slice((h % 8) * FD, (h % 8 + 1) * FD)
                pe.matmul(ps[:, 4, c], f_pT[:, r, 0:P], f_v[:, 0, d], start=True, stop=True)
                pe.matmul(ps[:, 5, c], f_pT[:, r, P:2 * P], f_v[:, 0, d], start=True, stop=False)
                pe.matmul(ps[:, 5, c], f_pT[:, r, 2 * P:3 * P], f_v[:, 1, d], start=False,
                          stop=True).then_inc(S["pv_done"], 1)

            def gate_unit(i):
                n, q = FOX_G + i, i % 2
                if i == 2:
                    pe.wait_ge(S["th_ready"], 1)
                use(n)
                for tb in range(TB):
                    last = wide(n % NS, q, tb, 6 + tb)
                last.then_inc(S["unit_used"], 1)

            gates = {2: 0, 6: 1, 10: 2, 14: 3}
            for i in range(FH + 2):
                if i < FH:
                    scores(i)
                if 1 <= i <= FH:
                    flip_probs(i - 1)
                if i >= 2:
                    values(i - 2)
                if i in gates:
                    gate_unit(gates[i])
            pe.wait_ge(S["th_ready"], 2)
            pe.wait_ge(S["half_read"], 1)
            flip_o(0, 6)
            output_units(FOX_O, 0, 3, LN_BANK[4])
            pe.wait_ge(S["half_read"], 2)
            flip_o(1, 4)
            output_units(FOX_O + 2, 1, 4, LN_BANK[4])
            flip_x(5)
            gate(1, GATE_1)
            pe.wait_ge(S["gate_read"], 8)
            ffn(3)


_INS = ["x", "p", "ffn1_w_in", "ffn1_w_out", "ln1_g", "ln1_b", "gla_w_in", "gla_w_a2", "gla_b_a",
        "gla_gn_g", "gla_gn_b", "gla_w_o", "fox_w_kvf", "fox_b_f", "fox_w_in", "fox_w_o", "ln2_g",
        "ln2_b", "ffn2_w_in", "ffn2_w_out", "ple_w_gate", "ple_w_proj", "ln3_g", "ln3_b"]


def kernel(**inputs):
    import numpy as _np
    import concourse.bacc as _bacc
    from concourse import mybir as _mybir
    from concourse.bass_utils import run_bass_kernel_spmd as _run

    nc = _bacc.Bacc("TRN2", target_bir_lowering=False, num_devices=1)
    arrays, args = {}, []
    for name in _INS:
        a = _np.ascontiguousarray(inputs[name])
        arrays[f"in_{name}"] = a
        args.append(nc.dram_tensor(f"in_{name}", a.shape, _mybir.dt.from_np(a.dtype),
                                   kind="ExternalInput").ap())
    shape = inputs["x"].shape
    o = nc.dram_tensor("out_0", shape, _mybir.dt.float32, kind="ExternalOutput").ap()
    trunk(nc, *args, o)
    r = _run(nc, [arrays], core_ids=[0])
    return r.results[0]["out_0"]
```

```python
import concourse.bass as bass
from concourse import mybir
from contextlib import ExitStack


def trunk(nc, x_in, p_in, ffn1_w_in, ffn1_w_out, ln1_g, ln1_b, gla_w_in, gla_w_a2, gla_b_a,
          gla_gn_g, gla_gn_b, gla_w_o, fox_w_kvf, fox_b_f, fox_w_in, fox_w_o, ln2_g, ln2_b,
          ffn2_w_in, ffn2_w_out, ple_w_gate, ple_w_proj, ln3_g, ln3_b, out):
    f32 = mybir.dt.float32
    f32r = mybir.dt.float32r
    u32 = mybir.dt.uint32
    ALU = mybir.AluOpType
    ACT = mybir.ActivationFunctionType

    P = 128
    TOK = x_in.shape[1]
    DM = x_in.shape[2]
    TB = TOK // P
    KT = DM // P
    DEPTH = p_in.shape[0]
    FF = ffn1_w_out.shape[1]
    HC = 256
    NCH = FF // HC
    FU = 3 * NCH
    WU = 2048
    NS = 3
    LOADS = 32
    ALPHA = (2 * DEPTH) ** 0.25
    EPS = 1e-5
    GH, DK, DV, RANK, CH = 4, 128, 256, 16, 64
    NC = TOK // CH
    TAU = 16.0
    FH, FD = 16, 64
    NEG = -1.0e30
    LAST_J = NCH - 1

    FFN1_0 = 0
    PP_0 = FFN1_0 + FU
    GLA_V = PP_0 + 1
    GLA_Q = GLA_V + 2
    GLA_K = GLA_Q + 2
    GLA_V2 = GLA_K + 2
    GLA_R = GLA_V2 + 2
    GLA_O = GLA_R + 4
    GATE_0 = GLA_O + 4
    FFN2_0 = GATE_0 + 4
    PP_1 = FFN2_0 + FU
    FFN1_1 = PP_1 + 1
    FOX_K = FFN1_1 + FU
    FOX_V = FOX_K + 4
    FOX_Q = FOX_V + 4
    FOX_G = FOX_Q + 4
    FOX_O = FOX_G + 4
    GATE_1 = FOX_O + 4
    FFN2_1 = GATE_1 + 4
    UNITS = FFN2_1 + FU
    FFN_BASE = [FFN1_0, FFN2_0, FFN1_1, FFN2_1]
    SPLIT_AT_HEAD = {1: FOX_G + 2, 5: FOX_G + 3, 9: FOX_O, 14: FOX_O + 1}
    FFN_X = [0, 2, 3, 5]
    LN_BANK = [[(4, 5), (6, 7)], [(4, 5), (2, 3)], [(4, 5), (6, 7)], [(4, 5), (6, 7)],
               [(6, 2), (7, 3)], [(4, 5), (6, 7)]]
    LN_SCALE = [0.5, 1.0, 0.5, 0.5, 1.0, 0.5]
    X_BANK = {0: (0, 2), 1: (4, 6), 2: (0, 6), 3: (4, 6), 5: (4, 0)}
    X_COUNT = {0: 0, 1: 4, 2: 8, 3: 12, 5: 16}
    H_COUNT = NCH + 2
    T_COUNT = NCH + 1

    w_in = [ffn1_w_in[0], ffn2_w_in[0], ffn1_w_in[1], ffn2_w_in[1]]
    w_out = [ffn1_w_out[0], ffn2_w_out[0], ffn1_w_out[1], ffn2_w_out[1]]
    ln_g = [ln1_g[0], ln2_g[0], ln3_g[0], ln1_g[1], ln2_g[1], ln3_g[1]]
    ln_b = [ln1_b[0], ln2_b[0], ln3_b[0], ln1_b[1], ln2_b[1], ln3_b[1]]

    def spread(vector):
        return vector.unsqueeze(0).broadcast_to([P, vector.shape[0]])

    def square(w, cols, q, n):
        return w[q * 512:(q + 1) * 512, cols + n * 512:cols + (n + 1) * 512] \
            .rearrange("(k p) c -> p k c", p=P)

    ctx = ExitStack()
    with ctx:
        def sb(name, shape, dt=f32):
            return ctx.enter_context(nc.sbuf_tensor(name, shape, dt))

        def sem(name):
            return ctx.enter_context(nc.semaphore(name))

        raw = sb("raw", [P, NS, WU])
        whi = sb("whi", [P, NS, WU], f32r)
        wlo = sb("wlo", [P, NS, WU], f32r)
        x = sb("x", [P, TB, DM])
        res = sb("res", [P, TB, DM])
        xhi = sb("xhi", [P, KT, TOK], f32r)
        xlo = sb("xlo", [P, KT, TOK], f32r)
        hhi = sb("hhi", [P, TB, 2, P], f32r)
        hlo = sb("hlo", [P, TB, 2, P], f32r)
        h2hi = sb("h2hi", [P, TB, 2, P], f32r)
        h2lo = sb("h2lo", [P, TB, 2, P], f32r)
        phi = sb("phi", [P, DEPTH, TB, 2, P], f32r)
        plo = sb("plo", [P, DEPTH, TB, 2, P], f32r)
        hid = sb("hid", [P, 2, TB, HC])
        pp = sb("pp", [P, TB, DM])
        gb = sb("gb", [P, 2, DM])
        mix = sb("mix", [P, 7 * 2048 + 384])
        pad = sb("pad", [P, TB, P])
        ba = sb("ba", [P, GH])
        bf = sb("bf", [P, FH])
        sraw = sb("sraw", [P, 2, KT, RANK])
        shi = sb("shi", [P, 2, KT, RANK], f32r)
        slo = sb("slo", [P, 2, KT, RANK], f32r)
        ident = sb("ident", [P, P])
        chunk_mask = sb("chunk_mask", [P, P])
        stats = sb("stats", [P, 8, 6])
        mv = sb("mv", [P, 8, 2])
        rstd = sb("rstd", [P, 8])
        mhalf = sb("mhalf", [P, 8])
        dec = sb("dec", [P, GH * NC])
        lf = sb("lf", [P, 2, TB, FH])
        ct = sb("ct", [P, TB, FH])
        cT = sb("cT", [P, TOK])
        ones16 = sb("ones16", [FH, TOK])
        nmax = sb("nmax", [P, FH, TB])
        rsum = sb("rsum", [P, TB, FH])
        rinv = sb("rinv", [P, TB, FH])
        ps = ctx.enter_context(nc.psum_tensor("ps", [P, 8, 512], f32))
        c_dram = nc.dram_tensor("c_scratch", (FH, TOK), f32, kind="Internal").ap()

        def part(at, n):
            return mix[:, at:at + n]

        p_raw = part(0, 1024).rearrange("p (l b c) -> p l b c", l=DEPTH, b=TB)
        g_v = part(0, 2048).rearrange("p (b c) -> p b c", b=TB)
        g_sr = part(2048, 2048).rearrange("p (b c) -> p b c", b=TB)
        gn = part(4096, 2048).rearrange("p (a c) -> p a c", a=2)
        cs = part(6144, 1024)
        lg = part(7168, 1024)
        qd = part(8192, 1024)
        ki = part(9216, 1024)
        ks = part(10240, 1024)
        state = part(11264, 3072).rearrange("p (n c) -> p n c", n=3)
        fresh = part(11264 + 2048, 1024)
        attn = cs
        wa2 = mix[0:RANK, 11264:11264 + GH * DK]
        aT = mix[0:RANK, 11776:11776 + TOK]
        kst = lg
        f_k = part(0, 2048).rearrange("p (m t) -> p m t", t=TOK)
        f_v = part(2048, 2048).rearrange("p (b c) -> p b c", b=TB)
        f_q = part(4096, 2048).rearrange("p (m t) -> p m t", t=TOK)
        f_th = part(6144, 2048).rearrange("p (b c) -> p b c", b=TB)
        c0 = part(8192, 2048).rearrange("p (h s) -> p h s", h=FH)
        c1 = part(10240, 4096).rearrange("p (h s) -> p h s", h=FH)
        f_pT = x[:, :, 512:512 + 3 * P]
        hid_flat = hid[:, :, :, :].rearrange("p a b c -> p (a b c)")
        f_l = [hid_flat[:, 0:3 * P], hid_flat[:, 3 * P:6 * P], part(7 * 2048, 3 * P)]

        raw_arrived = [sem(f"raw_arrived{s}") for s in range(NS)]
        names = """x0_loaded x1_loaded p_loaded wa2_loaded ba_loaded bf_loaded narrow_loaded gn_loaded
            gb_loaded hi_ready lo_ready unit_used narrow_hi narrow_lo ident_ready mask_ready
            const_ready x_flipped xT_hi xT_ready p_flipped pT_hi pT_ready silu_ready h_ready
            h_flipped hT_hi hT_ready tb0_done stats_ready rstd_ready x_ready res_ready
            pp_read gate_tanh gate_read alr_done alr_read aT_done aT_ready zT_done gu_half
            nz_ready log_ready cs_ready qd_ready ki_ready v_read kst_flipped kst_ready attn_done
            attn_ready kv_done state_ready sr_ready o_done ohat_ready on_ready
            o_flipped oT_hi oT_ready f_done f_ready lf_ready lfT_done cT_ready ctT_done ct_ready
            c_stored c_spread c_ready kT_ready fv_read qT_ready th_ready qk_done l_ready p_ready
            prob_flipped pT_read pv_done pv_read half_read act_step dve_step pool_step stored""".split()
        S = {n: sem(n) for n in names}

        def arrived(n):
            return LOADS * (n // NS + 1)

        block = ctx.enter_context(nc.Block())

        @block.sync
        def _(sp):
            def unit_halves(n, s, first, second, wait):
                if wait is not None:
                    sp.wait_ge(S["lo_ready"], wait)
                for h, src in enumerate((first, second)):
                    k = src.shape[1]
                    dst = raw[:, s, h * 1024:(h + 1) * 1024].rearrange("p (k c) -> p k c", k=k)
                    sp.dma_start(dst, src).then_inc(raw_arrived[s], 16)

            def unit(n, src):
                k = src.shape[1] // 2
                unit_halves(n, n % NS, src[:, 0:k, :], src[:, k:2 * k, :],
                            n - 2 if n >= NS else None)

            def ffn_in(f, j, q, n, s, wait):
                v = w_in[f][q * 512:(q + 1) * 512, :].rearrange("(k p) c -> p k c", p=P)
                if wait is not None:
                    sp.wait_ge(S["lo_ready"], wait)
                dst = raw[:, s, :].rearrange("p (k g c) -> p k g c", k=4, g=2)
                for g in range(2):
                    sp.dma_start(dst[:, :, g, :], v[:, :, bass.ds(j * HC + g * FF, HC)]) \
                        .then_inc(raw_arrived[s], 16)

            def ffn_out(f, j, n, s, wait):
                v = w_out[f].rearrange("(k p) c -> p k c", p=P)
                sp.wait_ge(S["lo_ready"], wait)
                dst = raw[:, s, :].rearrange("p (k c) -> p k c", k=2)
                for h in range(2):
                    sp.dma_start(dst[:, h:h + 1, :], v[:, bass.ds(j * 2 + h, 1), :]) \
                        .then_inc(raw_arrived[s], 16)

            def wait_of(n):
                return n - 2 if isinstance(n, int) is False or n >= NS else None

            def ffn_round(f, b, j):
                n = j * 3 + (b - 1)
                ffn_in(f, j, 0, n, (b + 2) % NS, wait_of(n))
                ffn_in(f, j, 1, n + 1, b % NS, wait_of(n + 1))
                ffn_out(f, j - 1, n + 2, (b + 1) % NS, n)

            def layer_norm_vectors(k):
                if k:
                    sp.wait_ge(S["x_ready"], 4 * k)
                sp.dma_start(gb[:, 0, :], spread(ln_g[k])).then_inc(S["gb_loaded"], 16)
                sp.dma_start(gb[:, 1, :], spread(ln_b[k])).then_inc(S["gb_loaded"], 16)

            def ffn(f, extra, between=None):
                b = FFN_BASE[f]
                for q in range(2):
                    ffn_in(f, 0, q, b + q, (b + q) % NS, wait_of(b + q))
                    if q == 0 and between:
                        between()
                ffn_round(f, b, 1)
                extra()
                with sp.Fori(2, NCH) as j:
                    ffn_round(f, b, j)
                ffn_out(f, LAST_J, b + FU - 1, (b + 2) % NS, b + FU - 3)

            def narrow(i, w, cols):
                sp.dma_start(sraw[:, i, :, :], w[:, cols:cols + RANK]
                             .rearrange("(k p) c -> p k c", p=P)).then_inc(S["narrow_loaded"], 16)

            def constants():
                sp.dma_start(p_raw.rearrange("p l b c -> p (l b) c"),
                             p_in.rearrange("l a (b p) c -> p (l a b) c", p=P)) \
                    .then_inc(S["p_loaded"], 16)
                layer_norm_vectors(0)
                sp.dma_start(gn[:, 0, :], spread(gla_gn_g[0])).then_inc(S["gn_loaded"], 16)
                sp.dma_start(gn[:, 1, :], spread(gla_gn_b[0])).then_inc(S["gn_loaded"], 16)
                sp.dma_start(wa2, gla_w_a2[0]).then_inc(S["wa2_loaded"], 16)
                with nc.allow_non_contiguous_dma(reason="512 values"):
                    sp.dma_start(ba[:, :], gla_b_a[0].rearrange("(h p) -> p h", p=P)) \
                        .then_inc(S["ba_loaded"], 16)
                sp.dma_start(bf[:, :], spread(fox_b_f)).then_inc(S["bf_loaded"], 16)
                narrow(0, gla_w_in[0], 2 * GH * DK + 2 * GH * DV)
                narrow(1, fox_w_kvf, 2 * FH * FD)

            xv = x_in[0].rearrange("(b p) c -> p b c", p=P)

            def load_x(tb):
                sp.dma_start(x[:, tb, :], xv[:, tb, :]).then_inc(S[f"x{tb}_loaded"], 16)
            load_x(0)
            ffn(0, constants, lambda: load_x(1))
            unit(PP_0, ple_w_proj[0].rearrange("(k p) c -> p k c", p=P))
            for i in range(12):
                unit(GLA_V + i, square(gla_w_in[0], 0, i % 2, (2, 0, 1, 3, 4, 5)[i // 2]))
                if i == 5:
                    layer_norm_vectors(1)
            for i in range(4):
                unit(GLA_O + i, square(gla_w_o[0], 0, i // 2, i % 2))
            for i in range(4):
                unit(GATE_0 + i, square(ple_w_gate[0], 0, i % 2, i // 2))
            ffn(1, lambda: layer_norm_vectors(2))
            unit(PP_1, ple_w_proj[1].rearrange("(k p) c -> p k c", p=P))
            ffn(2, lambda: layer_norm_vectors(3))
            for i in range(4):
                unit(FOX_K + i, square(fox_w_kvf, 0, i % 2, i // 2))
            for i in range(4):
                unit(FOX_V + i, square(fox_w_kvf, 0, i // 2, 2 + i % 2))
            for i in range(8):
                unit(FOX_Q + i, square(fox_w_in[0], 0, i % 2, i // 2))
                if i == 5:
                    layer_norm_vectors(4)
            for i in range(4):
                unit(FOX_O + i, square(fox_w_o[0], 0, i // 2, i % 2))
            for i in range(4):
                unit(GATE_1 + i, square(ple_w_gate[1], 0, i % 2, i // 2))
            ffn(3, lambda: layer_norm_vectors(5))
            ov = out[0].rearrange("(b p) c -> p b c", p=P)
            for i in range(4):
                sp.wait_ge(S["x_ready"], 4 * 5 + i + 1)
                at = slice(i % 2 * 512, i % 2 * 512 + 512)
                sp.dma_start(ov[:, i // 2, at], x[:, i // 2, at]).then_inc(S["stored"], 16)
            sp.wait_ge(S["stored"], 64)

        @block.gpsimd
        def _(pool):
            step = 0

            def chain(ins):
                nonlocal step
                ins.then_inc(S["pool_step"], 1)
                step += 1
                pool.wait_ge(S["pool_step"], step)

            chain(pool.memset(ident[:, :], 0.0))
            pool.affine_select(out=ident[:, :], in_=ident[:, :], compare_op=ALU.not_equal, fill=1.0,
                               base=0, pattern=[[-1, P]], channel_multiplier=1) \
                .then_inc(S["ident_ready"], 1)
            pool.memset(mhalf[:, :], -0.5).then_inc(S["const_ready"], 1)
            pool.memset(pad[:, :, :], 0.0).then_inc(S["const_ready"], 1)
            pool.memset(cT[:, :], 0.0).then_inc(S["const_ready"], 1)
            pool.memset(ones16[:, :], 1.0).then_inc(S["const_ready"], 1)
            chain(pool.memset(fresh, 1.0))
            pool.memset(fresh.rearrange("p (n t) -> p n t", t=CH)[:, :, 0:1], 0.0) \
                .then_inc(S["const_ready"], 1)
            chain(pool.memset(chunk_mask[:, :], 1.0))
            chain(pool.affine_select(out=chunk_mask[:, :], in_=chunk_mask[:, :],
                                     compare_op=ALU.is_ge, fill=0.0, base=0, pattern=[[1, P]],
                                     channel_multiplier=-1))
            pool.memset(chunk_mask[0:CH, CH:P], 0.0).then_inc(S["mask_ready"], 1)

            def reciprocal_deviation(count, at, n):
                pool.wait_ge(S["stats_ready"], count)
                chain(pool.tensor_scalar(rstd[:, at:at + n].unsqueeze(2), mv[:, at:at + n, 1:2],
                                         EPS, None, ALU.add))
                pool.tensor_tensor(rstd[:, at:at + n], rstd[:, at:at + n], mhalf[:, 0:n],
                                   ALU.pow).then_inc(S["rstd_ready"], 1)

            pool.wait_ge(S["const_ready"], 1)
            for tb in range(TB):
                reciprocal_deviation(tb + 1, 0, 1)
            for tb in range(TB):
                reciprocal_deviation(tb + 3, GH * tb, GH)
            for i in range(2 * 3):
                reciprocal_deviation(i + 5, 0, 1)
            pool.wait_ge(S["cT_ready"], 1)
            pool.dma_start(c_dram, cT[0:FH, :]).then_inc(S["c_stored"], 16)
            pool.wait_ge(S["c_stored"], 16)
            pool.dma_start(c1.rearrange("p h s -> p (h s)"), spread(c_dram.rearrange("h s -> (h s)"))) \
                .then_inc(S["c_spread"], 16)
            pool.wait_ge(S["c_spread"], 16)
            pool.wait_ge(S["ct_ready"], 1)
            for h in range(FH):
                last = pool.tensor_scalar(c0[:, h, :], c1[:, h, 0:P], -1.0, ct[:, 0, h:h + 1],
                                          ALU.mult, ALU.add)
            chain(last)
            for h in range(FH):
                last = pool.tensor_scalar(c1[:, h, :], c1[:, h, :], -1.0, ct[:, 1, h:h + 1],
                                          ALU.mult, ALU.add)
            chain(last)
            for c in (c0, c1[:, :, P:2 * P]):
                pool.affine_select(out=c, in_=c, compare_op=ALU.is_ge, fill=NEG, base=0,
                                   pattern=[[0, FH], [-1, P]], channel_multiplier=1) \
                    .then_inc(S["c_ready"], 1)
            for i in range(2 * 3, 2 * 5):
                reciprocal_deviation(i + 5, 0, 1)

        @block.scalar
        def _(act):
            step = 0

            def chain(ins):
                nonlocal step
                ins.then_inc(S["act_step"], 1)
                step += 1
                act.wait_ge(S["act_step"], step)

            def split(n, s, arrivals, used):
                act.wait_ge(raw_arrived[s], arrivals)
                if used is not None:
                    act.wait_ge(S["unit_used"], used)
                act.copy(whi[:, s, :], raw[:, s, :]).then_inc(S["hi_ready"], 1)

            def units(a, b):
                for n in range(a, b):
                    split(n, n % NS, arrived(n), n - 2 if n >= NS else None)

            def x_transposed(v, tb):
                for half in range(2):
                    act.wait_ge(S["x_flipped"], X_COUNT[v] + 2 * tb + half + 1)
                    act.copy(xhi[:, 4 * half:4 * half + 4, tb * P:(tb + 1) * P],
                             ps[:, X_BANK[v][tb] + half, :].rearrange("p (k t) -> p k t", t=P)) \
                        .then_inc(S["xT_hi"], 1)

            def residual(v, tb):
                if v:
                    act.wait_ge(S["x_ready"], 4 * (v - 1) + 2 * tb + 2)
                act.mul(res[:, tb, :], x[:, tb, :], ALPHA).then_inc(S["res_ready"], 1)

            def hidden_hi(count):
                act.wait_ge(S["h_flipped"], count)
                act.copy(hhi[:, :, :, :].rearrange("p b k t -> p b (k t)"), ps[:, 2:4, 0:HC]) \
                    .then_inc(S["hT_hi"], 1)

            def last_hidden_hi(f, tb):
                act.wait_ge(S["h_flipped"], T_COUNT * f + NCH + tb)
                act.copy(h2hi[:, tb, :, :].rearrange("p k t -> p (k t)"), ps[:, 2 + tb, 0:HC]) \
                    .then_inc(S["hT_hi"], 1)

            def silu(used):
                act.wait_ge(S["unit_used"], used)
                act.activation(hid[:, 0, :, :], ps[:, 0:2, 0:HC], ACT.Silu).then_inc(S["silu_ready"], 1)

            def silu_block(tb, done, count):
                act.wait_ge(done, count)
                act.activation(hid[:, 0, tb, :], ps[:, tb, 0:HC], ACT.Silu) \
                    .then_inc(S["silu_ready"], 1)

            def ffn(f, extra=None):
                b, it = FFN_BASE[f], f * T_COUNT
                silu_block(0, S["gu_half"], 2 * f + 1)
                units(b + 3, b + 4)
                silu_block(1, S["unit_used"], b + 2)
                if extra:
                    extra()
                units(b + 4, b + 5)
                with act.Fori(1, LAST_J) as j:
                    hidden_hi(j + it)
                    n = j * 3 + (b + 2)
                    split(n, (b + 2) % NS, (j + (b + 2) // NS + 1) * LOADS, n - 2)
                    silu(j * 3 + (b + 1))
                    split(n + 1, b % NS, (j + (b + 3) // NS + 1) * LOADS, n - 1)
                    split(n + 2, (b + 1) % NS, (j + (b + 4) // NS + 1) * LOADS, n)
                hidden_hi(it + LAST_J)
                silu_block(0, S["gu_half"], 2 * f + 2)
                units(b + FU - 1, b + FU)
                last_hidden_hi(f, 0)
                silu_block(1, S["unit_used"], b + 3 * LAST_J + 1)
                units(b + FU, min(b + FU + 1, UNITS))
                last_hidden_hi(f, 1)
                units(b + FU + 1, b + FU + 2) if b + FU < UNITS else None

            def narrow(i):
                act.wait_ge(S["narrow_loaded"], 32)
                act.copy(shi[:, i, :, :], sraw[:, i, :, :]).then_inc(S["narrow_hi"], 1)

            def p_transposed():
                act.wait_ge(S["p_flipped"], 1)
                act.copy(phi[:, :, :, :, :].rearrange("p l b k t -> p l (b k t)"), ps[:, 2:4, :]) \
                    .then_inc(S["pT_hi"], 1)
                narrow(0)
                narrow(1)

            def half_projection(tb, done, count):
                act.wait_ge(done, count)
                act.mul(pp[:, tb, :], ps[:, 2 * tb:2 * tb + 2, :].rearrange("p a c -> p (a c)"), 0.5) \
                    .then_inc(S["pp_read"], 1)

            def gate(layer, base):
                act.wait_ge(S["res_ready"], 2 * (3 * layer + 2) + 2)
                for n in range(2):
                    act.wait_ge(S["unit_used"], base + 2 * n + 2)
                    for tb in range(TB):
                        b = LN_BANK[3 * layer + 1][tb][n]
                        act.activation(x[:, tb, n * 512:(n + 1) * 512], ps[:, b, :], ACT.Tanh,
                                       scale=0.5).then_inc(S["gate_tanh"], 1)
                    if base + 4 + 1 + n < UNITS:
                        units(base + 4 + 1 + n, base + 4 + 2 + n)

            def o_transposed(count, half, b):
                act.wait_ge(S["o_flipped"], count)
                act.copy(xhi[:, 4 * half:4 * half + 4, :],
                         ps[:, b:b + 2, :].rearrange("p a (k t) -> p (a k) t", t=TOK)) \
                    .then_inc(S["oT_hi"], 1)

            x_transposed(0, 0)
            units(0, 1)
            x_transposed(0, 1)
            units(1, 3)
            act.wait_ge(S["x0_loaded"], 16)
            act.wait_ge(S["x1_loaded"], 16)
            for tb in range(TB):
                residual(0, tb)
            ffn(0, p_transposed)

            units(GLA_V + 1, GLA_V + 2)
            half_projection(0, S["tb0_done"], 2)
            x_transposed(1, 0)
            half_projection(1, S["unit_used"], PP_0 + 1)
            units(GLA_Q, GLA_Q + 1)
            x_transposed(1, 1)
            units(GLA_Q + 1, GLA_Q + 2)

            def v_read(c, used):
                act.wait_ge(S["unit_used"], used)
                act.copy(g_v[:, :, c * 512:(c + 1) * 512], ps[:, 2 * c:2 * c + 2, :]) \
                    .then_inc(S["v_read"], 1)

            v_read(0, GLA_V + 2)
            units(GLA_K, GLA_K + 1)
            residual(1, 0)
            residual(1, 1)
            units(GLA_K + 1, GLA_V2 + 1)
            act.wait_ge(S["nz_ready"], 1)
            chain(act.activation(lg, lg, ACT.Exp))
            act.activation(lg, lg, ACT.Ln, bias=1.0).then_inc(S["log_ready"], 1)
            units(GLA_V2 + 1, GLA_V2 + 2)
            act.wait_ge(S["cs_ready"], 1)
            act.activation(qd, cs, ACT.Exp, scale=1.0 / TAU).then_inc(S["act_step"], 1)
            act.activation(ki, cs, ACT.Exp, scale=-1.0 / TAU).then_inc(S["act_step"], 1)
            act.activation(ks, ks, ACT.Exp, scale=1.0 / TAU).then_inc(S["act_step"], 1)
            act.activation(dec[:, :], cs.rearrange("p (n t) -> p n t", t=CH)[:, :, CH - 1],
                           ACT.Exp, scale=1.0 / TAU).then_inc(S["act_step"], 1)
            step += 4
            units(GLA_R, GLA_R + 2)
            v_read(1, GLA_V2 + 2)
            units(GLA_R + 2, GLA_R + 4)
            for c in range(2):
                act.wait_ge(S["unit_used"], GLA_R + 2 * c + 2)
                act.activation(g_sr[:, :, c * 512:(c + 1) * 512], ps[:, 0:2, :], ACT.Silu) \
                    .then_inc(S["sr_ready"], 1)
                if c == 0:
                    units(GLA_O, GLA_O + 2)
                    o_transposed(1, 0, 6)
            units(GLA_O + 2, GLA_O + 3)
            o_transposed(2, 1, 0)
            units(GLA_O + 3, GATE_0 + 1)
            x_transposed(2, 0)
            units(GATE_0 + 1, GATE_0 + 2)
            residual(2, 0)
            x_transposed(2, 1)
            units(GATE_0 + 2, GATE_0 + 3)
            residual(2, 1)
            units(GATE_0 + 3, GATE_0 + 5)
            gate(0, GATE_0)
            ffn(1)

            units(FFN1_1 + 1, FFN1_1 + 2)
            half_projection(0, S["tb0_done"], 5)
            x_transposed(3, 0)
            half_projection(1, S["unit_used"], PP_1 + 1)
            units(FFN1_1 + 2, FFN1_1 + 3)
            x_transposed(3, 1)
            residual(3, 0)
            residual(3, 1)
            ffn(2)

            units(FOX_K + 2, FOX_K + 3)
            act.wait_ge(S["nz_ready"], 2)
            chain(act.activation(lf[:, 1, :, :], lf[:, 1, :, :], ACT.Exp))
            act.activation(lf[:, 1, :, :], lf[:, 1, :, :], ACT.Ln, bias=1.0) \
                .then_inc(S["log_ready"], 1)
            units(FOX_K + 3, FOX_V)
            for c in range(2):
                act.wait_ge(S["unit_used"], FOX_K + 2 * c + 2)
                act.copy(f_k[:, 4 * c:4 * c + 4, :].rearrange("p (a m) t -> p a (m t)", a=2),
                         ps[:, 2 * c:2 * c + 2, :]).then_inc(S["kT_ready"], 1)
                units(FOX_V + 2 * c, FOX_V + 2 * c + 2)
            o_transposed(3, 0, 6)
            units(FOX_Q, FOX_Q + 1)

            def fv_read(c):
                act.wait_ge(S["unit_used"], FOX_V + c + 3)
                act.copy(f_v[:, :, c * 512:(c + 1) * 512], ps[:, 2 * c:2 * c + 2, :]) \
                    .then_inc(S["fv_read"], 1)

            fv_read(0)
            units(FOX_Q + 1, FOX_Q + 2)
            o_transposed(4, 1, 4)
            fv_read(1)
            units(FOX_Q + 2, FOX_Q + 3)
            residual(4, 0)
            residual(4, 1)
            units(FOX_Q + 3, FOX_Q + 4)
            for c in range(2):
                act.wait_ge(S["unit_used"], FOX_Q + 2 * c + 2)
                b = (6, 2)[c]
                act.mul(f_q[:, 4 * c:4 * c + 4, :].rearrange("p (a m) t -> p a (m t)", a=2),
                        ps[:, b:b + 2, :], FD ** -0.5).then_inc(S["qT_ready"], 1)
                if c == 0:
                    units(FOX_G, FOX_G + 2)

            def softmax_exp(h):
                l = f_l[h % 3]
                act.wait_ge(S["l_ready"], 2 * h + 2)
                for tb, (a, n) in enumerate(((0, P), (P, 2 * P))):
                    act.activation(l[:, a:a + n], l[:, a:a + n], ACT.Exp, scale=-1.0,
                                   bias=nmax[:, h, tb:tb + 1], accum_out=rsum[:, tb, h:h + 1]) \
                        .then_inc(S["p_ready"], 1)

            def gate_half(c):
                act.wait_ge(S["unit_used"], FOX_G + 2 * c + 2)
                act.activation(f_th[:, :, c * 512:(c + 1) * 512], ps[:, 6:8, :], ACT.Tanh,
                               scale=0.5).then_inc(S["th_ready"], 1)

            for h in range(FH):
                softmax_exp(h)
                if h in SPLIT_AT_HEAD:
                    n = SPLIT_AT_HEAD[h]
                    units(n, n + 1)
                if h == 7:
                    gate_half(0)
            o_transposed(5, 0, 0)
            gate_half(1)
            units(FOX_O + 2, FOX_O + 3)
            o_transposed(6, 1, 4)
            units(FOX_O + 3, GATE_1 + 1)
            x_transposed(5, 0)
            units(GATE_1 + 1, GATE_1 + 2)
            residual(5, 0)
            x_transposed(5, 1)
            units(GATE_1 + 2, GATE_1 + 3)
            residual(5, 1)
            units(GATE_1 + 3, GATE_1 + 5)
            gate(1, GATE_1)
            ffn(3)

        @block.vector
        def _(dve):
            step = 0

            def note(ins):
                nonlocal step
                ins.then_inc(S["dve_step"], 1)
                step += 1

            def settle():
                dve.wait_ge(S["dve_step"], step)

            def split(n, s):
                dve.wait_ge(S["hi_ready"], n + 1)
                dve.tensor_tensor(wlo[:, s, :], raw[:, s, :], whi[:, s, :].bitcast(f32),
                                  ALU.subtract).then_inc(S["lo_ready"], 1)

            def units(a, b):
                for n in range(a, b):
                    split(n, n % NS)

            def x_transposed(v, tb):
                for half in range(2):
                    dve.wait_ge(S["xT_hi"], X_COUNT[v] + 2 * tb + half + 1)
                    at = slice(4 * half, 4 * half + 4)
                    dve.tensor_tensor(xlo[:, at, tb * P:(tb + 1) * P],
                                      ps[:, X_BANK[v][tb] + half, :]
                                      .rearrange("p (k t) -> p k t", t=P),
                                      xhi[:, at, tb * P:(tb + 1) * P].bitcast(f32),
                                      ALU.subtract).then_inc(S["xT_ready"], 1)

            def hidden_lo(count):
                dve.wait_ge(S["hT_hi"], count)
                dve.tensor_tensor(hlo[:, :, :, :].rearrange("p b k t -> p b (k t)"),
                                  ps[:, 2:4, 0:HC],
                                  hhi[:, :, :, :].rearrange("p b k t -> p b (k t)").bitcast(f32),
                                  ALU.subtract).then_inc(S["hT_ready"], 1)

            def last_hidden_lo(f, tb):
                dve.wait_ge(S["hT_hi"], T_COUNT * f + NCH + tb)
                dve.tensor_tensor(h2lo[:, tb, :, :].rearrange("p k t -> p (k t)"),
                                  ps[:, 2 + tb, 0:HC],
                                  h2hi[:, tb, :, :].rearrange("p k t -> p (k t)").bitcast(f32),
                                  ALU.subtract).then_inc(S["hT_ready"], 1)

            def hidden(count):
                dve.wait_ge(S["silu_ready"], count)
                dve.tensor_tensor(hid[:, 1, :, :], ps[:, 0:2, HC:2 * HC], hid[:, 0, :, :],
                                  ALU.mult).then_inc(S["h_ready"], 1)

            def hidden_block(tb, count):
                dve.wait_ge(S["silu_ready"], count)
                dve.tensor_tensor(hid[:, 1, tb, :], ps[:, tb, HC:2 * HC], hid[:, 0, tb, :],
                                  ALU.mult).then_inc(S["h_ready"], 1)

            def ffn(f, extra=None):
                b, it, ih = FFN_BASE[f], f * T_COUNT, f * H_COUNT
                hidden_block(0, ih + 1)
                units(b + 3, b + 4)
                hidden_block(1, ih + 2)
                if extra:
                    extra()
                units(b + 4, b + 5)
                with dve.Fori(1, LAST_J) as j:
                    hidden_lo(j + it)
                    n = j * 3 + (b + 2)
                    split(n, (b + 2) % NS)
                    hidden(j + (ih + 2))
                    split(n + 1, b % NS)
                    split(n + 2, (b + 1) % NS)
                hidden_lo(it + LAST_J)
                hidden_block(0, ih + H_COUNT - 1)
                units(b + FU - 1, b + FU)
                last_hidden_lo(f, 0)
                hidden_block(1, ih + H_COUNT)
                units(b + FU, min(b + FU + 1, UNITS))
                last_hidden_lo(f, 1)

            def p_transposed():
                dve.wait_ge(S["pT_hi"], 1)
                dve.tensor_tensor(plo[:, :, :, :, :].rearrange("p l b k t -> p l (b k t)"),
                                  ps[:, 2:4, :],
                                  phi[:, :, :, :, :].rearrange("p l b k t -> p l (b k t)").bitcast(f32),
                                  ALU.subtract).then_inc(S["pT_ready"], 1)
                dve.wait_ge(S["narrow_hi"], 2)
                dve.tensor_tensor(slo[:, :, :, :], sraw[:, :, :, :], shi[:, :, :, :].bitcast(f32),
                                  ALU.subtract).then_inc(S["narrow_lo"], 1)

            def sum_and_statistics(k, tb, done_sem, done):
                dve.wait_ge(done_sem, done)
                dve.wait_ge(S["res_ready"], 2 * k + tb + 1)
                for n in range(2):
                    half = res[:, tb, n * 512:(n + 1) * 512]
                    note(dve.scalar_tensor_tensor(out=half, in0=ps[:, LN_BANK[k][tb][n], :],
                                                  scalar=LN_SCALE[k], in1=half, op0=ALU.mult,
                                                  op1=ALU.add))
                settle()
                for n in range(2):
                    note(dve.bn_stats(stats[:, n, :], res[:, tb, n * 512:(n + 1) * 512]))
                settle()
                dve.bn_aggr(mv[:, 0, :], stats[:, 0:2, :].rearrange("p a b -> p (a b)")) \
                    .then_inc(S["stats_ready"], 1)

            def normalise(k, tb):
                count = 2 * k + tb + 1 + (2 if k else 0)
                dve.wait_ge(S["stats_ready"], count)
                dve.wait_ge(S["gb_loaded"], 32 * (k + 1))
                note(dve.scalar_tensor_tensor(out=res[:, tb, :], in0=res[:, tb, :],
                                              scalar=mv[:, 0, 0:1], in1=gb[:, 0, :],
                                              op0=ALU.subtract, op1=ALU.mult))
                settle()
                dve.wait_ge(S["rstd_ready"], count)
                for n in range(2):
                    at = slice(n * 512, (n + 1) * 512)
                    dve.scalar_tensor_tensor(out=x[:, tb, at], in0=res[:, tb, at],
                                             scalar=rstd[:, 0:1], in1=gb[:, 1, at],
                                             op0=ALU.mult, op1=ALU.add).then_inc(S["x_ready"], 1)

            def layer_norm(k, tb, done):
                done_sem = S["unit_used"] if tb else S["tb0_done"]
                sum_and_statistics(k, tb, done_sem, done)
                normalise(k, tb)

            def o_transposed(count, half, b):
                dve.wait_ge(S["oT_hi"], count)
                dve.tensor_tensor(xlo[:, 4 * half:4 * half + 4, :],
                                  ps[:, b:b + 2, :].rearrange("p a (k t) -> p (a k) t", t=TOK),
                                  xhi[:, 4 * half:4 * half + 4, :].bitcast(f32),
                                  ALU.subtract).then_inc(S["oT_ready"], 1)

            def log_sigmoid_parts(z, nz):
                dve.scalar_tensor_tensor(out=nz, in0=z, scalar=-1.0, in1=z, op0=ALU.mult,
                                         op1=ALU.min).then_inc(S["nz_ready"], 1)

            def gate(layer, base):
                for n in range(2):
                    for tb in range(TB):
                        dve.wait_ge(S["gate_tanh"], 4 * layer + 2 * n + tb + 1)
                        dve.wait_ge(S["pp_read"], 2 * layer + tb + 1)
                        at = slice(n * 512, (n + 1) * 512)
                        note(dve.scalar_tensor_tensor(out=x[:, tb, at], in0=x[:, tb, at], scalar=1.0,
                                                      in1=pp[:, tb, at], op0=ALU.add, op1=ALU.mult))
                        settle()
                        dve.wait_ge(S["res_ready"], 2 * (3 * layer + 2) + 2)
                        ins = dve.tensor_tensor(res[:, tb, at], res[:, tb, at], x[:, tb, at], ALU.add)
                        ins.then_inc(S["gate_read"], 1)
                    units(base + 4 + 1 + n, base + 4 + 2 + n)
                dve.wait_ge(S["gate_read"], 4 * (layer + 1))

            x_transposed(0, 0)
            units(0, 1)
            x_transposed(0, 1)
            units(1, 3)
            ffn(0, p_transposed)

            layer_norm(0, 0, 1)
            units(GLA_V, GLA_V + 1)
            x_transposed(1, 0)
            units(GLA_V + 1, GLA_V + 2)
            layer_norm(0, 1, FFN1_0 + FU)
            x_transposed(1, 1)
            units(GLA_Q, GLA_Q + 2)

            dve.wait_ge(S["alr_done"], 1)
            dve.wait_ge(S["const_ready"], 5)
            dve.tensor_copy(pad[:, :, 0:RANK], ps[:, 2:4, 0:RANK]).then_inc(S["alr_read"], 1)
            dve.wait_ge(S["aT_done"], 1)
            dve.tensor_copy(aT, ps[0:RANK, 2, 0:TOK]).then_inc(S["aT_ready"], 1)
            units(GLA_K, GLA_K + 2)
            dve.wait_ge(S["zT_done"], 1)
            dve.wait_ge(S["ba_loaded"], 16)
            for h in range(GH):
                note(dve.tensor_scalar(cs[:, h * TOK:(h + 1) * TOK],
                                       ps[:, 2 + h // 2, (h % 2) * TOK:(h % 2 + 1) * TOK],
                                       ba[:, h:h + 1], None, ALU.add))
            settle()
            log_sigmoid_parts(cs, lg)
            units(GLA_V2, GLA_V2 + 1)
            dve.wait_ge(S["log_ready"], 1)
            note(dve.scalar_tensor_tensor(out=lg, in0=cs, scalar=0.0, in1=lg, op0=ALU.min,
                                          op1=ALU.subtract))
            settle()
            note(dve.tensor_tensor_scan(cs, fresh, lg, 0.0, ALU.mult, ALU.add))
            settle()
            csv = cs.rearrange("p (n t) -> p n t", t=CH)
            dve.tensor_tensor(ks.rearrange("p (n t) -> p n t", t=CH),
                              csv[:, :, CH - 1:CH].broadcast_to([P, GH * NC, CH]), csv,
                              ALU.subtract).then_inc(S["cs_ready"], 1)
            units(GLA_V2 + 1, GLA_V2 + 2)
            dve.wait_ge(S["act_step"], 5)
            dve.wait_ge(S["unit_used"], GLA_Q + 2)
            dve.scalar_tensor_tensor(out=qd, in0=ps[:, 4:6, :].rearrange("p a c -> p (a c)"),
                                     scalar=DK ** -0.5, in1=qd, op0=ALU.mult, op1=ALU.mult) \
                .then_inc(S["qd_ready"], 1)
            note(dve.memset(attn, 0.0))
            dve.wait_ge(S["unit_used"], GLA_K + 2)
            for e in (ki, ks):
                dve.tensor_tensor(e, ps[:, 6:8, :].rearrange("p a c -> p (a c)"), e, ALU.mult) \
                    .then_inc(S["ki_ready"], 1)
            units(GLA_R, GLA_R + 2)
            for tb in range(TB):
                dve.wait_ge(S["kst_flipped"], tb + 1)
                dve.tensor_copy(kst[:, tb * 512:(tb + 1) * 512], ps[:, 4 + tb, :]) \
                    .then_inc(S["kst_ready"], 1)
            dve.wait_ge(S["attn_done"], 1)
            dve.wait_ge(S["mask_ready"], 1)
            settle()
            for tb in range(TB):
                dve.copy_predicated(attn[:, tb * 512:(tb + 1) * 512].rearrange("p (h t) -> p h t", h=GH),
                                    chunk_mask[:, :].bitcast(u32).unsqueeze(1).broadcast_to([P, GH, P]),
                                    ps[:, 6 + tb, :].rearrange("p (h t) -> p h t", h=GH)) \
                    .then_inc(S["attn_ready"], 1)
            units(GLA_R + 2, GLA_R + 3)
            dve.wait_ge(S["kv_done"], 1)
            note(dve.tensor_copy(state[:, 0, :], ps[:, 4:6, :].rearrange("p a c -> p (a c)")))
            settle()
            for n in (1, 2):
                dve.wait_ge(S["kv_done"], n + 1)
                b = (4, 2, 6)[n]
                for h in range(GH):
                    note(dve.scalar_tensor_tensor(
                        out=state[:, n, h * DV:(h + 1) * DV],
                        in0=state[:, n - 1, h * DV:(h + 1) * DV],
                        scalar=dec[:, h * NC + n:h * NC + n + 1],
                        in1=ps[:, b + h // 2, (h % 2) * DV:(h % 2 + 1) * DV],
                        op0=ALU.mult, op1=ALU.add))
                settle()
            dve.engine_nop().then_inc(S["state_ready"], 1)
            units(GLA_R + 3, GLA_R + 4)

            ob = [4, 2]

            def head_psum(tb, h):
                return ps[:, ob[tb] + h // 2, (h % 2) * DV:(h % 2 + 1) * DV]

            for tb in range(TB):
                dve.wait_ge(S["o_done"], tb + 1)
                for h in range(GH):
                    note(dve.bn_stats(stats[:, GH * tb + h, :], head_psum(tb, h)))
                settle()
                for h in range(GH):
                    note(dve.bn_aggr(mv[:, GH * tb + h, :], stats[:, GH * tb + h, :]))
                settle()
                dve.engine_nop().then_inc(S["stats_ready"], 1)
            dve.wait_ge(S["gn_loaded"], 32)

            def normalised_heads(c):
                pairs = [(tb, h) for tb in range(TB) for h in (2 * c, 2 * c + 1)]
                for tb, h in pairs:
                    at, i = slice(h * DV, (h + 1) * DV), GH * tb + h
                    note(dve.scalar_tensor_tensor(out=x[:, tb, at], in0=head_psum(tb, h),
                                                  scalar=mv[:, i, 0:1], in1=gn[:, 0, at],
                                                  op0=ALU.subtract, op1=ALU.mult))
                settle()
                dve.engine_nop().then_inc(S["ohat_ready"], 1)
                dve.wait_ge(S["rstd_ready"], 4)
                for tb, h in pairs:
                    at, i = slice(h * DV, (h + 1) * DV), GH * tb + h
                    note(dve.scalar_tensor_tensor(out=x[:, tb, at], in0=x[:, tb, at],
                                                  scalar=rstd[:, i:i + 1], in1=gn[:, 1, at],
                                                  op0=ALU.mult, op1=ALU.add))

            def gated_output(c):
                v = x[:, :, c * 512:(c + 1) * 512]
                dve.wait_ge(S["sr_ready"], c + 1)
                settle()
                dve.tensor_tensor(v, v, g_sr[:, :, c * 512:(c + 1) * 512], ALU.mult) \
                    .then_inc(S["on_ready"], 1)

            normalised_heads(0)
            gated_output(0)
            units(GLA_O, GLA_O + 1)
            o_transposed(1, 0, 6)
            normalised_heads(1)
            units(GLA_O + 1, GLA_O + 2)
            gated_output(1)
            units(GLA_O + 2, GLA_O + 3)
            o_transposed(2, 1, 0)
            units(GLA_O + 3, GATE_0 + 1)
            layer_norm(1, 0, 3)
            x_transposed(2, 0)
            units(GATE_0 + 1, GATE_0 + 2)
            layer_norm(1, 1, GLA_O + 4)
            x_transposed(2, 1)
            units(GATE_0 + 2, GATE_0 + 5)
            gate(0, GATE_0)
            ffn(1)

            layer_norm(2, 0, 4)
            units(FFN1_1, FFN1_1 + 1)
            x_transposed(3, 0)
            units(FFN1_1 + 1, FFN1_1 + 2)
            layer_norm(2, 1, FFN2_0 + FU)
            x_transposed(3, 1)
            units(FFN1_1 + 2, FFN1_1 + 3)
            ffn(2)

            dve.wait_ge(S["f_done"], 1)
            dve.wait_ge(S["bf_loaded"], 16)
            note(dve.tensor_tensor(lf[:, 0, :, :], ps[:, 2:4, 0:FH],
                                   bf[:, :].unsqueeze(1).broadcast_to([P, TB, FH]), ALU.add))
            settle()
            dve.engine_nop().then_inc(S["f_ready"], 1)
            log_sigmoid_parts(lf[:, 0, :, :], lf[:, 1, :, :])
            units(FOX_K + 1, FOX_K + 2)
            layer_norm(3, 0, 6)
            units(FOX_K + 2, FOX_K + 4)
            layer_norm(3, 1, FFN1_1 + FU)
            dve.wait_ge(S["log_ready"], 2)
            dve.scalar_tensor_tensor(out=pad[:, :, 0:FH], in0=lf[:, 0, :, :], scalar=0.0,
                                     in1=lf[:, 1, :, :], op0=ALU.min, op1=ALU.subtract) \
                .then_inc(S["lf_ready"], 1)
            units(FOX_V, FOX_V + 1)
            dve.wait_ge(S["lfT_done"], 1)
            dve.tensor_tensor_scan(cT[0:FH, :], ones16[:, :], ps[0:FH, 4, 0:TOK], 0.0, ALU.mult,
                                   ALU.add).then_inc(S["cT_ready"], 1)
            units(FOX_V + 1, FOX_V + 2)
            dve.wait_ge(S["ctT_done"], 1)
            dve.tensor_copy(ct[:, :, :], ps[:, 5, 0:TB * P].rearrange("p (b c) -> p b c", b=TB)[:, :, 0:FH]) \
                .then_inc(S["ct_ready"], 1)
            units(FOX_V + 2, FOX_V + 4)
            o_transposed(3, 0, 6)
            units(FOX_Q, FOX_Q + 2)
            o_transposed(4, 1, 4)
            units(FOX_Q + 2, FOX_G + 2)
            dve.wait_ge(S["c_ready"], 2)

            def logits(h):
                r, l = h % 2, f_l[h % 3]
                dve.wait_ge(S["qk_done"], h + 1)
                if h >= 3:
                    dve.wait_ge(S["prob_flipped"], h - 2)
                for tb, (a, n, c) in enumerate(((0, P, c0), (P, 2 * P, c1))):
                    dve.tensor_tensor_reduce(out=l[:, a:a + n], in0=ps[:, r, a:a + n],
                                             in1=c[:, h, :], scale=-1.0, scalar=3.0e38,
                                             op0=ALU.add, op1=ALU.min,
                                             accum_out=nmax[:, h, tb:tb + 1]) \
                        .then_inc(S["l_ready"], 1)

            def probs_transposed(h):
                r = h % 2
                dve.wait_ge(S["prob_flipped"], h + 1)
                if h >= 2:
                    dve.wait_ge(S["pv_done"], h - 1)
                dve.tensor_copy(f_pT[:, r, :], ps[:, 2 + r, 0:3 * P]).then_inc(S["pT_read"], 1)

            def head_output(half):
                hs = slice(8 * half, 8 * half + 8)
                dve.wait_ge(S["pv_done"], 8 * half + 8)
                dve.wait_ge(S["p_ready"], 2 * (8 * half + 8))
                note(dve.reciprocal(rinv[:, :, hs], rsum[:, :, hs]))
                settle()
                note(dve.tensor_scalar(rinv[:, :, hs], rinv[:, :, hs], 0.5, None, ALU.mult))
                settle()
                for tb in range(TB):
                    o = x[:, tb, 512 * half:512 * half + 512]
                    note(dve.tensor_tensor(o.rearrange("p (h d) -> p h d", d=FD),
                                           ps[:, 4 + tb, :].rearrange("p (h d) -> p h d", d=FD),
                                           rinv[:, tb, hs].unsqueeze(2).broadcast_to([P, 8, FD]),
                                           ALU.mult))
                settle()
                dve.engine_nop().then_inc(S["pv_read"], 1)
                dve.wait_ge(S["th_ready"], half + 1)
                for tb in range(TB):
                    at = slice(512 * half, 512 * half + 512)
                    note(dve.scalar_tensor_tensor(out=x[:, tb, at], in0=f_th[:, tb, at], scalar=1.0,
                                                  in1=x[:, tb, at], op0=ALU.add, op1=ALU.mult))
                settle()
                dve.engine_nop().then_inc(S["half_read"], 1)

            for i in range(FH + 2):
                if i < FH:
                    logits(i)
                if i >= 2:
                    probs_transposed(i - 2)
                if i in SPLIT_AT_HEAD:
                    n = SPLIT_AT_HEAD[i]
                    units(n, n + 1)
                if i == 10:
                    head_output(0)
            o_transposed(5, 0, 0)
            head_output(1)
            units(FOX_O + 2, FOX_O + 3)
            o_transposed(6, 1, 4)
            units(FOX_O + 3, GATE_1 + 1)
            layer_norm(4, 0, 7)
            x_transposed(5, 0)
            units(GATE_1 + 1, GATE_1 + 2)
            layer_norm(4, 1, FOX_O + 4)
            x_transposed(5, 1)
            units(GATE_1 + 2, GATE_1 + 5)
            gate(1, GATE_1)
            ffn(3)
            layer_norm(5, 0, 8)
            layer_norm(5, 1, UNITS)

        @block.tensor
        def _(pe):
            def product(dst, a, b, start, stop):
                return pe.matmul(dst, a, b, start=start, stop=stop, skip_group_check=True)

            def three(dst, ahi, alo, bhi, blo, first, last):
                product(dst, ahi, bhi, first, False)
                product(dst, ahi, blo, False, False)
                return product(dst, alo, bhi, False, last)

            def use(n):
                pe.wait_ge(S["lo_ready"], n + 1)

            def wide(s, q, tb, bank, cols=512):
                t = slice(tb * P, (tb + 1) * P)
                for k in range(4):
                    at = slice(k * 512, k * 512 + 512)
                    last = three(ps[:, bank, :], xhi[:, 4 * q + k, t], xlo[:, 4 * q + k, t],
                                 whi[:, s, at], wlo[:, s, at], q == 0 and k == 0, q == 1 and k == 3)
                return last

            def feature_major(s, q, banks):
                for m in range(4):
                    dst = ps[:, banks[m // 2], (m % 2) * TOK:(m % 2 + 1) * TOK]
                    for k in range(4):
                        at = slice(k * 512 + m * P, k * 512 + (m + 1) * P)
                        last = three(dst, whi[:, s, at], wlo[:, s, at], xhi[:, 4 * q + k, :],
                                     xlo[:, 4 * q + k, :], q == 0 and k == 0 and m % 2 == 0,
                                     q == 1 and k == 3)
                return last

            def deep(s, hi, lo, tb, banks, first, last):
                for n in range(2):
                    for k in range(2):
                        at = slice(k * 1024 + n * 512, k * 1024 + n * 512 + 512)
                        ins = three(ps[:, banks + n, :], hi[:, tb, k, :], lo[:, tb, k, :],
                                    whi[:, s, at], wlo[:, s, at], first and k == 0,
                                    last and k == 1)
                return ins

            def flip_x(v, tb):
                for half in range(2):
                    if v:
                        pe.wait_ge(S["x_ready"], 4 * (v - 1) + 2 * tb + half + 1)
                    for k in range(4):
                        at = (4 * half + k) * P
                        last = pe.transpose(ps[:, X_BANK[v][tb] + half, k * P:(k + 1) * P],
                                            x[:, tb, at:at + P], ident[:, :])
                    last.then_inc(S["x_flipped"], 1)

            def flip_hidden_block(tb):
                for k in range(2):
                    last = pe.transpose(ps[:, 2 + tb, k * P:(k + 1) * P],
                                        hid[:, 1, tb, k * P:(k + 1) * P], ident[:, :])
                return last

            def flip_h(h_count):
                pe.wait_ge(S["h_ready"], h_count)
                flip_hidden_block(0)
                flip_hidden_block(1).then_inc(S["h_flipped"], 1)

            def block_of_units(n, bank, v, tb):
                for q in range(2):
                    pe.wait_ge(S["xT_ready"], X_COUNT[v] + 2 * tb + q + 1)
                    use(n + q)
                    last = wide((n + q) % NS, q, tb, bank)
                    if tb == TB - 1:
                        last.then_inc(S["unit_used"], 1)
                return last

            def two_units(n, banks):
                for q in range(2):
                    use(n + q)
                    for tb in range(TB):
                        last = wide((n + q) % NS, q, tb, banks[tb])
                    last.then_inc(S["unit_used"], 1)

            def two_feature_units(n, banks):
                for q in range(2):
                    use(n + q)
                    feature_major((n + q) % NS, q, banks).then_inc(S["unit_used"], 1)

            def ffn_in(n, s, q):
                use(n)
                for tb in range(TB):
                    last = wide(s, q, tb, tb)
                last.then_inc(S["unit_used"], 1)

            def ffn_out(n, s, t_count, first):
                pe.wait_ge(S["hT_ready"], t_count)
                use(n)
                deep(s, hhi, hlo, 0, 4, first, False)
                deep(s, hhi, hlo, 1, 6, first, False).then_inc(S["unit_used"], 1)

            def ffn(f, flipped, banks_read, count):
                b, it, ih = FFN_BASE[f], f * T_COUNT, f * H_COUNT
                v = FFN_X[f]
                for tb in range(TB):
                    if tb >= flipped:
                        flip_x(v, tb)
                    last = block_of_units(b, tb, v, tb)
                    if tb == 0:
                        last.then_inc(S["gu_half"], 1)
                if f == 0:
                    flip_p()

                use(b + 2)
                for tb in range(TB):
                    pe.wait_ge(S["h_ready"], ih + tb + 1)
                    last = wide((b + 2) % NS, 0, tb, tb)
                last.then_inc(S["unit_used"], 1)
                pe.wait_ge(banks_read, count)
                flip_h(ih + 2)
                ffn_in(b + 3, b % NS, 1)
                ffn_out(b + 4, (b + 1) % NS, it + 1, True)

                with pe.Fori(2, LAST_J) as j:
                    n = j * 3 + (b - 1)
                    pe.wait_ge(S["h_ready"], j + (ih + 1))
                    ffn_in(n, (b + 2) % NS, 0)
                    flip_h(j + (ih + 1))
                    ffn_in(n + 1, b % NS, 1)
                    ffn_out(n + 2, (b + 1) % NS, j + it, False)

                n = b + 3 * LAST_J - 1
                pe.wait_ge(S["h_ready"], ih + LAST_J + 1)
                use(n)
                wide(n % NS, 0, 0, 0)
                flip_h(ih + LAST_J + 1)
                use(n + 1)
                wide((n + 1) % NS, 1, 0, 0).then_inc(S["gu_half"], 1)
                wide(n % NS, 0, 1, 1).then_inc(S["unit_used"], 1)
                pe.wait_ge(S["hT_ready"], it + LAST_J)
                use(n + 2)
                deep((n + 2) % NS, hhi, hlo, 0, 4, False, False)
                pe.wait_ge(S["h_ready"], ih + H_COUNT - 1)
                flip_hidden_block(0).then_inc(S["h_flipped"], 1)
                wide((n + 1) % NS, 1, 1, 1).then_inc(S["unit_used"], 1)
                pe.wait_ge(S["hT_ready"], it + T_COUNT - 1)
                use(n + 3)
                deep(n % NS, h2hi, h2lo, 0, 4, False, True).then_inc(S["tb0_done"], 1)
                pe.wait_ge(S["h_ready"], ih + H_COUNT)
                flip_hidden_block(1).then_inc(S["h_flipped"], 1)
                deep((n + 2) % NS, hhi, hlo, 1, 6, False, False).then_inc(S["unit_used"], 1)
                pe.wait_ge(S["hT_ready"], it + T_COUNT)
                deep(n % NS, h2hi, h2lo, 1, 6, False, True).then_inc(S["unit_used"], 1)

            def projection(layer, n, v):
                use(n)
                s = n % NS
                deep(s, phi[:, layer], plo[:, layer], 0, 0, True, True).then_inc(S["tb0_done"], 1)
                flip_x(v, 0)
                deep(s, phi[:, layer], plo[:, layer], 1, 2, True, True).then_inc(S["unit_used"], 1)
                pe.wait_ge(S["pp_read"], 2 * layer + 1)

            def narrow(i, b, done):
                pe.wait_ge(S["narrow_lo"], 1)
                for tb in range(TB):
                    t = slice(tb * P, (tb + 1) * P)
                    for k in range(KT):
                        last = three(ps[:, b + tb, 0:RANK], xhi[:, k, t], xlo[:, k, t],
                                     shi[:, i, k, :], slo[:, i, k, :], k == 0, k == KT - 1)
                last.then_inc(S[done], 1)

            def flip_pad(b, done):
                for tb in range(TB):
                    last = pe.transpose(ps[:, b, tb * P:(tb + 1) * P], pad[:, tb, :], ident[:, :])
                last.then_inc(S[done], 1)

            def flip_o(half, b):
                for k in range(4):
                    for tb in range(TB):
                        last = pe.transpose(
                            ps[:, b + k // 2, (k % 2) * TOK + tb * P:(k % 2) * TOK + (tb + 1) * P],
                            x[:, tb, (4 * half + k) * P:(4 * half + k + 1) * P], ident[:, :])
                last.then_inc(S["o_flipped"], 1)

            def output_unit(n, half, bank, c):
                use(n)
                for tb in range(TB):
                    last = wide(n % NS, half, tb, bank[tb][c])
                last.then_inc(S["unit_used"], 1)

            def output_blocks(n, bank):
                for tb in range(TB):
                    for c in range(2):
                        use(n + c)
                        last = wide((n + c) % NS, 1, tb, bank[tb][c])
                        if tb == TB - 1:
                            last.then_inc(S["unit_used"], 1)
                    if tb == 0:
                        last.then_inc(S["tb0_done"], 1)

            def gate(layer, base):
                bank, v = LN_BANK[3 * layer + 1], 3 * layer + 2
                for tb in range(TB):
                    flip_x(v, tb)
                    block_of_units(base, bank[tb][0], v, tb)
                two_units(base + 2, [bank[0][1], bank[1][1]])

            def flip_p():
                pe.wait_ge(S["p_loaded"], 16)
                for layer in range(DEPTH):
                    for tb in range(TB):
                        for k in range(2):
                            i = 2 * tb + k
                            last = pe.transpose(ps[:, 2 + layer, i * P:(i + 1) * P],
                                                p_raw[:, layer, tb, k * P:(k + 1) * P], ident[:, :])
                last.then_inc(S["p_flipped"], 1)

            pe.wait_ge(S["ident_ready"], 1)
            pe.wait_ge(S["x0_loaded"], 16)
            flip_x(0, 0)
            pe.wait_ge(S["x1_loaded"], 16)
            flip_x(0, 1)
            ffn(0, 2, S["pT_ready"], 1)
            projection(0, PP_0, 1)

            block_of_units(GLA_V, 0, 1, 0)
            flip_x(1, 1)
            block_of_units(GLA_V, 1, 1, 1)
            pe.wait_ge(S["pp_read"], 2)
            narrow(0, 2, "alr_done")
            n = GLA_Q
            use(n)
            feature_major(n % NS, 0, (4, 5)).then_inc(S["unit_used"], 1)
            pe.wait_ge(S["alr_read"], 1)
            flip_pad(2, "aT_done")
            use(n + 1)
            feature_major((n + 1) % NS, 1, (4, 5)).then_inc(S["unit_used"], 1)
            pe.wait_ge(S["aT_ready"], 1)
            pe.wait_ge(S["wa2_loaded"], 16)
            for h in range(GH):
                last = pe.matmul(ps[:, 2 + h // 2, (h % 2) * TOK:(h % 2 + 1) * TOK],
                                 wa2[:, h * DK:(h + 1) * DK], aT, start=True, stop=True)
            last.then_inc(S["zT_done"], 1)
            two_feature_units(GLA_K, (6, 7))
            pe.wait_ge(S["nz_ready"], 1)
            two_units(GLA_V2, (2, 3))
            pe.wait_ge(S["v_read"], 1)
            n = GLA_R
            use(n)
            for tb in range(TB):
                last = wide(n % NS, 0, tb, tb)
            last.then_inc(S["unit_used"], 1)
            pe.wait_ge(S["qd_ready"], 1)
            pe.wait_ge(S["ki_ready"], 2)
            for tb in range(TB):
                for h in range(GH):
                    last = pe.transpose(ps[:, 4 + tb, h * P:(h + 1) * P],
                                        ks[:, h * TOK + tb * P:h * TOK + (tb + 1) * P], ident[:, :])
                last.then_inc(S["kst_flipped"], 1)
            for tb in range(TB):
                for h in range(GH):
                    t = slice(h * TOK + tb * P, h * TOK + (tb + 1) * P)
                    last = pe.matmul(ps[:, 6 + tb, h * P:(h + 1) * P], ki[:, t], qd[:, t],
                                     start=True, stop=True)
            last.then_inc(S["attn_done"], 1)
            use(n + 1)
            wide((n + 1) % NS, 1, 0, 0)
            pe.wait_ge(S["v_read"], 2)
            pe.wait_ge(S["kst_ready"], 2)
            pe.wait_ge(S["attn_ready"], 2)
            for c, b in enumerate((4, 2, 6)):
                t = slice((c % 2) * CH, (c % 2 + 1) * CH)
                for h in range(GH):
                    last = pe.matmul(ps[:, b + h // 2, (h % 2) * DV:(h % 2 + 1) * DV],
                                     kst[t, (c // 2) * 512 + h * DK:(c // 2) * 512 + (h + 1) * DK],
                                     g_v[t, c // 2, h * DV:(h + 1) * DV], start=True, stop=True)
                last.then_inc(S["kv_done"], 1)
            wide((n + 1) % NS, 1, 1, 1).then_inc(S["unit_used"], 1)
            pe.wait_ge(S["state_ready"], 1)
            for tb, b in enumerate((4, 2)):
                for h in range(GH):
                    o = ps[:, b + h // 2, (h % 2) * DV:(h % 2 + 1) * DV]
                    last = pe.matmul(o, attn[:, tb * 512 + h * P:tb * 512 + (h + 1) * P],
                                     g_v[:, tb, h * DV:(h + 1) * DV], start=True, stop=False,
                                     skip_group_check=True)
                    for e in range(2):
                        c = 2 * tb + e
                        if c == 0:
                            continue
                        last = pe.matmul(o[e * CH:(e + 1) * CH, :],
                                         qd[:, h * TOK + c * CH:h * TOK + (c + 1) * CH],
                                         state[:, c - 1, h * DV:(h + 1) * DV], start=False,
                                         stop=e == 1, skip_group_check=True)
                last.then_inc(S["o_done"], 1)
            pe.wait_ge(S["sr_ready"], 1)
            n = GLA_R + 2
            use(n)
            for tb in range(TB):
                last = wide(n % NS, 0, tb, tb)
            last.then_inc(S["unit_used"], 1)
            use(n + 1)
            wide((n + 1) % NS, 1, 0, 0)
            pe.wait_ge(S["on_ready"], 1)
            flip_o(0, 6)
            wide((n + 1) % NS, 1, 1, 1).then_inc(S["unit_used"], 1)
            pe.wait_ge(S["ohat_ready"], 2)
            pe.wait_ge(S["oT_ready"], 1)
            output_unit(GLA_O, 0, LN_BANK[1], 0)
            pe.wait_ge(S["on_ready"], 2)
            flip_o(1, 0)
            output_unit(GLA_O + 1, 0, LN_BANK[1], 1)
            pe.wait_ge(S["oT_ready"], 2)
            output_blocks(GLA_O + 2, LN_BANK[1])
            gate(0, GATE_0)
            ffn(1, 2, S["gate_read"], 4)
            projection(1, PP_1, 3)
            ffn(2, 1, S["pp_read"], 4)

            narrow(1, 2, "f_done")
            two_feature_units(FOX_K, (0, 1))
            pe.wait_ge(S["f_ready"], 1)
            two_feature_units(FOX_K + 2, (2, 3))
            pe.wait_ge(S["lf_ready"], 1)
            flip_pad(4, "lfT_done")

            def value_unit(q, c):
                n = FOX_V + 2 * q + c
                use(n)
                for tb in range(TB):
                    last = wide(n % NS, q, tb, 2 * c + tb)
                last.then_inc(S["unit_used"], 1)

            pe.wait_ge(S["kT_ready"], 1)
            value_unit(0, 0)
            pe.wait_ge(S["cT_ready"], 1)
            for tb in range(TB):
                last = pe.transpose(ps[:, 5, tb * P:(tb + 1) * P], cT[:, tb * P:(tb + 1) * P],
                                    ident[:, :])
            last.then_inc(S["ctT_done"], 1)
            pe.wait_ge(S["kT_ready"], 2)
            value_unit(0, 1)
            pe.wait_ge(S["x_ready"], 4 * 4)
            flip_o(0, 6)
            value_unit(1, 0)
            value_unit(1, 1)
            pe.wait_ge(S["ct_ready"], 1)
            flip_o(1, 4)
            for c, banks in enumerate(((6, 7), (2, 3))):
                if c:
                    pe.wait_ge(S["fv_read"], 2)
                for q in range(2):
                    pe.wait_ge(S["oT_ready"], 3 + q)
                    n = FOX_Q + 2 * c + q
                    use(n)
                    feature_major(n % NS, q, banks).then_inc(S["unit_used"], 1)

            def scores(h):
                r = h % 2
                if h >= 2:
                    pe.wait_ge(S["l_ready"], 2 * (h - 1))
                else:
                    pe.wait_ge(S["qT_ready"], 1)
                row = slice(r * FD, (r + 1) * FD)
                for tb, (a, n) in enumerate(((0, P), (P, 2 * P))):
                    last = pe.matmul(ps[:, r, a:a + n], f_q[row, h // 2, tb * P:(tb + 1) * P],
                                     f_k[row, h // 2, 0:n], start=True, stop=True)
                last.then_inc(S["qk_done"], 1)

            def flip_probs(h):
                r = h % 2
                pe.wait_ge(S["p_ready"], 2 * h + 2)
                if h >= 2:
                    pe.wait_ge(S["pT_read"], h - 1)
                else:
                    pe.wait_ge(S["qT_ready"], 2)
                for i in range(3):
                    last = pe.transpose(ps[:, 2 + r, i * P:(i + 1) * P],
                                        f_l[h % 3][:, i * P:(i + 1) * P], ident[:, :])
                last.then_inc(S["prob_flipped"], 1)

            def values(h):
                pe.wait_ge(S["pT_read"], h + 1)
                if h == 8:
                    pe.wait_ge(S["pv_read"], 1)
                r, d = h % 2, slice(h * FD, (h + 1) * FD)
                c = slice((h % 8) * FD, (h % 8 + 1) * FD)
                pe.matmul(ps[:, 4, c], f_pT[:, r, 0:P], f_v[:, 0, d], start=True, stop=True)
                pe.matmul(ps[:, 5, c], f_pT[:, r, P:2 * P], f_v[:, 0, d], start=True, stop=False)
                pe.matmul(ps[:, 5, c], f_pT[:, r, 2 * P:3 * P], f_v[:, 1, d], start=False,
                          stop=True).then_inc(S["pv_done"], 1)

            def gate_piece(i):
                n, q, tb, k0 = FOX_G + i // 4, i // 4 % 2, i // 2 % 2, i % 2 * 2
                if i in (0, 8):
                    pe.wait_ge(*((S["qT_ready"], 1), (S["th_ready"], 1))[i // 8])
                use(n)
                t = slice(tb * P, (tb + 1) * P)
                for k in (k0, k0 + 1):
                    at = slice(k * 512, k * 512 + 512)
                    last = three(ps[:, 6 + tb, :], xhi[:, 4 * q + k, t], xlo[:, 4 * q + k, t],
                                 whi[:, n % NS, at], wlo[:, n % NS, at], q == 0 and k == 0,
                                 q == 1 and k == 3)
                if i % 4 == 3:
                    last.then_inc(S["unit_used"], 1)

            pieces = [0, 1, 2, 3, 4, 5, 6, 7, None, 8, 9, 10, 11, 12, 13, None, 14, 15, None]
            for i in range(FH + 3):
                if i < FH:
                    scores(i)
                if pieces[i] is not None:
                    gate_piece(pieces[i])
                if 2 <= i < FH + 2:
                    flip_probs(i - 2)
                if i >= 3:
                    values(i - 3)
                if i == FH:
                    pe.wait_ge(S["half_read"], 1)
                    pe.wait_ge(S["l_ready"], 2 * FH)
                    flip_o(0, 0)
            pe.wait_ge(S["th_ready"], 2)
            pe.wait_ge(S["oT_ready"], 5)
            output_unit(FOX_O, 0, LN_BANK[4], 0)
            pe.wait_ge(S["half_read"], 2)
            flip_o(1, 4)
            output_unit(FOX_O + 1, 0, LN_BANK[4], 1)
            pe.wait_ge(S["oT_ready"], 6)
            output_blocks(FOX_O + 2, LN_BANK[4])
            gate(1, GATE_1)
            ffn(3, 2, S["gate_read"], 8)


_INS = ["x", "p", "ffn1_w_in", "ffn1_w_out", "ln1_g", "ln1_b", "gla_w_in", "gla_w_a2", "gla_b_a",
        "gla_gn_g", "gla_gn_b", "gla_w_o", "fox_w_kvf", "fox_b_f", "fox_w_in", "fox_w_o", "ln2_g",
        "ln2_b", "ffn2_w_in", "ffn2_w_out", "ple_w_gate", "ple_w_proj", "ln3_g", "ln3_b"]


def kernel(**inputs):
    import numpy as _np
    import concourse.bacc as _bacc
    from concourse import mybir as _mybir
    from concourse.bass_utils import run_bass_kernel_spmd as _run

    nc = _bacc.Bacc("TRN2", target_bir_lowering=False, num_devices=1)
    arrays, args = {}, []
    for name in _INS:
        a = _np.ascontiguousarray(inputs[name])
        arrays[f"in_{name}"] = a
        args.append(nc.dram_tensor(f"in_{name}", a.shape, _mybir.dt.from_np(a.dtype),
                                   kind="ExternalInput").ap())
    shape = inputs["x"].shape
    o = nc.dram_tensor("out_0", shape, _mybir.dt.float32, kind="ExternalOutput").ap()
    trunk(nc, *args, o)
    r = _run(nc, [arrays], core_ids=[0])
    return r.results[0]["out_0"]
```

```python
import concourse.bass as bass
from concourse import mybir
from contextlib import ExitStack


def trunk(nc, x_in, p_in, ffn1_w_in, ffn1_w_out, ln1_g, ln1_b, gla_w_in, gla_w_a2, gla_b_a,
          gla_gn_g, gla_gn_b, gla_w_o, fox_w_kvf, fox_b_f, fox_w_in, fox_w_o, ln2_g, ln2_b,
          ffn2_w_in, ffn2_w_out, ple_w_gate, ple_w_proj, ln3_g, ln3_b, out):
    f32 = mybir.dt.float32
    f32r = mybir.dt.float32r
    u32 = mybir.dt.uint32
    ALU = mybir.AluOpType
    ACT = mybir.ActivationFunctionType

    P = 128
    TOK = x_in.shape[1]
    DM = x_in.shape[2]
    TB = TOK // P
    KT = DM // P
    DEPTH = p_in.shape[0]
    FF = ffn1_w_out.shape[1]
    HC = 256
    NCH = FF // HC
    FU = 3 * NCH
    WU = 2048
    NS = 3
    LOADS = 32
    ALPHA = (2 * DEPTH) ** 0.25
    EPS = 1e-5
    GH, DK, DV, RANK, CH = 4, 128, 256, 16, 64
    NC = TOK // CH
    TAU = 16.0
    FH, FD = 16, 64
    NEG = -1.0e30
    LAST_J = NCH - 1

    FFN1_0 = 0
    PP_0 = FFN1_0 + FU
    GLA_V = PP_0 + 1
    GLA_Q = GLA_V + 2
    GLA_K = GLA_Q + 2
    GLA_V2 = GLA_K + 2
    GLA_R = GLA_V2 + 2
    GLA_O = GLA_R + 4
    GATE_0 = GLA_O + 4
    FFN2_0 = GATE_0 + 4
    PP_1 = FFN2_0 + FU
    FFN1_1 = PP_1 + 1
    FOX_K = FFN1_1 + FU
    FOX_V = FOX_K + 4
    FOX_Q = FOX_V + 4
    FOX_G = FOX_Q + 4
    FOX_O = FOX_G + 4
    GATE_1 = FOX_O + 4
    FFN2_1 = GATE_1 + 4
    UNITS = FFN2_1 + FU
    FFN_BASE = [FFN1_0, FFN2_0, FFN1_1, FFN2_1]
    SPLIT_AT_HEAD = {1: FOX_G + 2, 5: FOX_G + 3, 8: FOX_O, 12: FOX_O + 1}
    LN_DONE = [(1, PP_0), (3, GATE_0), (4, PP_1), (6, FOX_K), (7, GATE_1), (8, UNITS)]
    HALF_DONE = [(1, 2), (3, None), (4, 5), (6, 7), (8, None), (9, 10)]
    LN_OF = [0, 2, 3, 5]
    FFN_X = [0, 2, 3, 5]
    LN_BANK = [[(4, 5), (6, 7)], [(4, 5), (2, 3)], [(4, 5), (6, 7)], [(4, 5), (6, 7)],
               [(6, 2), (7, 3)], [(4, 5), (6, 7)]]
    LN_SCALE = [0.5, 1.0, 0.5, 0.5, 1.0, 0.5]
    X_BANK = {0: (0, 2), 1: (4, 6), 2: (0, 6), 3: (4, 6), 5: (4, 0)}
    X_COUNT = {0: 0, 1: 4, 2: 8, 3: 12, 5: 16}
    H_COUNT = NCH + 2
    T_COUNT = NCH + 1

    w_in = [ffn1_w_in[0], ffn2_w_in[0], ffn1_w_in[1], ffn2_w_in[1]]
    w_out = [ffn1_w_out[0], ffn2_w_out[0], ffn1_w_out[1], ffn2_w_out[1]]
    ln_g = [ln1_g[0], ln2_g[0], ln3_g[0], ln1_g[1], ln2_g[1], ln3_g[1]]
    ln_b = [ln1_b[0], ln2_b[0], ln3_b[0], ln1_b[1], ln2_b[1], ln3_b[1]]

    def spread(vector):
        return vector.unsqueeze(0).broadcast_to([P, vector.shape[0]])

    def square(w, cols, q, n):
        return w[q * 512:(q + 1) * 512, cols + n * 512:cols + (n + 1) * 512] \
            .rearrange("(k p) c -> p k c", p=P)

    ctx = ExitStack()
    with ctx:
        def sb(name, shape, dt=f32):
            return ctx.enter_context(nc.sbuf_tensor(name, shape, dt))

        def sem(name):
            return ctx.enter_context(nc.semaphore(name))

        raw = sb("raw", [P, NS, WU])
        whi = sb("whi", [P, NS, WU], f32r)
        wlo = sb("wlo", [P, NS, WU], f32r)
        x = sb("x", [P, TB, DM])
        res = sb("res", [P, TB, DM])
        xhi = sb("xhi", [P, KT, TOK], f32r)
        xlo = sb("xlo", [P, KT, TOK], f32r)
        hhi = sb("hhi", [P, TB, 2, P], f32r)
        hlo = sb("hlo", [P, TB, 2, P], f32r)
        h2hi = sb("h2hi", [P, TB, 2, P], f32r)
        h2lo = sb("h2lo", [P, TB, 2, P], f32r)
        phi = sb("phi", [P, DEPTH, TB, 2, P], f32r)
        plo = sb("plo", [P, DEPTH, TB, 2, P], f32r)
        hid = sb("hid", [P, 2, TB, HC])
        pp = sb("pp", [P, TB, DM])
        gb = sb("gb", [P, 2, DM])
        mix = sb("mix", [P, 7 * 2048 + 384])
        ba = sb("ba", [P, GH])
        bf = sb("bf", [FH, 1])
        sraw = sb("sraw", [P, 2, KT, RANK])
        shi = sb("shi", [P, 2, KT, RANK], f32r)
        slo = sb("slo", [P, 2, KT, RANK], f32r)
        ident = sb("ident", [P, P])
        chunk_mask = sb("chunk_mask", [P, P])
        stats = sb("stats", [P, 8, 6])
        mv = sb("mv", [P, 8, 2])
        rstd = sb("rstd", [P, 8])
        sums = sb("sums", [P, 2])
        nmean = sb("nmean", [P, TB])
        sqsum = sb("sqsum", [P, TB])
        mhalf = sb("mhalf", [P, 8])
        dec = sb("dec", [P, GH * NC])
        ct = sb("ct", [P, TB, FH])
        cT = sb("cT", [P, TOK])
        ones16 = sb("ones16", [FH, TOK])
        nmax = sb("nmax", [P, FH, TB])
        rsum = sb("rsum", [P, TB, FH])
        rinv = sb("rinv", [P, TB, FH])
        ps = ctx.enter_context(nc.psum_tensor("ps", [P, 8, 512], f32))
        c_dram = nc.dram_tensor("c_scratch", (FH, TOK), f32, kind="Internal").ap()

        def part(at, n):
            return mix[:, at:at + n]

        p_raw = part(0, 1024).rearrange("p (l b c) -> p l b c", l=DEPTH, b=TB)
        g_v = part(0, 2048).rearrange("p (b c) -> p b c", b=TB)
        g_sr = part(2048, 2048).rearrange("p (b c) -> p b c", b=TB)
        gn = part(4096, 2048).rearrange("p (a c) -> p a c", a=2)
        cs = part(6144, 1024)
        lg = part(7168, 1024)
        qd = part(8192, 1024)
        ki = part(9216, 1024)
        ks = part(10240, 1024)
        state = part(11264, 3072).rearrange("p (n c) -> p n c", n=3)
        fresh = part(11264 + 2048, 1024)
        attn = cs
        wa2 = mix[0:RANK, 11264:11264 + GH * DK]
        aT = mix[0:RANK, 11776:11776 + TOK]
        kst = lg
        f_k = part(0, 2048).rearrange("p (m t) -> p m t", t=TOK)
        f_v = part(2048, 2048).rearrange("p (b c) -> p b c", b=TB)
        f_q = part(4096, 2048).rearrange("p (m t) -> p m t", t=TOK)
        lf = mix[0:FH, 6144:6144 + 2 * TOK].rearrange("p (a t) -> p a t", a=2)
        f_th = part(6144, 2048).rearrange("p (b c) -> p b c", b=TB)
        c0 = part(8192, 2048).rearrange("p (h s) -> p h s", h=FH)
        c1 = part(10240, 4096).rearrange("p (h s) -> p h s", h=FH)
        f_pT = x[:, :, 512:512 + 3 * P]
        hid_flat = hid[:, :, :, :].rearrange("p a b c -> p (a b c)")
        f_l = [hid_flat[:, 0:3 * P], hid_flat[:, 3 * P:6 * P], part(7 * 2048, 3 * P)]

        raw_arrived = [sem(f"raw_arrived{s}") for s in range(NS)]
        names = """x0_loaded x1_loaded half_arrived half_hi half_lo p_loaded wa2_loaded ba_loaded bf_loaded narrow_loaded gn_loaded
            gb_loaded hi_ready lo_ready unit_used narrow_hi narrow_lo ident_ready mask_ready
            const_ready x_flipped xT_hi xT_ready p_flipped pT_hi pT_ready silu_ready h_ready
            h_flipped hT_hi hT_ready half_sums tb0_done stats_ready mean_ready var_ready
            rstd_ready x_ready res_ready
            pp_read gate_tanh gate_read alr_done  aT_ready zT_done gu_half
            nz_ready log_ready cs_ready qd_ready ki_ready v_read kst_flipped kst_ready attn_done
            attn_ready kv_done state_ready sr_ready o_done ohat_ready on_ready
            o_flipped oT_hi oT_ready f_done f_ready  cT_ready ctT_done ct_ready
            c_stored c_spread c_ready kT_ready fv_read qT_ready th_ready qk_done l_ready p_ready
            prob_flipped pT_read pv_done pv_read half_read act_step dve_step pool_step stored""".split()
        S = {n: sem(n) for n in names}

        def arrived(n):
            return LOADS * (n // NS + 1)

        block = ctx.enter_context(nc.Block())

        @block.sync
        def _(sp):
            def unit_halves(n, s, first, second, wait):
                if wait is not None:
                    sp.wait_ge(S["lo_ready"], wait)
                for h, src in enumerate((first, second)):
                    k = src.shape[1]
                    dst = raw[:, s, h * 1024:(h + 1) * 1024].rearrange("p (k c) -> p k c", k=k)
                    sp.dma_start(dst, src).then_inc(raw_arrived[s], 16)

            def unit(n, src):
                k = src.shape[1] // 2
                unit_halves(n, n % NS, src[:, 0:k, :], src[:, k:2 * k, :],
                            n - 2 if n >= NS else None)

            def ffn_in(f, j, q, n, s, wait):
                v = w_in[f][q * 512:(q + 1) * 512, :].rearrange("(k p) c -> p k c", p=P)
                if wait is not None:
                    sp.wait_ge(S["lo_ready"], wait)
                dst = raw[:, s, :].rearrange("p (k g c) -> p k g c", k=4, g=2)
                for g in range(2):
                    sp.dma_start(dst[:, :, g, :], v[:, :, bass.ds(j * HC + g * FF, HC)]) \
                        .then_inc(raw_arrived[s], 16)

            def ffn_out(f, j, n, s, wait):
                v = w_out[f].rearrange("(k p) c -> p k c", p=P)
                sp.wait_ge(S["lo_ready"], wait)
                dst = raw[:, s, :].rearrange("p (k c) -> p k c", k=2)
                for h in range(2):
                    sp.dma_start(dst[:, h:h + 1, :], v[:, bass.ds(j * 2 + h, 1), :]) \
                        .then_inc(raw_arrived[s], 16)

            def wait_of(n):
                return n - 2 if isinstance(n, int) is False or n >= NS else None

            def ffn_round(f, b, j):
                n = j * 3 + (b - 1)
                ffn_in(f, j, 0, n, (b + 2) % NS, wait_of(n))
                ffn_in(f, j, 1, n + 1, b % NS, wait_of(n + 1))
                ffn_out(f, j - 1, n + 2, (b + 1) % NS, n)

            def layer_norm_vectors(k):
                if k:
                    sp.wait_ge(S["x_ready"], 4 * k)
                sp.dma_start(gb[:, 0, :], spread(ln_g[k])).then_inc(S["gb_loaded"], 16)
                sp.dma_start(gb[:, 1, :], spread(ln_b[k])).then_inc(S["gb_loaded"], 16)

            def first_unit():
                v = w_in[0][0:512, :].rearrange("(k p) c -> p k c", p=P)
                dst = raw[:, 0, :].rearrange("p (k g c) -> p k g c", k=4, g=2)
                for half, signal in enumerate((S["half_arrived"], raw_arrived[0])):
                    ks_ = slice(2 * half, 2 * half + 2)
                    for g in range(2):
                        sp.dma_start(dst[:, ks_, g, :], v[:, ks_, g * FF:g * FF + HC]) \
                            .then_inc(signal, 16)

            def ffn(f, extra):
                b = FFN_BASE[f]
                for q in range(2):
                    if f == 0 and q == 0:
                        first_unit()
                        load_x(1)
                    else:
                        ffn_in(f, 0, q, b + q, (b + q) % NS, wait_of(b + q))
                if f == 0:
                    sp.dma_start(p_raw.rearrange("p l b c -> p (l b) c"),
                                 p_in.rearrange("l a (b p) c -> p (l a b) c", p=P)) \
                        .then_inc(S["p_loaded"], 16)
                ffn_round(f, b, 1)
                extra()
                with sp.Fori(2, NCH) as j:
                    ffn_round(f, b, j)
                ffn_out(f, LAST_J, b + FU - 1, (b + 2) % NS, b + FU - 3)

            def narrow(i, w, cols):
                sp.dma_start(sraw[:, i, :, :], w[:, cols:cols + RANK]
                             .rearrange("(k p) c -> p k c", p=P)).then_inc(S["narrow_loaded"], 16)

            def constants():
                layer_norm_vectors(0)
                sp.dma_start(gn[:, 0, :], spread(gla_gn_g[0])).then_inc(S["gn_loaded"], 16)
                sp.dma_start(gn[:, 1, :], spread(gla_gn_b[0])).then_inc(S["gn_loaded"], 16)
                sp.dma_start(wa2, gla_w_a2[0]).then_inc(S["wa2_loaded"], 16)
                with nc.allow_non_contiguous_dma(reason="512 values"):
                    sp.dma_start(ba[:, :], gla_b_a[0].rearrange("(h p) -> p h", p=P)) \
                        .then_inc(S["ba_loaded"], 16)
                with nc.allow_non_contiguous_dma(reason="16 values"):
                    sp.dma_start(bf[:, :], fox_b_f.rearrange("(h o) -> h o", o=1)) \
                        .then_inc(S["bf_loaded"], 16)
                narrow(0, gla_w_in[0], 2 * GH * DK + 2 * GH * DV)
                narrow(1, fox_w_kvf, 2 * FH * FD)

            xv = x_in[0].rearrange("(b p) c -> p b c", p=P)

            def load_x(tb):
                sp.dma_start(x[:, tb, :], xv[:, tb, :]).then_inc(S[f"x{tb}_loaded"], 16)
            load_x(0)
            ffn(0, constants)
            unit(PP_0, ple_w_proj[0].rearrange("(k p) c -> p k c", p=P))
            for i in range(12):
                unit(GLA_V + i, square(gla_w_in[0], 0, i % 2, (2, 0, 1, 3, 4, 5)[i // 2]))
                if i == 5:
                    layer_norm_vectors(1)
            for i in range(4):
                unit(GLA_O + i, square(gla_w_o[0], 0, i // 2, i % 2))
            for i in range(4):
                unit(GATE_0 + i, square(ple_w_gate[0], 0, i % 2, i // 2))
            ffn(1, lambda: layer_norm_vectors(2))
            unit(PP_1, ple_w_proj[1].rearrange("(k p) c -> p k c", p=P))
            ffn(2, lambda: layer_norm_vectors(3))
            for i in range(4):
                unit(FOX_K + i, square(fox_w_kvf, 0, i % 2, i // 2))
            for i in range(4):
                unit(FOX_V + i, square(fox_w_kvf, 0, i // 2, 2 + i % 2))
            for i in range(8):
                unit(FOX_Q + i, square(fox_w_in[0], 0, i % 2, i // 2))
                if i == 5:
                    layer_norm_vectors(4)
            for i in range(4):
                unit(FOX_O + i, square(fox_w_o[0], 0, i // 2, i % 2))
            for i in range(4):
                unit(GATE_1 + i, square(ple_w_gate[1], 0, i % 2, i // 2))
            ffn(3, lambda: layer_norm_vectors(5))
            ov = out[0].rearrange("(b p) c -> p b c", p=P)
            for i in range(4):
                sp.wait_ge(S["x_ready"], 4 * 5 + i + 1)
                at = slice(i % 2 * 512, i % 2 * 512 + 512)
                sp.dma_start(ov[:, i // 2, at], x[:, i // 2, at]).then_inc(S["stored"], 16)
            sp.wait_ge(S["stored"], 64)

        @block.gpsimd
        def _(pool):
            step = 0

            def chain(ins):
                nonlocal step
                ins.then_inc(S["pool_step"], 1)
                step += 1
                pool.wait_ge(S["pool_step"], step)

            chain(pool.memset(ident[:, :], 0.0))
            pool.affine_select(out=ident[:, :], in_=ident[:, :], compare_op=ALU.not_equal, fill=1.0,
                               base=0, pattern=[[-1, P]], channel_multiplier=1) \
                .then_inc(S["ident_ready"], 1)
            pool.memset(mhalf[:, :], -0.5).then_inc(S["const_ready"], 1)
            pool.memset(cT[:, :], 0.0).then_inc(S["const_ready"], 1)
            pool.memset(ones16[:, :], 1.0).then_inc(S["const_ready"], 1)
            chain(pool.memset(fresh, 1.0))
            pool.memset(fresh.rearrange("p (n t) -> p n t", t=CH)[:, :, 0:1], 0.0) \
                .then_inc(S["const_ready"], 1)
            chain(pool.memset(chunk_mask[:, :], 1.0))
            chain(pool.affine_select(out=chunk_mask[:, :], in_=chunk_mask[:, :],
                                     compare_op=ALU.is_ge, fill=0.0, base=0, pattern=[[1, P]],
                                     channel_multiplier=-1))
            pool.memset(chunk_mask[0:CH, CH:P], 0.0).then_inc(S["mask_ready"], 1)

            def reciprocal_deviation(count, tb):
                pool.wait_ge(S["var_ready"], count)
                chain(pool.tensor_scalar(rstd[:, tb:tb + 1], sqsum[:, tb:tb + 1], 1.0 / DM, EPS,
                                         ALU.mult, ALU.add))
                pool.tensor_tensor(rstd[:, tb:tb + 1], rstd[:, tb:tb + 1], mhalf[:, 0:1],
                                   ALU.pow).then_inc(S["rstd_ready"], 1)

            def reciprocal_head_deviations(tb):
                h = slice(GH * tb, GH * tb + GH)
                pool.wait_ge(S["stats_ready"], tb + 1)
                chain(pool.tensor_scalar(rstd[:, h].unsqueeze(2), mv[:, h, 1:2], EPS, None,
                                         ALU.add))
                pool.tensor_tensor(rstd[:, h], rstd[:, h], mhalf[:, 0:GH], ALU.pow) \
                    .then_inc(S["rstd_ready"], 1)

            pool.wait_ge(S["const_ready"], 1)
            for i in range(2):
                reciprocal_deviation(i + 1, i % 2)
            for tb in range(TB):
                reciprocal_head_deviations(tb)
            for i in range(2, 2 * 4):
                reciprocal_deviation(i + 1, i % 2)
            pool.wait_ge(S["cT_ready"], 1)
            pool.dma_start(c_dram, cT[0:FH, :]).then_inc(S["c_stored"], 16)
            pool.wait_ge(S["c_stored"], 16)
            pool.dma_start(c1.rearrange("p h s -> p (h s)"), spread(c_dram.rearrange("h s -> (h s)"))) \
                .then_inc(S["c_spread"], 16)
            pool.wait_ge(S["c_spread"], 16)
            pool.wait_ge(S["ct_ready"], 1)
            for h in range(FH):
                last = pool.tensor_scalar(c0[:, h, :], c1[:, h, 0:P], -1.0, ct[:, 0, h:h + 1],
                                          ALU.mult, ALU.add)
            chain(last)
            for h in range(FH):
                last = pool.tensor_scalar(c1[:, h, :], c1[:, h, :], -1.0, ct[:, 1, h:h + 1],
                                          ALU.mult, ALU.add)
            chain(last)
            for c in (c0, c1[:, :, P:2 * P]):
                pool.affine_select(out=c, in_=c, compare_op=ALU.is_ge, fill=NEG, base=0,
                                   pattern=[[0, FH], [-1, P]], channel_multiplier=1) \
                    .then_inc(S["c_ready"], 1)
            for i in range(2 * 4, 2 * 6):
                reciprocal_deviation(i + 1, i % 2)

        @block.scalar
        def _(act):
            step = 0

            def chain(ins):
                nonlocal step
                ins.then_inc(S["act_step"], 1)
                step += 1
                act.wait_ge(S["act_step"], step)

            def split(n, s, arrivals, used):
                act.wait_ge(raw_arrived[s], arrivals)
                if used is not None:
                    act.wait_ge(S["unit_used"], used)
                act.copy(whi[:, s, :], raw[:, s, :]).then_inc(S["hi_ready"], 1)

            def units(a, b):
                for n in range(a, b):
                    split(n, n % NS, arrived(n), n - 2 if n >= NS else None)

            def x_transposed(v, tb):
                for half in range(2):
                    act.wait_ge(S["x_flipped"], X_COUNT[v] + 2 * tb + half + 1)
                    act.copy(xhi[:, 4 * half:4 * half + 4, tb * P:(tb + 1) * P],
                             ps[:, X_BANK[v][tb] + half, :].rearrange("p (k t) -> p k t", t=P)) \
                        .then_inc(S["xT_hi"], 1)

            def residual(v, tb):
                if v:
                    act.wait_ge(S["x_ready"], 4 * (v - 1) + 2 * tb + 2)
                act.mul(res[:, tb, :], x[:, tb, :], ALPHA).then_inc(S["res_ready"], 1)

            def deviation(k, tb):
                act.wait_ge(S["mean_ready"], 2 * k + tb + 1)
                act.activation(hid_flat, res[:, tb, :], ACT.Square, bias=nmean[:, tb:tb + 1],
                               accum_out=sqsum[:, tb:tb + 1]).then_inc(S["var_ready"], 1)

            def hidden_hi(count):
                act.wait_ge(S["h_flipped"], count)
                act.copy(hhi[:, :, :, :].rearrange("p b k t -> p b (k t)"), ps[:, 2:4, 0:HC]) \
                    .then_inc(S["hT_hi"], 1)

            def last_hidden_hi(f, tb):
                act.wait_ge(S["h_flipped"], T_COUNT * f + NCH + tb)
                act.copy(h2hi[:, tb, :, :].rearrange("p k t -> p (k t)"), ps[:, 2 + tb, 0:HC]) \
                    .then_inc(S["hT_hi"], 1)

            def silu(used):
                act.wait_ge(S["unit_used"], used)
                act.activation(hid[:, 0, :, :], ps[:, 0:2, 0:HC], ACT.Silu).then_inc(S["silu_ready"], 1)

            def silu_block(tb, done, count):
                act.wait_ge(done, count)
                act.activation(hid[:, 0, tb, :], ps[:, tb, 0:HC], ACT.Silu) \
                    .then_inc(S["silu_ready"], 1)

            def ffn(f, extra=None):
                b, it = FFN_BASE[f], f * T_COUNT
                silu_block(0, S["gu_half"], 2 * f + 1)
                units(b + 3, b + 4)
                silu_block(1, S["unit_used"], b + 2)
                if extra:
                    extra()
                units(b + 4, b + 5)
                if f == 0:
                    act.wait_ge(S["x0_loaded"], 16)
                    act.wait_ge(S["x1_loaded"], 16)
                    for tb in range(TB):
                        residual(0, tb)
                    narrow(0)
                    narrow(1)
                with act.Fori(1, LAST_J) as j:
                    hidden_hi(j + it)
                    n = j * 3 + (b + 2)
                    split(n, (b + 2) % NS, (j + (b + 2) // NS + 1) * LOADS, n - 2)
                    silu(j * 3 + (b + 1))
                    split(n + 1, b % NS, (j + (b + 3) // NS + 1) * LOADS, n - 1)
                    split(n + 2, (b + 1) % NS, (j + (b + 4) // NS + 1) * LOADS, n)
                hidden_hi(it + LAST_J)
                silu_block(0, S["gu_half"], 2 * f + 2)
                units(b + FU - 1, b + FU)
                last_hidden_hi(f, 0)
                silu_block(1, S["unit_used"], b + 3 * LAST_J + 1)
                units(b + FU, min(b + FU + 1, UNITS))
                last_hidden_hi(f, 1)
                units(b + FU + 1, b + FU + 2) if b + FU < UNITS else None
                if f != 2:
                    deviation(LN_OF[f], 0)

            def narrow(i):
                act.wait_ge(S["narrow_loaded"], 32)
                act.copy(shi[:, i, :, :], sraw[:, i, :, :]).then_inc(S["narrow_hi"], 1)

            def p_transposed():
                act.wait_ge(S["p_flipped"], 1)
                act.copy(phi[:, :, :, :, :].rearrange("p l b k t -> p l (b k t)"), ps[:, 2:4, :]) \
                    .then_inc(S["pT_hi"], 1)

            def half_projection(tb, done, count):
                act.wait_ge(done, count)
                act.mul(pp[:, tb, :], ps[:, 2 * tb:2 * tb + 2, :].rearrange("p a c -> p (a c)"), 0.5) \
                    .then_inc(S["pp_read"], 1)

            def gate(layer, base):
                act.wait_ge(S["res_ready"], 2 * (3 * layer + 2) + 2)
                for n in range(2):
                    act.wait_ge(S["unit_used"], base + 2 * n + 2)
                    for tb in range(TB):
                        b = LN_BANK[3 * layer + 1][tb][n]
                        act.activation(x[:, tb, n * 512:(n + 1) * 512], ps[:, b, :], ACT.Tanh,
                                       scale=0.5).then_inc(S["gate_tanh"], 1)
                    if base + 4 + 1 + n < UNITS:
                        units(base + 4 + 1 + n, base + 4 + 2 + n)

            def o_transposed(count, half, b):
                act.wait_ge(S["o_flipped"], count)
                act.copy(xhi[:, 4 * half:4 * half + 4, :],
                         ps[:, b:b + 2, :].rearrange("p a (k t) -> p (a k) t", t=TOK)) \
                    .then_inc(S["oT_hi"], 1)

            x_transposed(0, 0)
            act.wait_ge(S["half_arrived"], 32)
            act.copy(whi[:, 0, 0:1024], raw[:, 0, 0:1024]).then_inc(S["half_hi"], 1)
            act.wait_ge(raw_arrived[0], LOADS)
            act.copy(whi[:, 0, 1024:WU], raw[:, 0, 1024:WU]).then_inc(S["hi_ready"], 1)
            x_transposed(0, 1)
            units(1, 3)
            ffn(0, p_transposed)

            units(GLA_V + 1, GLA_V + 2)
            half_projection(0, S["tb0_done"], 2)
            x_transposed(1, 0)
            deviation(0, 1)
            half_projection(1, S["unit_used"], PP_0 + 1)
            units(GLA_Q, GLA_Q + 1)
            x_transposed(1, 1)
            units(GLA_Q + 1, GLA_Q + 2)

            def v_read(c, used):
                act.wait_ge(S["unit_used"], used)
                act.copy(g_v[:, :, c * 512:(c + 1) * 512], ps[:, 2 * c:2 * c + 2, :]) \
                    .then_inc(S["v_read"], 1)

            v_read(0, GLA_V + 2)
            units(GLA_K, GLA_K + 1)
            residual(1, 0)
            residual(1, 1)
            units(GLA_K + 1, GLA_V2 + 1)
            act.wait_ge(S["nz_ready"], 1)
            chain(act.activation(lg, lg, ACT.Exp))
            act.activation(lg, lg, ACT.Ln, bias=1.0).then_inc(S["log_ready"], 1)
            units(GLA_V2 + 1, GLA_V2 + 2)
            act.wait_ge(S["cs_ready"], 1)
            act.activation(qd, cs, ACT.Exp, scale=1.0 / TAU).then_inc(S["act_step"], 1)
            act.activation(ki, cs, ACT.Exp, scale=-1.0 / TAU).then_inc(S["act_step"], 1)
            act.activation(ks, ks, ACT.Exp, scale=1.0 / TAU).then_inc(S["act_step"], 1)
            act.activation(dec[:, :], cs.rearrange("p (n t) -> p n t", t=CH)[:, :, CH - 1],
                           ACT.Exp, scale=1.0 / TAU).then_inc(S["act_step"], 1)
            step += 4
            units(GLA_R, GLA_R + 2)
            v_read(1, GLA_V2 + 2)
            units(GLA_R + 2, GLA_R + 4)
            for c in range(2):
                act.wait_ge(S["unit_used"], GLA_R + 2 * c + 2)
                act.activation(g_sr[:, :, c * 512:(c + 1) * 512], ps[:, 0:2, :], ACT.Silu) \
                    .then_inc(S["sr_ready"], 1)
                if c == 0:
                    units(GLA_O, GLA_O + 2)
                    o_transposed(1, 0, 6)
            units(GLA_O + 2, GLA_O + 3)
            o_transposed(2, 1, 0)
            units(GLA_O + 3, GATE_0 + 1)
            deviation(1, 0)
            units(GATE_0 + 1, GATE_0 + 2)
            x_transposed(2, 0)
            deviation(1, 1)
            x_transposed(2, 1)
            units(GATE_0 + 2, GATE_0 + 3)
            residual(2, 0)
            residual(2, 1)
            units(GATE_0 + 3, GATE_0 + 5)
            gate(0, GATE_0)
            ffn(1)

            units(FFN1_1 + 1, FFN1_1 + 2)
            half_projection(0, S["tb0_done"], 5)
            x_transposed(3, 0)
            deviation(2, 1)
            half_projection(1, S["unit_used"], PP_1 + 1)
            units(FFN1_1 + 2, FFN1_1 + 3)
            x_transposed(3, 1)
            residual(3, 0)
            residual(3, 1)
            ffn(2)

            act.wait_ge(S["nz_ready"], 2)
            chain(act.activation(lf[:, 1, :], lf[:, 1, :], ACT.Exp))
            act.activation(lf[:, 1, :], lf[:, 1, :], ACT.Ln, bias=1.0) \
                .then_inc(S["log_ready"], 1)
            deviation(3, 0)
            units(FOX_K + 2, FOX_V)
            deviation(3, 1)
            for c in range(2):
                act.wait_ge(S["unit_used"], FOX_K + 2 * c + 2)
                act.copy(f_k[:, 4 * c:4 * c + 4, :].rearrange("p (a m) t -> p a (m t)", a=2),
                         ps[:, 2 * c:2 * c + 2, :]).then_inc(S["kT_ready"], 1)
                units(FOX_V + 2 * c, FOX_V + 2 * c + 2)
            o_transposed(3, 0, 6)
            units(FOX_Q, FOX_Q + 1)

            def fv_read(c):
                act.wait_ge(S["unit_used"], FOX_V + c + 3)
                act.copy(f_v[:, :, c * 512:(c + 1) * 512], ps[:, 2 * c:2 * c + 2, :]) \
                    .then_inc(S["fv_read"], 1)

            fv_read(0)
            units(FOX_Q + 1, FOX_Q + 2)
            o_transposed(4, 1, 4)
            fv_read(1)
            units(FOX_Q + 2, FOX_Q + 3)
            residual(4, 0)
            residual(4, 1)
            units(FOX_Q + 3, FOX_Q + 4)
            for c in range(2):
                act.wait_ge(S["unit_used"], FOX_Q + 2 * c + 2)
                b = (6, 2)[c]
                act.mul(f_q[:, 4 * c:4 * c + 4, :].rearrange("p (a m) t -> p a (m t)", a=2),
                        ps[:, b:b + 2, :], FD ** -0.5).then_inc(S["qT_ready"], 1)
                if c == 0:
                    units(FOX_G, FOX_G + 2)

            def softmax_exp(h):
                l = f_l[h % 3]
                act.wait_ge(S["l_ready"], 2 * h + 2)
                for tb, (a, n) in enumerate(((0, P), (P, 2 * P))):
                    act.activation(l[:, a:a + n], l[:, a:a + n], ACT.Exp, scale=-1.0,
                                   bias=nmax[:, h, tb:tb + 1], accum_out=rsum[:, tb, h:h + 1]) \
                        .then_inc(S["p_ready"], 1)

            def gate_half(c):
                act.wait_ge(S["unit_used"], FOX_G + 2 * c + 2)
                act.activation(f_th[:, :, c * 512:(c + 1) * 512], ps[:, 6:8, :], ACT.Tanh,
                               scale=0.5).then_inc(S["th_ready"], 1)

            for h in range(FH):
                softmax_exp(h)
                if h in SPLIT_AT_HEAD:
                    n = SPLIT_AT_HEAD[h]
                    units(n, n + 1)
                if h == 7:
                    gate_half(0)
            o_transposed(5, 0, 0)
            gate_half(1)
            units(FOX_O + 2, FOX_O + 3)
            o_transposed(6, 1, 4)
            units(FOX_O + 3, GATE_1 + 1)
            deviation(4, 0)
            units(GATE_1 + 1, GATE_1 + 2)
            x_transposed(5, 0)
            deviation(4, 1)
            x_transposed(5, 1)
            units(GATE_1 + 2, GATE_1 + 3)
            residual(5, 0)
            residual(5, 1)
            units(GATE_1 + 3, GATE_1 + 5)
            gate(1, GATE_1)
            ffn(3)
            deviation(5, 1)

        @block.vector
        def _(dve):
            step = 0

            def note(ins):
                nonlocal step
                ins.then_inc(S["dve_step"], 1)
                step += 1

            def settle():
                dve.wait_ge(S["dve_step"], step)

            def split(n, s):
                dve.wait_ge(S["hi_ready"], n + 1)
                dve.tensor_tensor(wlo[:, s, :], raw[:, s, :], whi[:, s, :].bitcast(f32),
                                  ALU.subtract).then_inc(S["lo_ready"], 1)

            def half_split(n, half):
                dve.wait_ge(S["hi_ready"], n + 1)
                at = slice(1024 * half, 1024 * half + 1024)
                ins = dve.tensor_tensor(wlo[:, n % NS, at], raw[:, n % NS, at],
                                        whi[:, n % NS, at].bitcast(f32), ALU.subtract)
                if half == 1:
                    ins.then_inc(S["lo_ready"], 1)

            def units(a, b):
                for n in range(a, b):
                    split(n, n % NS)

            def x_transposed(v, tb, halves=(0, 1)):
                for half in halves:
                    dve.wait_ge(S["xT_hi"], X_COUNT[v] + 2 * tb + half + 1)
                    at = slice(4 * half, 4 * half + 4)
                    dve.tensor_tensor(xlo[:, at, tb * P:(tb + 1) * P],
                                      ps[:, X_BANK[v][tb] + half, :]
                                      .rearrange("p (k t) -> p k t", t=P),
                                      xhi[:, at, tb * P:(tb + 1) * P].bitcast(f32),
                                      ALU.subtract).then_inc(S["xT_ready"], 1)

            def hidden_lo(count):
                dve.wait_ge(S["hT_hi"], count)
                dve.tensor_tensor(hlo[:, :, :, :].rearrange("p b k t -> p b (k t)"),
                                  ps[:, 2:4, 0:HC],
                                  hhi[:, :, :, :].rearrange("p b k t -> p b (k t)").bitcast(f32),
                                  ALU.subtract).then_inc(S["hT_ready"], 1)

            def last_hidden_lo(f, tb):
                dve.wait_ge(S["hT_hi"], T_COUNT * f + NCH + tb)
                dve.tensor_tensor(h2lo[:, tb, :, :].rearrange("p k t -> p (k t)"),
                                  ps[:, 2 + tb, 0:HC],
                                  h2hi[:, tb, :, :].rearrange("p k t -> p (k t)").bitcast(f32),
                                  ALU.subtract).then_inc(S["hT_ready"], 1)

            def hidden(count):
                dve.wait_ge(S["silu_ready"], count)
                dve.tensor_tensor(hid[:, 1, :, :], ps[:, 0:2, HC:2 * HC], hid[:, 0, :, :],
                                  ALU.mult).then_inc(S["h_ready"], 1)

            def hidden_block(tb, count):
                dve.wait_ge(S["silu_ready"], count)
                dve.tensor_tensor(hid[:, 1, tb, :], ps[:, tb, HC:2 * HC], hid[:, 0, tb, :],
                                  ALU.mult).then_inc(S["h_ready"], 1)

            def ffn(f, extra=None):
                b, it, ih = FFN_BASE[f], f * T_COUNT, f * H_COUNT
                hidden_block(0, ih + 1)
                units(b + 3, b + 4)
                hidden_block(1, ih + 2)
                if extra:
                    extra()
                units(b + 4, b + 5)
                if f == 0:
                    narrow()
                with dve.Fori(1, LAST_J) as j:
                    hidden_lo(j + it)
                    n = j * 3 + (b + 2)
                    split(n, (b + 2) % NS)
                    hidden(j + (ih + 2))
                    split(n + 1, b % NS)
                    split(n + 2, (b + 1) % NS)
                hidden_lo(it + LAST_J)
                hidden_block(0, ih + H_COUNT - 1)
                units(b + FU - 1, b + FU)
                last_hidden_lo(f, 0)
                hidden_block(1, ih + H_COUNT)
                units(b + FU, min(b + FU + 1, UNITS))
                if f == 3:
                    residual_sum(LN_OF[f], 0)
                last_hidden_lo(f, 1)
                if f < 2:
                    residual_sum(LN_OF[f], 0)

            def p_transposed():
                dve.wait_ge(S["pT_hi"], 1)
                dve.tensor_tensor(plo[:, :, :, :, :].rearrange("p l b k t -> p l (b k t)"),
                                  ps[:, 2:4, :],
                                  phi[:, :, :, :, :].rearrange("p l b k t -> p l (b k t)").bitcast(f32),
                                  ALU.subtract).then_inc(S["pT_ready"], 1)

            def narrow():
                dve.wait_ge(S["narrow_hi"], 2)
                dve.tensor_tensor(slo[:, :, :, :], sraw[:, :, :, :], shi[:, :, :, :].bitcast(f32),
                                  ALU.subtract).then_inc(S["narrow_lo"], 1)

            def half_sum(k, tb, n):
                if n == 0 and HALF_DONE[k][tb]:
                    dve.wait_ge(S["half_sums"], HALF_DONE[k][tb])
                else:
                    dve.wait_ge(S["unit_used"] if tb else S["tb0_done"],
                                LN_DONE[k][tb] - (n == 0))
                dve.wait_ge(S["res_ready"], 2 * k + tb + 1)
                half = res[:, tb, n * 512:(n + 1) * 512]
                note(dve.scalar_tensor_tensor(out=half, in0=ps[:, LN_BANK[k][tb][n], :],
                                              scalar=LN_SCALE[k], in1=half, op0=ALU.mult,
                                              op1=ALU.add, accum_out=sums[:, n:n + 1]))

            def negated_mean(k, tb):
                settle()
                dve.tensor_scalar(nmean[:, tb:tb + 1], sums[:, 0:1], sums[:, 1:2], -1.0 / DM,
                                  ALU.add, ALU.mult).then_inc(S["mean_ready"], 1)

            def residual_sum(k, tb):
                half_sum(k, tb, 0)
                half_sum(k, tb, 1)
                negated_mean(k, tb)

            def centre(k, tb):
                dve.wait_ge(S["mean_ready"], 2 * k + tb + 1)
                dve.wait_ge(S["gb_loaded"], 32 * (k + 1))
                note(dve.scalar_tensor_tensor(out=x[:, tb, :], in0=res[:, tb, :],
                                              scalar=nmean[:, tb:tb + 1], in1=gb[:, 0, :],
                                              op0=ALU.add, op1=ALU.mult))

            def normalise(k, tb, halves=(0, 1)):
                settle()
                dve.wait_ge(S["rstd_ready"], 2 * k + tb + 1 + (2 if k else 0))
                for n in halves:
                    at = slice(n * 512, (n + 1) * 512)
                    dve.scalar_tensor_tensor(out=x[:, tb, at], in0=x[:, tb, at],
                                             scalar=rstd[:, tb:tb + 1], in1=gb[:, 1, at],
                                             op0=ALU.mult, op1=ALU.add).then_inc(S["x_ready"], 1)

            def layer_norm(k, tb):
                residual_sum(k, tb)
                centre(k, tb)
                normalise(k, tb)

            def log_sigmoid_parts(z, nz):
                dve.scalar_tensor_tensor(out=nz, in0=z, scalar=-1.0, in1=z, op0=ALU.mult,
                                         op1=ALU.min).then_inc(S["nz_ready"], 1)

            def gate(layer, base):
                for n in range(2):
                    for tb in range(TB):
                        dve.wait_ge(S["gate_tanh"], 4 * layer + 2 * n + tb + 1)
                        dve.wait_ge(S["pp_read"], 2 * layer + tb + 1)
                        at = slice(n * 512, (n + 1) * 512)
                        note(dve.scalar_tensor_tensor(out=x[:, tb, at], in0=x[:, tb, at], scalar=1.0,
                                                      in1=pp[:, tb, at], op0=ALU.add, op1=ALU.mult))
                        settle()
                        dve.wait_ge(S["res_ready"], 2 * (3 * layer + 2) + 2)
                        ins = dve.tensor_tensor(res[:, tb, at], res[:, tb, at], x[:, tb, at], ALU.add)
                        ins.then_inc(S["gate_read"], 1)
                    units(base + 4 + 1 + n, base + 4 + 2 + n)
                dve.wait_ge(S["gate_read"], 4 * (layer + 1))

            def o_transposed(count, half, b):
                dve.wait_ge(S["oT_hi"], count)
                dve.tensor_tensor(xlo[:, 4 * half:4 * half + 4, :],
                                  ps[:, b:b + 2, :].rearrange("p a (k t) -> p (a k) t", t=TOK),
                                  xhi[:, 4 * half:4 * half + 4, :].bitcast(f32),
                                  ALU.subtract).then_inc(S["oT_ready"], 1)

            def log_sigmoid_parts(z, nz):
                dve.scalar_tensor_tensor(out=nz, in0=z, scalar=-1.0, in1=z, op0=ALU.mult,
                                         op1=ALU.min).then_inc(S["nz_ready"], 1)

            def gate(layer, base):
                for n in range(2):
                    for tb in range(TB):
                        dve.wait_ge(S["gate_tanh"], 4 * layer + 2 * n + tb + 1)
                        dve.wait_ge(S["pp_read"], 2 * layer + tb + 1)
                        at = slice(n * 512, (n + 1) * 512)
                        note(dve.scalar_tensor_tensor(out=x[:, tb, at], in0=x[:, tb, at], scalar=1.0,
                                                      in1=pp[:, tb, at], op0=ALU.add, op1=ALU.mult))
                        settle()
                        dve.wait_ge(S["res_ready"], 2 * (3 * layer + 2) + 2)
                        ins = dve.tensor_tensor(res[:, tb, at], res[:, tb, at], x[:, tb, at], ALU.add)
                        ins.then_inc(S["gate_read"], 1)
                    units(base + 4 + 1 + n, base + 4 + 2 + n)
                dve.wait_ge(S["gate_read"], 4 * (layer + 1))

            x_transposed(0, 0)
            for at, hi, lo in ((slice(0, 1024), S["half_hi"], S["half_lo"]),
                               (slice(1024, WU), S["hi_ready"], S["lo_ready"])):
                dve.wait_ge(hi, 1)
                dve.tensor_tensor(wlo[:, 0, at], raw[:, 0, at], whi[:, 0, at].bitcast(f32),
                                  ALU.subtract).then_inc(lo, 1)
            x_transposed(0, 1)
            units(1, 3)
            ffn(0, p_transposed)

            centre(0, 0)
            units(GLA_V, GLA_V + 1)
            normalise(0, 0)
            residual_sum(0, 1)
            x_transposed(1, 0)
            centre(0, 1)
            normalise(0, 1, (0,))
            units(GLA_V + 1, GLA_V + 2)
            normalise(0, 1, (1,))
            x_transposed(1, 1)
            units(GLA_Q, GLA_Q + 2)

            dve.wait_ge(S["alr_done"], 1)
            dve.wait_ge(S["const_ready"], 4)
            dve.tensor_copy(aT, ps[0:RANK, 2, 0:TOK]).then_inc(S["aT_ready"], 1)
            units(GLA_K, GLA_K + 2)
            dve.wait_ge(S["zT_done"], 1)
            dve.wait_ge(S["ba_loaded"], 16)
            for h in range(GH):
                note(dve.tensor_scalar(cs[:, h * TOK:(h + 1) * TOK],
                                       ps[:, 2 + h // 2, (h % 2) * TOK:(h % 2 + 1) * TOK],
                                       ba[:, h:h + 1], None, ALU.add))
            settle()
            log_sigmoid_parts(cs, lg)
            units(GLA_V2, GLA_V2 + 1)
            dve.wait_ge(S["log_ready"], 1)
            note(dve.scalar_tensor_tensor(out=lg, in0=cs, scalar=0.0, in1=lg, op0=ALU.min,
                                          op1=ALU.subtract))
            settle()
            note(dve.tensor_tensor_scan(cs, fresh, lg, 0.0, ALU.mult, ALU.add))
            settle()
            csv = cs.rearrange("p (n t) -> p n t", t=CH)
            dve.tensor_tensor(ks.rearrange("p (n t) -> p n t", t=CH),
                              csv[:, :, CH - 1:CH].broadcast_to([P, GH * NC, CH]), csv,
                              ALU.subtract).then_inc(S["cs_ready"], 1)
            units(GLA_V2 + 1, GLA_V2 + 2)
            dve.wait_ge(S["act_step"], 5)
            dve.wait_ge(S["unit_used"], GLA_Q + 2)
            dve.scalar_tensor_tensor(out=qd, in0=ps[:, 4:6, :].rearrange("p a c -> p (a c)"),
                                     scalar=DK ** -0.5, in1=qd, op0=ALU.mult, op1=ALU.mult) \
                .then_inc(S["qd_ready"], 1)
            note(dve.memset(attn, 0.0))
            dve.wait_ge(S["unit_used"], GLA_K + 2)
            for e in (ki, ks):
                dve.tensor_tensor(e, ps[:, 6:8, :].rearrange("p a c -> p (a c)"), e, ALU.mult) \
                    .then_inc(S["ki_ready"], 1)
            units(GLA_R, GLA_R + 2)
            for tb in range(TB):
                dve.wait_ge(S["kst_flipped"], tb + 1)
                dve.tensor_copy(kst[:, tb * 512:(tb + 1) * 512], ps[:, 4 + tb, :]) \
                    .then_inc(S["kst_ready"], 1)
            dve.wait_ge(S["attn_done"], 1)
            dve.wait_ge(S["mask_ready"], 1)
            settle()
            for tb in range(TB):
                dve.copy_predicated(attn[:, tb * 512:(tb + 1) * 512].rearrange("p (h t) -> p h t", h=GH),
                                    chunk_mask[:, :].bitcast(u32).unsqueeze(1).broadcast_to([P, GH, P]),
                                    ps[:, 6 + tb, :].rearrange("p (h t) -> p h t", h=GH)) \
                    .then_inc(S["attn_ready"], 1)
            units(GLA_R + 2, GLA_R + 3)
            dve.wait_ge(S["kv_done"], 1)
            note(dve.tensor_copy(state[:, 0, :], ps[:, 4:6, :].rearrange("p a c -> p (a c)")))
            settle()
            for n in (1, 2):
                dve.wait_ge(S["kv_done"], n + 1)
                b = (4, 2, 6)[n]
                for h in range(GH):
                    note(dve.scalar_tensor_tensor(
                        out=state[:, n, h * DV:(h + 1) * DV],
                        in0=state[:, n - 1, h * DV:(h + 1) * DV],
                        scalar=dec[:, h * NC + n:h * NC + n + 1],
                        in1=ps[:, b + h // 2, (h % 2) * DV:(h % 2 + 1) * DV],
                        op0=ALU.mult, op1=ALU.add))
                settle()
            dve.engine_nop().then_inc(S["state_ready"], 1)
            units(GLA_R + 3, GLA_R + 4)

            ob = [4, 2]

            def head_psum(tb, h):
                return ps[:, ob[tb] + h // 2, (h % 2) * DV:(h % 2 + 1) * DV]

            for tb in range(TB):
                dve.wait_ge(S["o_done"], tb + 1)
                for h in range(GH):
                    note(dve.bn_stats(stats[:, GH * tb + h, :], head_psum(tb, h)))
                settle()
                for h in range(GH):
                    note(dve.bn_aggr(mv[:, GH * tb + h, :], stats[:, GH * tb + h, :]))
                settle()
                dve.engine_nop().then_inc(S["stats_ready"], 1)
            dve.wait_ge(S["gn_loaded"], 32)

            def pairs(c):
                return [(tb, h, slice(h * DV, (h + 1) * DV), GH * tb + h)
                        for tb in range(TB) for h in (2 * c, 2 * c + 1)]

            def centred_heads(c):
                for tb, h, at, i in pairs(c):
                    note(dve.scalar_tensor_tensor(out=x[:, tb, at], in0=head_psum(tb, h),
                                                  scalar=mv[:, i, 0:1], in1=gn[:, 0, at],
                                                  op0=ALU.subtract, op1=ALU.mult))
                settle()
                dve.engine_nop().then_inc(S["ohat_ready"], 1)

            def normalised_heads(c):
                dve.wait_ge(S["rstd_ready"], 4)
                for tb, h, at, i in pairs(c):
                    note(dve.scalar_tensor_tensor(out=x[:, tb, at], in0=x[:, tb, at],
                                                  scalar=rstd[:, i:i + 1], in1=gn[:, 1, at],
                                                  op0=ALU.mult, op1=ALU.add))

            def gated_output(c):
                v = x[:, :, c * 512:(c + 1) * 512]
                dve.wait_ge(S["sr_ready"], c + 1)
                settle()
                dve.tensor_tensor(v, v, g_sr[:, :, c * 512:(c + 1) * 512], ALU.mult) \
                    .then_inc(S["on_ready"], 1)

            centred_heads(0)
            normalised_heads(0)
            gated_output(0)
            units(GLA_O, GLA_O + 1)
            centred_heads(1)
            o_transposed(1, 0, 6)
            normalised_heads(1)
            units(GLA_O + 1, GLA_O + 2)
            gated_output(1)
            units(GLA_O + 2, GLA_O + 3)
            o_transposed(2, 1, 0)
            units(GLA_O + 3, GATE_0 + 1)
            layer_norm(1, 0)
            half_sum(1, 1, 0)
            half_split(GATE_0 + 1, 0)
            x_transposed(2, 0, (0,))
            half_sum(1, 1, 1)
            negated_mean(1, 1)
            half_split(GATE_0 + 1, 1)
            x_transposed(2, 0, (1,))
            centre(1, 1)
            normalise(1, 1)
            x_transposed(2, 1)
            units(GATE_0 + 2, GATE_0 + 5)
            gate(0, GATE_0)
            ffn(1)

            centre(2, 0)
            units(FFN1_1, FFN1_1 + 1)
            normalise(2, 0)
            residual_sum(2, 1)
            x_transposed(3, 0)
            centre(2, 1)
            normalise(2, 1, (0,))
            units(FFN1_1 + 1, FFN1_1 + 2)
            normalise(2, 1, (1,))
            x_transposed(3, 1)
            units(FFN1_1 + 2, FFN1_1 + 3)
            ffn(2)

            dve.wait_ge(S["f_done"], 1)
            dve.wait_ge(S["bf_loaded"], 16)
            note(dve.tensor_scalar(lf[:, 0, :], ps[0:FH, 2, 0:TOK], bf[:, 0:1], None, ALU.add))
            settle()
            dve.engine_nop().then_inc(S["f_ready"], 1)
            log_sigmoid_parts(lf[:, 0, :], lf[:, 1, :])
            units(FOX_K + 1, FOX_K + 2)
            layer_norm(3, 0)
            units(FOX_K + 2, FOX_K + 4)
            layer_norm(3, 1)
            dve.wait_ge(S["log_ready"], 2)
            note(dve.scalar_tensor_tensor(out=lf[:, 0, :], in0=lf[:, 0, :], scalar=0.0,
                                          in1=lf[:, 1, :], op0=ALU.min, op1=ALU.subtract))
            settle()
            dve.tensor_tensor_scan(cT[0:FH, :], ones16[:, :], lf[:, 0, :], 0.0, ALU.mult,
                                   ALU.add).then_inc(S["cT_ready"], 1)
            units(FOX_V, FOX_V + 1)
            units(FOX_V + 1, FOX_V + 2)
            dve.wait_ge(S["ctT_done"], 1)
            dve.tensor_copy(ct[:, :, :], ps[:, 5, 0:TB * P].rearrange("p (b c) -> p b c", b=TB)[:, :, 0:FH]) \
                .then_inc(S["ct_ready"], 1)
            units(FOX_V + 2, FOX_V + 4)
            o_transposed(3, 0, 6)
            units(FOX_Q, FOX_Q + 2)
            o_transposed(4, 1, 4)
            units(FOX_Q + 2, FOX_G + 2)
            dve.wait_ge(S["c_ready"], 2)

            def logits(h):
                r, l = h % 2, f_l[h % 3]
                dve.wait_ge(S["qk_done"], h + 1)
                if h >= 3:
                    dve.wait_ge(S["prob_flipped"], h - 2)
                for tb, (a, n, c) in enumerate(((0, P, c0), (P, 2 * P, c1))):
                    dve.tensor_tensor_reduce(out=l[:, a:a + n], in0=ps[:, r, a:a + n],
                                             in1=c[:, h, :], scale=-1.0, scalar=3.0e38,
                                             op0=ALU.add, op1=ALU.min,
                                             accum_out=nmax[:, h, tb:tb + 1]) \
                        .then_inc(S["l_ready"], 1)

            def probs_transposed(h):
                r = h % 2
                dve.wait_ge(S["prob_flipped"], h + 1)
                if h >= 2:
                    dve.wait_ge(S["pv_done"], h - 1)
                dve.tensor_copy(f_pT[:, r, :], ps[:, 2 + r, 0:3 * P]).then_inc(S["pT_read"], 1)

            def head_output(half):
                hs = slice(8 * half, 8 * half + 8)
                dve.wait_ge(S["p_ready"], 2 * (8 * half + 8))
                note(dve.reciprocal(rinv[:, :, hs], rsum[:, :, hs]))
                settle()
                note(dve.tensor_scalar(rinv[:, :, hs], rinv[:, :, hs], 0.5, None, ALU.mult))
                settle()
                dve.wait_ge(S["pv_done"], 8 * half + 8)
                for tb in range(TB):
                    o = x[:, tb, 512 * half:512 * half + 512]
                    note(dve.tensor_tensor(o.rearrange("p (h d) -> p h d", d=FD),
                                           ps[:, 4 + tb, :].rearrange("p (h d) -> p h d", d=FD),
                                           rinv[:, tb, hs].unsqueeze(2).broadcast_to([P, 8, FD]),
                                           ALU.mult))
                settle()
                dve.engine_nop().then_inc(S["pv_read"], 1)
                dve.wait_ge(S["th_ready"], half + 1)
                for tb in range(TB):
                    at = slice(512 * half, 512 * half + 512)
                    note(dve.scalar_tensor_tensor(out=x[:, tb, at], in0=f_th[:, tb, at], scalar=1.0,
                                                  in1=x[:, tb, at], op0=ALU.add, op1=ALU.mult))
                settle()
                dve.engine_nop().then_inc(S["half_read"], 1)

            for i in range(FH + 2):
                if i < FH:
                    logits(i)
                if i >= 2:
                    probs_transposed(i - 2)
                for half in range(2):
                    if i - half in SPLIT_AT_HEAD:
                        half_split(SPLIT_AT_HEAD[i - half], half)
                if i == 10:
                    head_output(0)
            o_transposed(5, 0, 0)
            head_output(1)
            units(FOX_O + 2, FOX_O + 3)
            o_transposed(6, 1, 4)
            units(FOX_O + 3, GATE_1 + 1)
            layer_norm(4, 0)
            half_sum(4, 1, 0)
            half_split(GATE_1 + 1, 0)
            x_transposed(5, 0, (0,))
            half_sum(4, 1, 1)
            negated_mean(4, 1)
            half_split(GATE_1 + 1, 1)
            x_transposed(5, 0, (1,))
            centre(4, 1)
            normalise(4, 1)
            x_transposed(5, 1)
            units(GATE_1 + 2, GATE_1 + 5)
            gate(1, GATE_1)
            ffn(3)
            centre(5, 0)
            normalise(5, 0)
            layer_norm(5, 1)

        @block.tensor
        def _(pe):
            def product(dst, a, b, start, stop):
                return pe.matmul(dst, a, b, start=start, stop=stop, skip_group_check=True)

            def three(dst, ahi, alo, bhi, blo, first, last):
                product(dst, ahi, bhi, first, False)
                product(dst, ahi, blo, False, False)
                return product(dst, alo, bhi, False, last)

            def use(n):
                pe.wait_ge(S["lo_ready"], n + 1)

            def wide(s, q, tb, bank, middle=None):
                t = slice(tb * P, (tb + 1) * P)
                for k in range(4):
                    if middle is not None and k == middle[0]:
                        middle[1]()
                    at = slice(k * 512, k * 512 + 512)
                    last = three(ps[:, bank, :], xhi[:, 4 * q + k, t], xlo[:, 4 * q + k, t],
                                 whi[:, s, at], wlo[:, s, at], q == 0 and k == 0, q == 1 and k == 3)
                return last

            def feature_major(s, q, banks):
                for m in range(4):
                    dst = ps[:, banks[m // 2], (m % 2) * TOK:(m % 2 + 1) * TOK]
                    for k in range(4):
                        at = slice(k * 512 + m * P, k * 512 + (m + 1) * P)
                        last = three(dst, whi[:, s, at], wlo[:, s, at], xhi[:, 4 * q + k, :],
                                     xlo[:, 4 * q + k, :], q == 0 and k == 0 and m % 2 == 0,
                                     q == 1 and k == 3)
                return last

            def deep(s, hi, lo, tb, banks, first, last, half_done=None):
                for n in range(2):
                    for k in range(2):
                        at = slice(k * 1024 + n * 512, k * 1024 + n * 512 + 512)
                        ins = three(ps[:, banks + n, :], hi[:, tb, k, :], lo[:, tb, k, :],
                                    whi[:, s, at], wlo[:, s, at], first and k == 0,
                                    last and k == 1)
                    if n == 0 and half_done is not None:
                        ins.then_inc(half_done, 1)
                return ins

            def flip_x(v, tb, halves=(0, 1)):
                for half in halves:
                    if v:
                        pe.wait_ge(S["x_ready"], 4 * (v - 1) + 2 * tb + half + 1)
                    for k in range(4):
                        at = (4 * half + k) * P
                        last = pe.transpose(ps[:, X_BANK[v][tb] + half, k * P:(k + 1) * P],
                                            x[:, tb, at:at + P], ident[:, :])
                    last.then_inc(S["x_flipped"], 1)

            def warm(n):
                for _ in range(n):
                    pe.transpose(ps[:, 7, 0:P], ident[:, :], ident[:, :])

            def flip_hidden_block(tb):
                for k in range(2):
                    last = pe.transpose(ps[:, 2 + tb, k * P:(k + 1) * P],
                                        hid[:, 1, tb, k * P:(k + 1) * P], ident[:, :])
                return last

            def flip_h(h_count):
                pe.wait_ge(S["h_ready"], h_count)
                flip_hidden_block(0)
                flip_hidden_block(1).then_inc(S["h_flipped"], 1)

            def block_of_units(n, bank, v, tb, flipping=False):
                for q in range(2):
                    pe.wait_ge(S["xT_ready"], X_COUNT[v] + 2 * tb + q + 1)
                    use(n + q)
                    last = wide((n + q) % NS, q, tb, bank)
                    if flipping:
                        flip_x(v, 1, (q,))
                    if tb == TB - 1:
                        last.then_inc(S["unit_used"], 1)
                return last

            def two_units(n, banks):
                for q in range(2):
                    use(n + q)
                    for tb in range(TB):
                        last = wide((n + q) % NS, q, tb, banks[tb])
                    last.then_inc(S["unit_used"], 1)

            def two_feature_units(n, banks):
                for q in range(2):
                    use(n + q)
                    feature_major((n + q) % NS, q, banks).then_inc(S["unit_used"], 1)

            def ffn_in(n, s, q):
                use(n)
                for tb in range(TB):
                    last = wide(s, q, tb, tb)
                last.then_inc(S["unit_used"], 1)

            def ffn_out(n, s, t_count, first):
                pe.wait_ge(S["hT_ready"], t_count)
                use(n)
                deep(s, hhi, hlo, 0, 4, first, False)
                deep(s, hhi, hlo, 1, 6, first, False).then_inc(S["unit_used"], 1)

            def ffn(f, flipped, banks_read, count):
                b, it, ih = FFN_BASE[f], f * T_COUNT, f * H_COUNT
                v = FFN_X[f]
                if f == 0:
                    warm(13)
                    pe.wait_ge(S["x0_loaded"], 16)
                    flip_x(0, 0)
                    warm(24)

                    def flip_second():
                        use(0)
                        pe.wait_ge(S["x1_loaded"], 16)
                        flip_x(0, 1)

                    pe.wait_ge(S["xT_ready"], 1)
                    pe.wait_ge(S["half_lo"], 1)
                    wide(0, 0, 0, 0, middle=(2, flip_second))
                    pe.wait_ge(S["xT_ready"], 3)
                    wide(0, 0, 1, 1).then_inc(S["unit_used"], 1)
                    use(1)
                    pe.wait_ge(S["xT_ready"], 4)
                    wide(1, 1, 0, 0).then_inc(S["gu_half"], 1)
                    wide(1, 1, 1, 1).then_inc(S["unit_used"], 1)
                    flip_p()
                else:
                    for tb in range(TB):
                        last = block_of_units(b, tb, v, tb, flipping=flipped == 1 and tb == 0)
                        if tb == 0:
                            last.then_inc(S["gu_half"], 1)

                use(b + 2)
                for tb in range(TB):
                    pe.wait_ge(S["h_ready"], ih + tb + 1)
                    last = wide((b + 2) % NS, 0, tb, tb)
                last.then_inc(S["unit_used"], 1)
                pe.wait_ge(banks_read, count)
                flip_h(ih + 2)
                ffn_in(b + 3, b % NS, 1)
                ffn_out(b + 4, (b + 1) % NS, it + 1, True)

                with pe.Fori(2, LAST_J) as j:
                    n = j * 3 + (b - 1)
                    pe.wait_ge(S["h_ready"], j + (ih + 1))
                    ffn_in(n, (b + 2) % NS, 0)
                    flip_h(j + (ih + 1))
                    ffn_in(n + 1, b % NS, 1)
                    ffn_out(n + 2, (b + 1) % NS, j + it, False)

                n = b + 3 * LAST_J - 1
                pe.wait_ge(S["h_ready"], ih + LAST_J + 1)
                use(n)
                wide(n % NS, 0, 0, 0)
                flip_h(ih + LAST_J + 1)
                use(n + 1)
                wide((n + 1) % NS, 1, 0, 0).then_inc(S["gu_half"], 1)
                wide(n % NS, 0, 1, 1).then_inc(S["unit_used"], 1)
                pe.wait_ge(S["hT_ready"], it + LAST_J)
                use(n + 2)
                deep((n + 2) % NS, hhi, hlo, 0, 4, False, False)
                pe.wait_ge(S["h_ready"], ih + H_COUNT - 1)
                flip_hidden_block(0).then_inc(S["h_flipped"], 1)
                wide((n + 1) % NS, 1, 1, 1).then_inc(S["unit_used"], 1)
                pe.wait_ge(S["hT_ready"], it + T_COUNT - 1)
                use(n + 3)
                deep(n % NS, h2hi, h2lo, 0, 4, False, True, S["half_sums"]).then_inc(S["tb0_done"], 1)
                pe.wait_ge(S["h_ready"], ih + H_COUNT)
                flip_hidden_block(1).then_inc(S["h_flipped"], 1)
                deep((n + 2) % NS, hhi, hlo, 1, 6, False, False).then_inc(S["unit_used"], 1)
                pe.wait_ge(S["hT_ready"], it + T_COUNT)
                deep(n % NS, h2hi, h2lo, 1, 6, False, True, S["half_sums"]) \
                    .then_inc(S["unit_used"], 1)

            def projection(layer, n, v):
                use(n)
                s = n % NS
                deep(s, phi[:, layer], plo[:, layer], 0, 0, True, True).then_inc(S["tb0_done"], 1)
                flip_x(v, 0)
                deep(s, phi[:, layer], plo[:, layer], 1, 2, True, True).then_inc(S["unit_used"], 1)
                pe.wait_ge(S["pp_read"], 2 * layer + 1)

            def narrow(i, b, done):
                pe.wait_ge(S["narrow_lo"], 1)
                for k in range(KT):
                    last = three(ps[0:RANK, b, 0:TOK], shi[:, i, k, :], slo[:, i, k, :],
                                 xhi[:, k, :], xlo[:, k, :], k == 0, k == KT - 1)
                last.then_inc(S[done], 1)

            def flip_o(half, b):
                for k in range(4):
                    for tb in range(TB):
                        last = pe.transpose(
                            ps[:, b + k // 2, (k % 2) * TOK + tb * P:(k % 2) * TOK + (tb + 1) * P],
                            x[:, tb, (4 * half + k) * P:(4 * half + k + 1) * P], ident[:, :])
                last.then_inc(S["o_flipped"], 1)

            def output_unit(n, half, bank, c):
                use(n)
                for tb in range(TB):
                    last = wide(n % NS, half, tb, bank[tb][c])
                last.then_inc(S["unit_used"], 1)

            def output_blocks(n, bank, v):
                def flip_first():
                    flip_x(v, 0, (0,))

                for tb in range(TB):
                    for c in range(2):
                        use(n + c)
                        last = wide((n + c) % NS, 1, tb, bank[tb][c],
                                    middle=(3, flip_first) if (tb, c) == (1, 1) else None)
                        last.then_inc(*((S["half_sums"], 1), (S["tb0_done"], 1))[c] if tb == 0
                                      else (S["unit_used"], 1))

            def gate(layer, base):
                bank, v = LN_BANK[3 * layer + 1], 3 * layer + 2

                def flip_second():
                    flip_x(v, 1, (0,))

                flip_x(v, 0, (1,))
                for tb in range(TB):
                    for q in range(2):
                        pe.wait_ge(S["xT_ready"], X_COUNT[v] + 2 * tb + q + 1)
                        use(base + q)
                        last = wide((base + q) % NS, q, tb, bank[tb][0],
                                    middle=(3, flip_second) if (tb, q) == (0, 1) else None)
                        if tb == 1:
                            last.then_inc(S["unit_used"], 1)
                    if tb == 0:
                        flip_x(v, 1, (1,))
                two_units(base + 2, [bank[0][1], bank[1][1]])

            def flip_p():
                pe.wait_ge(S["p_loaded"], 16)
                for layer in range(DEPTH):
                    for tb in range(TB):
                        for k in range(2):
                            i = 2 * tb + k
                            last = pe.transpose(ps[:, 2 + layer, i * P:(i + 1) * P],
                                                p_raw[:, layer, tb, k * P:(k + 1) * P], ident[:, :])
                last.then_inc(S["p_flipped"], 1)

            pe.wait_ge(S["ident_ready"], 1)
            ffn(0, 0, S["pT_ready"], 1)
            projection(0, PP_0, 1)

            block_of_units(GLA_V, 0, 1, 0, flipping=True)
            block_of_units(GLA_V, 1, 1, 1)
            pe.wait_ge(S["pp_read"], 2)
            narrow(0, 2, "alr_done")
            n = GLA_Q
            use(n)
            feature_major(n % NS, 0, (4, 5)).then_inc(S["unit_used"], 1)
            use(n + 1)
            feature_major((n + 1) % NS, 1, (4, 5)).then_inc(S["unit_used"], 1)
            pe.wait_ge(S["aT_ready"], 1)
            pe.wait_ge(S["wa2_loaded"], 16)
            for h in range(GH):
                last = pe.matmul(ps[:, 2 + h // 2, (h % 2) * TOK:(h % 2 + 1) * TOK],
                                 wa2[:, h * DK:(h + 1) * DK], aT, start=True, stop=True)
            last.then_inc(S["zT_done"], 1)
            two_feature_units(GLA_K, (6, 7))
            pe.wait_ge(S["nz_ready"], 1)
            two_units(GLA_V2, (2, 3))
            pe.wait_ge(S["v_read"], 1)
            n = GLA_R
            use(n)
            for tb in range(TB):
                last = wide(n % NS, 0, tb, tb)
            last.then_inc(S["unit_used"], 1)
            pe.wait_ge(S["qd_ready"], 1)
            pe.wait_ge(S["ki_ready"], 2)
            for tb in range(TB):
                for h in range(GH):
                    last = pe.transpose(ps[:, 4 + tb, h * P:(h + 1) * P],
                                        ks[:, h * TOK + tb * P:h * TOK + (tb + 1) * P], ident[:, :])
                last.then_inc(S["kst_flipped"], 1)
            for tb in range(TB):
                for h in range(GH):
                    t = slice(h * TOK + tb * P, h * TOK + (tb + 1) * P)
                    last = pe.matmul(ps[:, 6 + tb, h * P:(h + 1) * P], ki[:, t], qd[:, t],
                                     start=True, stop=True)
            last.then_inc(S["attn_done"], 1)
            use(n + 1)
            wide((n + 1) % NS, 1, 0, 0)
            pe.wait_ge(S["v_read"], 2)
            pe.wait_ge(S["kst_ready"], 2)
            pe.wait_ge(S["attn_ready"], 2)
            for c, b in enumerate((4, 2, 6)):
                t = slice((c % 2) * CH, (c % 2 + 1) * CH)
                for h in range(GH):
                    last = pe.matmul(ps[:, b + h // 2, (h % 2) * DV:(h % 2 + 1) * DV],
                                     kst[t, (c // 2) * 512 + h * DK:(c // 2) * 512 + (h + 1) * DK],
                                     g_v[t, c // 2, h * DV:(h + 1) * DV], start=True, stop=True)
                last.then_inc(S["kv_done"], 1)
            wide((n + 1) % NS, 1, 1, 1).then_inc(S["unit_used"], 1)
            pe.wait_ge(S["state_ready"], 1)
            for tb, b in enumerate((4, 2)):
                for h in range(GH):
                    o = ps[:, b + h // 2, (h % 2) * DV:(h % 2 + 1) * DV]
                    last = pe.matmul(o, attn[:, tb * 512 + h * P:tb * 512 + (h + 1) * P],
                                     g_v[:, tb, h * DV:(h + 1) * DV], start=True, stop=False,
                                     skip_group_check=True)
                    for e in range(2):
                        c = 2 * tb + e
                        if c == 0:
                            continue
                        last = pe.matmul(o[e * CH:(e + 1) * CH, :],
                                         qd[:, h * TOK + c * CH:h * TOK + (c + 1) * CH],
                                         state[:, c - 1, h * DV:(h + 1) * DV], start=False,
                                         stop=e == 1, skip_group_check=True)
                last.then_inc(S["o_done"], 1)
            pe.wait_ge(S["sr_ready"], 1)
            n = GLA_R + 2
            use(n)
            for tb in range(TB):
                last = wide(n % NS, 0, tb, tb)
            last.then_inc(S["unit_used"], 1)
            use(n + 1)
            wide((n + 1) % NS, 1, 0, 0)
            pe.wait_ge(S["on_ready"], 1)
            flip_o(0, 6)
            wide((n + 1) % NS, 1, 1, 1).then_inc(S["unit_used"], 1)
            pe.wait_ge(S["oT_ready"], 1)
            output_unit(GLA_O, 0, LN_BANK[1], 0)
            pe.wait_ge(S["on_ready"], 2)
            flip_o(1, 0)
            pe.wait_ge(S["ohat_ready"], 2)
            output_unit(GLA_O + 1, 0, LN_BANK[1], 1)
            pe.wait_ge(S["oT_ready"], 2)
            output_blocks(GLA_O + 2, LN_BANK[1], 2)
            gate(0, GATE_0)
            ffn(1, 2, S["gate_read"], 4)
            projection(1, PP_1, 3)
            ffn(2, 1, S["pp_read"], 4)

            narrow(1, 2, "f_done")
            two_feature_units(FOX_K, (0, 1))
            pe.wait_ge(S["f_ready"], 1)
            two_feature_units(FOX_K + 2, (2, 3))

            def value_unit(q, c):
                n = FOX_V + 2 * q + c
                use(n)
                for tb in range(TB):
                    last = wide(n % NS, q, tb, 2 * c + tb)
                last.then_inc(S["unit_used"], 1)

            pe.wait_ge(S["kT_ready"], 1)
            value_unit(0, 0)
            pe.wait_ge(S["x_ready"], 4 * 4)
            pe.wait_ge(S["cT_ready"], 1)
            for tb in range(TB):
                last = pe.transpose(ps[:, 5, tb * P:(tb + 1) * P], cT[:, tb * P:(tb + 1) * P],
                                    ident[:, :])
            last.then_inc(S["ctT_done"], 1)
            pe.wait_ge(S["kT_ready"], 2)
            value_unit(0, 1)
            flip_o(0, 6)
            value_unit(1, 0)
            value_unit(1, 1)
            pe.wait_ge(S["ct_ready"], 1)
            flip_o(1, 4)
            for c, banks in enumerate(((6, 7), (2, 3))):
                if c:
                    pe.wait_ge(S["fv_read"], 2)
                for q in range(2):
                    pe.wait_ge(S["oT_ready"], 3 + q)
                    n = FOX_Q + 2 * c + q
                    use(n)
                    feature_major(n % NS, q, banks).then_inc(S["unit_used"], 1)

            def scores(h):
                r = h % 2
                if h >= 2:
                    pe.wait_ge(S["l_ready"], 2 * (h - 1))
                else:
                    pe.wait_ge(S["qT_ready"], 1)
                row = slice(r * FD, (r + 1) * FD)
                for tb, (a, n) in enumerate(((0, P), (P, 2 * P))):
                    last = pe.matmul(ps[:, r, a:a + n], f_q[row, h // 2, tb * P:(tb + 1) * P],
                                     f_k[row, h // 2, 0:n], start=True, stop=True)
                last.then_inc(S["qk_done"], 1)

            def flip_probs(h):
                r = h % 2
                pe.wait_ge(S["p_ready"], 2 * h + 2)
                if h >= 2:
                    pe.wait_ge(S["pT_read"], h - 1)
                else:
                    pe.wait_ge(S["qT_ready"], 2)
                for i in range(3):
                    last = pe.transpose(ps[:, 2 + r, i * P:(i + 1) * P],
                                        f_l[h % 3][:, i * P:(i + 1) * P], ident[:, :])
                last.then_inc(S["prob_flipped"], 1)

            def values(h):
                pe.wait_ge(S["pT_read"], h + 1)
                if h == 8:
                    pe.wait_ge(S["pv_read"], 1)
                r, d = h % 2, slice(h * FD, (h + 1) * FD)
                c = slice((h % 8) * FD, (h % 8 + 1) * FD)
                pe.matmul(ps[:, 4, c], f_pT[:, r, 0:P], f_v[:, 0, d], start=True, stop=True)
                pe.matmul(ps[:, 5, c], f_pT[:, r, P:2 * P], f_v[:, 0, d], start=True, stop=False)
                pe.matmul(ps[:, 5, c], f_pT[:, r, 2 * P:3 * P], f_v[:, 1, d], start=False,
                          stop=True).then_inc(S["pv_done"], 1)

            def gate_piece(i):
                n, q, tb, k0 = FOX_G + i // 4, i // 4 % 2, i // 2 % 2, i % 2 * 2
                if i in (0, 8):
                    pe.wait_ge(*((S["qT_ready"], 1), (S["th_ready"], 1))[i // 8])
                use(n)
                t = slice(tb * P, (tb + 1) * P)
                for k in (k0, k0 + 1):
                    at = slice(k * 512, k * 512 + 512)
                    last = three(ps[:, 6 + tb, :], xhi[:, 4 * q + k, t], xlo[:, 4 * q + k, t],
                                 whi[:, n % NS, at], wlo[:, n % NS, at], q == 0 and k == 0,
                                 q == 1 and k == 3)
                if i % 4 == 3:
                    last.then_inc(S["unit_used"], 1)

            pieces = [(0,), (1,), (2,), (3,), (4,), (5,), (6,), (7,), (), (8,), (9,), (10, 11), (),
                      (12,), (13,), (), (14,), (15,), ()]
            for i in range(FH + 3):
                if i < FH:
                    scores(i)
                if 2 <= i < FH + 2:
                    flip_probs(i - 2)
                for piece in pieces[i]:
                    gate_piece(piece)
                if i >= 3:
                    values(i - 3)
                if i == FH:
                    pe.wait_ge(S["half_read"], 1)
                    pe.wait_ge(S["l_ready"], 2 * FH)
                    flip_o(0, 0)
            pe.wait_ge(S["th_ready"], 2)
            pe.wait_ge(S["oT_ready"], 5)
            output_unit(FOX_O, 0, LN_BANK[4], 0)
            pe.wait_ge(S["half_read"], 2)
            flip_o(1, 4)
            output_unit(FOX_O + 1, 0, LN_BANK[4], 1)
            pe.wait_ge(S["oT_ready"], 6)
            output_blocks(FOX_O + 2, LN_BANK[4], 5)
            gate(1, GATE_1)
            ffn(3, 2, S["gate_read"], 8)


_INS = ["x", "p", "ffn1_w_in", "ffn1_w_out", "ln1_g", "ln1_b", "gla_w_in", "gla_w_a2", "gla_b_a",
        "gla_gn_g", "gla_gn_b", "gla_w_o", "fox_w_kvf", "fox_b_f", "fox_w_in", "fox_w_o", "ln2_g",
        "ln2_b", "ffn2_w_in", "ffn2_w_out", "ple_w_gate", "ple_w_proj", "ln3_g", "ln3_b"]


def kernel(**inputs):
    import numpy as _np
    import concourse.bacc as _bacc
    from concourse import mybir as _mybir
    from concourse.bass_utils import run_bass_kernel_spmd as _run

    nc = _bacc.Bacc("TRN2", target_bir_lowering=False, num_devices=1)
    arrays, args = {}, []
    for name in _INS:
        a = _np.ascontiguousarray(inputs[name])
        arrays[f"in_{name}"] = a
        args.append(nc.dram_tensor(f"in_{name}", a.shape, _mybir.dt.from_np(a.dtype),
                                   kind="ExternalInput").ap())
    shape = inputs["x"].shape
    o = nc.dram_tensor("out_0", shape, _mybir.dt.float32, kind="ExternalOutput").ap()
    trunk(nc, *args, o)
    r = _run(nc, [arrays], core_ids=[0])
    return r.results[0]["out_0"]
```
